# Optimizing a Trainium2 kernel written in Bass

```python
import math
import jax, jax.numpy as jnp
from jax import lax
import numpy as np
import jax
import jax.numpy as jnp

D_MODEL = 1024
BATCH = 1
SEQ = 256
DEPTH = 1

CONV_DIM = D_MODEL
CONV_KERNEL = 31
SSM_EXPAND = 2
SSM_DIM = SSM_EXPAND * D_MODEL
SSM_HEAD_DIM = 64
SSM_HEADS = SSM_DIM // SSM_HEAD_DIM
SSM_GROUPS = 4
SSM_STATE = 128
SSM_CONV = 4
SSM_CHUNK = 128
SSM_BC = 2 * SSM_GROUPS * SSM_STATE
FFN_DIM = 2816
FFN_CONV = 3
DN_ALPHA = (2 * DEPTH) ** 0.25
DN_BETA = (8 * DEPTH) ** -0.25
LN_EPS = 1e-5
RMS_EPS = 1e-5
IN_SIZES = (2 * CONV_DIM, SSM_DIM, SSM_DIM + SSM_BC, SSM_HEADS, D_MODEL, D_MODEL)
IN_DIM = sum(IN_SIZES)


def layer_norm(x, g, b):
    xf = x.astype(jnp.float32)
    mu = jnp.mean(xf, axis=-1, keepdims=True)
    var = jnp.mean(jnp.square(xf - mu), axis=-1, keepdims=True)
    return ((xf - mu) * lax.rsqrt(var + LN_EPS) * g.astype(jnp.float32)
            + b.astype(jnp.float32)).astype(x.dtype)

def causal_dwconv(x, w, b):
    k = w.shape[0]
    y = lax.conv_general_dilated(
        x, w[:, None, :].astype(x.dtype), window_strides=(1,),
        padding=[(k - 1, 0)], dimension_numbers=("NWC", "WIO", "NWC"),
        feature_group_count=x.shape[-1])
    return y + b.astype(x.dtype)

def split_in(u):
    idx = [int(v) for v in np.cumsum(IN_SIZES)[:-1]]
    return jnp.split(u, idx, axis=-1)

def conformer_branch(u_glu, dw_w, dw_b, ln_g, ln_b, w_out):
    a, g = jnp.split(u_glu, 2, axis=-1)
    v = a * jax.nn.sigmoid(g)
    v = causal_dwconv(v, dw_w, dw_b)
    v = jax.nn.silu(layer_norm(v, ln_g, ln_b))
    return v @ w_out

def ssd_chunked(x, dt, a_head, bm, cm):
    b, t, h, p = x.shape
    g, n = bm.shape[2], bm.shape[3]
    r = h // g
    L = SSM_CHUNK
    c = t // L
    xs = (x * dt[..., None]).reshape(b, c, L, g, r, p)
    a = (dt * a_head).reshape(b, c, L, g, r).transpose(0, 1, 3, 4, 2)
    bc = bm.reshape(b, c, L, g, n)
    cc = cm.reshape(b, c, L, g, n)
    a_cs = jnp.cumsum(a, axis=-1)
    seg = a_cs[..., :, None] - a_cs[..., None, :]
    causal = jnp.tril(jnp.ones((L, L), dtype=bool))
    decay = jnp.where(causal, jnp.exp(jnp.where(causal, seg, 0.0)), 0.0)
    cb = jnp.einsum("bclgn,bcsgn->bcgls", cc, bc)
    y_diag = jnp.einsum("bcgrls,bcsgrp->bclgrp", cb[:, :, :, None] * decay, xs)
    decay_states = jnp.exp(a_cs[..., -1:] - a_cs)
    states = jnp.einsum("bclgn,bcgrl,bclgrp->bcgrpn", bc, decay_states, xs)
    chunk_decay = jnp.exp(a_cs[..., -1])

    def step(carry, inp):
        s_c, d_c = inp
        return d_c[..., None, None] * carry + s_c, carry

    init = jnp.zeros((b, g, r, p, n), states.dtype)
    _, prev = lax.scan(step, init, (jnp.moveaxis(states, 1, 0),
                                    jnp.moveaxis(chunk_decay, 1, 0)))
    prev = jnp.moveaxis(prev, 0, 1)
    y_off = jnp.einsum("bclgn,bcgrpn,bcgrl->bclgrp", cc, prev, jnp.exp(a_cs))
    return (y_diag + y_off).reshape(b, t, h, p)

def ssd_branch(z, xbc, dt_raw, conv_w, conv_b, dt_bias, a_log, d_skip, norm_w, w_out):
    bsz, t, _ = z.shape
    xbc = jax.nn.silu(causal_dwconv(xbc, conv_w, conv_b))
    gn = SSM_GROUPS * SSM_STATE
    xs = xbc[..., :SSM_DIM]
    bm = xbc[..., SSM_DIM:SSM_DIM + gn].reshape(bsz, t, SSM_GROUPS, SSM_STATE)
    cm = xbc[..., SSM_DIM + gn:].reshape(bsz, t, SSM_GROUPS, SSM_STATE)
    dt = jax.nn.softplus(dt_raw.astype(jnp.float32) + dt_bias.astype(jnp.float32))
    a_head = -jnp.exp(a_log.astype(jnp.float32))
    xh = xs.reshape(bsz, t, SSM_HEADS, SSM_HEAD_DIM).astype(jnp.float32)
    y = ssd_chunked(xh, dt, a_head, bm.astype(jnp.float32), cm.astype(jnp.float32))
    y = y + xh * d_skip.astype(jnp.float32)[:, None]
    yg = (y.reshape(bsz, t, SSM_DIM) * jax.nn.silu(z.astype(jnp.float32)))
    yg = yg.reshape(bsz, t, SSM_GROUPS, SSM_DIM // SSM_GROUPS)
    yg = yg * lax.rsqrt(jnp.mean(jnp.square(yg), axis=-1, keepdims=True) + RMS_EPS)
    yn = (yg.reshape(bsz, t, SSM_DIM) * norm_w.astype(jnp.float32)).astype(z.dtype)
    return yn @ w_out

def conv_ffn(h, w_up, dw_w, dw_b, w_down):
    u = causal_dwconv(h @ w_up, dw_w, dw_b)
    gate, val = jnp.split(u, 2, axis=-1)
    return (jax.nn.silu(gate) * val) @ w_down

def first_inputs(seed: int = 0) -> dict:
    key = jax.random.key(seed)
    ks = jax.random.split(key, 32)
    f32 = jnp.float32
    nrm = lambda k, shape, s: (jax.random.normal(k, shape, f32) * s).astype(f32)
    gain = lambda k, shape: 1.0 + 0.05 * jax.random.normal(k, shape, f32)
    small = lambda k, shape: 0.02 * jax.random.normal(k, shape, f32)
    dt0 = jnp.exp(jax.random.uniform(ks[12], (DEPTH, SSM_HEADS), f32)
                  * (math.log(0.1) - math.log(0.001)) + math.log(0.001))
    return {
        "x": jax.random.normal(ks[0], (BATCH, SEQ, D_MODEL), f32),
        "ln_in_g": gain(ks[1], (D_MODEL,)),
        "ln_in_b": small(ks[2], (D_MODEL,)),
        "w_in": nrm(ks[3], (DEPTH, D_MODEL, IN_DIM), D_MODEL ** -0.5),
        "conv_dw_w": nrm(ks[4], (DEPTH, CONV_KERNEL, CONV_DIM), CONV_KERNEL ** -0.5),
        "conv_dw_b": small(ks[5], (DEPTH, CONV_DIM)),
        "conv_ln_g": gain(ks[6], (DEPTH, CONV_DIM)),
        "conv_ln_b": small(ks[7], (DEPTH, CONV_DIM)),
        "w_conv_out": nrm(ks[8], (DEPTH, CONV_DIM, D_MODEL), DN_BETA * CONV_DIM ** -0.5),
        "ssm_conv_w": nrm(ks[9], (DEPTH, SSM_CONV, SSM_DIM + SSM_BC), SSM_CONV ** -0.5),
        "ssm_conv_b": small(ks[10], (DEPTH, SSM_DIM + SSM_BC)),
        "ssm_dt_bias": dt0 + jnp.log(-jnp.expm1(-dt0)),
        "ssm_a_log": jnp.log(jax.random.uniform(ks[13], (DEPTH, SSM_HEADS), f32, 1.0, 16.0)),
        "ssm_d": gain(ks[14], (DEPTH, SSM_HEADS)),
        "ssm_norm_w": gain(ks[15], (DEPTH, SSM_DIM)),
        "w_ssm_out": nrm(ks[16], (DEPTH, SSM_DIM, D_MODEL), DN_BETA * SSM_DIM ** -0.5),
        "w_o": nrm(ks[17], (DEPTH, D_MODEL, D_MODEL), DN_BETA * D_MODEL ** -0.5),
        "ln1_g": gain(ks[18], (DEPTH, D_MODEL)),
        "ln1_b": small(ks[19], (DEPTH, D_MODEL)),
        "w_ffn_up": nrm(ks[20], (DEPTH, D_MODEL, 2 * FFN_DIM), DN_BETA * D_MODEL ** -0.5),
        "ffn_dw_w": nrm(ks[21], (DEPTH, FFN_CONV, 2 * FFN_DIM), FFN_CONV ** -0.5),
        "ffn_dw_b": small(ks[22], (DEPTH, 2 * FFN_DIM)),
        "w_ffn_down": nrm(ks[23], (DEPTH, FFN_DIM, D_MODEL), DN_BETA * FFN_DIM ** -0.5),
        "ln2_g": gain(ks[24], (DEPTH, D_MODEL)),
        "ln2_b": small(ks[25], (DEPTH, D_MODEL)),
    }

def first_block(x, ln_in_g, ln_in_b, w_in, conv_dw_w, conv_dw_b, conv_ln_g, conv_ln_b,
              w_conv_out, ssm_conv_w, ssm_conv_b, ssm_dt_bias, ssm_a_log, ssm_d,
              ssm_norm_w, w_ssm_out, w_o, ln1_g, ln1_b, w_ffn_up, ffn_dw_w, ffn_dw_b,
              w_ffn_down, ln2_g, ln2_b):
    h = layer_norm(x, ln_in_g, ln_in_b)
    for l in range(DEPTH):
        u = h @ w_in[l]
        u_glu, z, xbc, dt_raw, gate_a, gate_b = split_in(u)
        y_a = conformer_branch(u_glu, conv_dw_w[l], conv_dw_b[l], conv_ln_g[l],
                               conv_ln_b[l], w_conv_out[l])
        y_b = ssd_branch(z, xbc, dt_raw, ssm_conv_w[l], ssm_conv_b[l], ssm_dt_bias[l],
                         ssm_a_log[l], ssm_d[l], ssm_norm_w[l], w_ssm_out[l])
        mix = (jax.nn.sigmoid(gate_a) * y_a + jax.nn.sigmoid(gate_b) * y_b) @ w_o[l]
        h = layer_norm(DN_ALPHA * h + mix, ln1_g[l], ln1_b[l])
        ffn = conv_ffn(h, w_ffn_up[l], ffn_dw_w[l], ffn_dw_b[l], w_ffn_down[l])
        h = layer_norm(DN_ALPHA * h + ffn, ln2_g[l], ln2_b[l])
    return h


MOBA_HEADS = 8
MOBA_HEAD_DIM = 64
MOBA_BLOCK = 256
MOBA_TOPK = 3
MOBA_Q_CHUNK = 64
DIFF_HEADS = 4
DIFF_HEAD_DIM = 64
ATTN_Q_BLOCK = 128
ROPE_THETA = 10000.0
N_GROUPS = 4
EXPERTS_PER_GROUP = 8
N_EXPERTS = N_GROUPS * EXPERTS_PER_GROUP
EXPERT_TOPK = 2
D_EXPERT = 512
NORM_EPS = 1e-6
NEG_INF = -1e30
MOBA_WIDTH = MOBA_HEADS * MOBA_HEAD_DIM
DIFF_QK_WIDTH = DIFF_HEADS * 2 * DIFF_HEAD_DIM
DIFF_V_WIDTH = DIFF_HEADS * 2 * DIFF_HEAD_DIM
_SEGMENTS = (MOBA_WIDTH, MOBA_WIDTH, MOBA_WIDTH, DIFF_QK_WIDTH, DIFF_QK_WIDTH, DIFF_V_WIDTH, D_MODEL, D_MODEL)
IN_WIDTH = sum(_SEGMENTS)
IN_SPLITS = tuple(int(s) for s in np.cumsum(_SEGMENTS)[:-1])


def rmsnorm(x, g):
    xf = x.astype(jnp.float32)
    y = xf * lax.rsqrt(jnp.mean(xf * xf, axis=-1, keepdims=True) + NORM_EPS)
    return (y * g.astype(jnp.float32)).astype(x.dtype)

def rope_tables(seq, dim):
    inv = 1.0 / (ROPE_THETA ** (jnp.arange(0, dim, 2, dtype=jnp.float32) / dim))
    ang = jnp.arange(seq, dtype=jnp.float32)[:, None] * inv[None, :]
    return jnp.cos(ang), jnp.sin(ang)

def apply_rope(x, cos, sin):
    xf = x.astype(jnp.float32)
    half = x.shape[-1] // 2
    x1, x2 = xf[..., :half], xf[..., half:]
    return jnp.concatenate([x1 * cos - x2 * sin, x2 * cos + x1 * sin], axis=-1).astype(x.dtype)

def to_heads(t, n, d):
    b, s = t.shape[:2]
    return t.reshape(b, s, n, d).transpose(0, 2, 1, 3)

def moba_attention(q, k, v):
    B, H, S, dh = q.shape
    nb = -(-S // MOBA_BLOCK)
    topk = min(MOBA_TOPK, nb)
    pad = nb * MOBA_BLOCK - S
    kp = jnp.pad(k, ((0, 0), (0, 0), (0, pad), (0, 0)))
    vp = jnp.pad(v, ((0, 0), (0, 0), (0, pad), (0, 0)))
    k_blocks = kp.reshape(B, H, nb, MOBA_BLOCK, dh)
    v_blocks = vp.reshape(B, H, nb, MOBA_BLOCK, dh)
    k_mean = jnp.mean(k_blocks.astype(jnp.float32), axis=3)
    scale = dh ** -0.5
    nc = S // MOBA_Q_CHUNK
    q_chunks = q.reshape(B, H, nc, MOBA_Q_CHUNK, dh).transpose(2, 0, 1, 3, 4)
    starts = jnp.arange(nc, dtype=jnp.int32) * MOBA_Q_CHUNK
    b_idx = jnp.arange(B)[:, None, None, None]
    h_idx = jnp.arange(H)[None, :, None, None]
    block_ids = jnp.arange(nb, dtype=jnp.int32)
    own_offsets = jnp.arange(MOBA_BLOCK, dtype=jnp.int32)

    def chunk(args):
        qb, start = args
        blk = start // MOBA_BLOCK
        qpos = start + jnp.arange(MOBA_Q_CHUNK, dtype=jnp.int32)
        gate = jnp.einsum('bhqd,bhnd->bhqn', qb.astype(jnp.float32), k_mean)
        gate = jnp.where(block_ids < blk, gate, NEG_INF)
        _, sel = lax.top_k(gate, topk)
        valid = sel < blk
        ks = k_blocks[b_idx, h_idx, sel]
        vs = v_blocks[b_idx, h_idx, sel]
        s_sel = jnp.einsum('bhqd,bhqjnd->bhqjn', qb, ks).astype(jnp.float32) * scale
        s_sel = jnp.where(valid[..., None], s_sel, NEG_INF)
        s_sel = s_sel.reshape(B, H, MOBA_Q_CHUNK, topk * MOBA_BLOCK)
        k_own = lax.dynamic_slice_in_dim(kp, blk * MOBA_BLOCK, MOBA_BLOCK, axis=2)
        v_own = lax.dynamic_slice_in_dim(vp, blk * MOBA_BLOCK, MOBA_BLOCK, axis=2)
        s_own = jnp.einsum('bhqd,bhnd->bhqn', qb, k_own).astype(jnp.float32) * scale
        kpos = blk * MOBA_BLOCK + own_offsets
        s_own = jnp.where(kpos[None, :] <= qpos[:, None], s_own, NEG_INF)
        p = jax.nn.softmax(jnp.concatenate([s_sel, s_own], axis=-1), axis=-1).astype(v.dtype)
        p_sel = p[..., :topk * MOBA_BLOCK].reshape(B, H, MOBA_Q_CHUNK, topk, MOBA_BLOCK)
        p_own = p[..., topk * MOBA_BLOCK:]
        return (jnp.einsum('bhqjn,bhqjnd->bhqd', p_sel, vs)
                + jnp.einsum('bhqn,bhnd->bhqd', p_own, v_own))

    out = lax.map(chunk, (q_chunks, starts))
    return out.transpose(1, 2, 0, 3, 4).reshape(B, H, S, dh)

def diff_attention(q, k, v, lam):
    B, H2, S, dk = q.shape
    H = H2 // 2
    scale = dk ** -0.5
    nq = S // ATTN_Q_BLOCK
    q_blocks = q.reshape(B, H2, nq, ATTN_Q_BLOCK, dk).transpose(2, 0, 1, 3, 4)
    starts = jnp.arange(nq, dtype=jnp.int32) * ATTN_Q_BLOCK
    kpos = jnp.arange(S, dtype=jnp.int32)

    def block(args):
        qb, start = args
        s = jnp.einsum('bhqd,bhkd->bhqk', qb, k).astype(jnp.float32) * scale
        qpos = start + jnp.arange(ATTN_Q_BLOCK, dtype=jnp.int32)
        s = jnp.where(kpos[None, :] <= qpos[:, None], s, NEG_INF)
        p = jax.nn.softmax(s, axis=-1).reshape(B, H, 2, ATTN_Q_BLOCK, S)
        a = (p[:, :, 0] - lam * p[:, :, 1]).astype(v.dtype)
        return jnp.einsum('bhqk,bhkd->bhqd', a, v)

    out = lax.map(block, (q_blocks, starts))
    return out.transpose(1, 2, 0, 3, 4).reshape(B, H, S, 2 * dk)

def hierarchical_moe(h, w_group, b_group, w_expert, b_expert, w_gate, w_up, w_down):
    B, S, D = h.shape
    t = h.reshape(B * S, D)
    T = t.shape[0]
    g_prob = jax.nn.softmax((t @ w_group).astype(jnp.float32) + b_group, axis=-1)
    g_w, g_idx = lax.top_k(g_prob, 1)
    e_logits = ((t @ w_expert).astype(jnp.float32) + b_expert).reshape(T, N_GROUPS, EXPERTS_PER_GROUP)
    e_in_group = jnp.take_along_axis(e_logits, g_idx[:, :, None], axis=1)[:, 0]
    e_prob = jax.nn.softmax(e_in_group, axis=-1)
    e_w, e_idx = lax.top_k(e_prob, EXPERT_TOPK)
    e_w = e_w / jnp.sum(e_w, axis=-1, keepdims=True)
    weights = (g_w * e_w).reshape(-1)
    expert = (g_idx * EXPERTS_PER_GROUP + e_idx).reshape(-1)
    order = jnp.argsort(expert)
    tok = order // EXPERT_TOPK
    xs = t[tok]
    sizes = jnp.bincount(expert, length=N_EXPERTS).astype(jnp.int32)
    hid = jax.nn.silu(lax.ragged_dot(xs, w_gate, sizes)) * lax.ragged_dot(xs, w_up, sizes)
    out = lax.ragged_dot(hid.astype(xs.dtype), w_down, sizes)
    out = out * weights[order][:, None].astype(out.dtype)
    y = jnp.zeros_like(t).at[tok].add(out.astype(t.dtype))
    return y.reshape(B, S, D)

def second_inputs(seed: int = 0) -> dict:
    key = jax.random.key(seed)
    ks = jax.random.split(key, 24)
    D = D_MODEL

    def nrm(k, shape, scale):
        return jax.random.normal(k, shape, jnp.float32) * scale

    return {
        'x': nrm(ks[0], (BATCH, SEQ, D), 1.0),
        'c': nrm(ks[1], (BATCH, D), 1.0),
        'w_ada': nrm(ks[2], (DEPTH, D, 6 * D), 0.5 * D ** -0.5),
        'b_ada': nrm(ks[3], (DEPTH, 6 * D), 0.02),
        'norm1_g': 1.0 + nrm(ks[4], (DEPTH, D), 0.02),
        'w_in': nrm(ks[5], (DEPTH, D, IN_WIDTH), D ** -0.5),
        'lambda_q1': nrm(ks[6], (DEPTH, DIFF_HEAD_DIM), 0.1),
        'lambda_k1': nrm(ks[7], (DEPTH, DIFF_HEAD_DIM), 0.1),
        'lambda_q2': nrm(ks[8], (DEPTH, DIFF_HEAD_DIM), 0.1),
        'lambda_k2': nrm(ks[9], (DEPTH, DIFF_HEAD_DIM), 0.1),
        'diff_subln_g': 1.0 + nrm(ks[10], (DEPTH, 2 * DIFF_HEAD_DIM), 0.02),
        'w_proj_moba': nrm(ks[11], (DEPTH, MOBA_WIDTH, D), MOBA_WIDTH ** -0.5),
        'w_proj_diff': nrm(ks[12], (DEPTH, DIFF_V_WIDTH, D), DIFF_V_WIDTH ** -0.5),
        'w_out': nrm(ks[13], (DEPTH, D, D), D ** -0.5),
        'norm2_g': 1.0 + nrm(ks[14], (DEPTH, D), 0.02),
        'w_group': nrm(ks[15], (DEPTH, D, N_GROUPS), D ** -0.5),
        'b_group': nrm(ks[16], (DEPTH, N_GROUPS), 0.01),
        'w_expert': nrm(ks[17], (DEPTH, D, N_EXPERTS), D ** -0.5),
        'b_expert': nrm(ks[18], (DEPTH, N_EXPERTS), 0.01),
        'w_gate': nrm(ks[19], (DEPTH, N_EXPERTS, D, D_EXPERT), D ** -0.5),
        'w_up': nrm(ks[20], (DEPTH, N_EXPERTS, D, D_EXPERT), D ** -0.5),
        'w_down': nrm(ks[21], (DEPTH, N_EXPERTS, D_EXPERT, D), D_EXPERT ** -0.5),
        'final_g': 1.0 + nrm(ks[22], (D,), 0.02),
    }

def second_block(x, c, w_ada, b_ada, norm1_g, w_in, lambda_q1, lambda_k1, lambda_q2, lambda_k2,
              diff_subln_g, w_proj_moba, w_proj_diff, w_out, norm2_g, w_group, b_group,
              w_expert, b_expert, w_gate, w_up, w_down, final_g):
    S = x.shape[1]
    cos_m, sin_m = rope_tables(S, MOBA_HEAD_DIM)
    cos_d, sin_d = rope_tables(S, DIFF_HEAD_DIM)
    c_act = jax.nn.silu(c)
    for l in range(DEPTH):
        mod = c_act @ w_ada[l] + b_ada[l]
        sh1, sc1, g1, sh2, sc2, g2 = jnp.split(mod, 6, axis=-1)

        h = rmsnorm(x, norm1_g[l]) * (1.0 + sc1[:, None, :]) + sh1[:, None, :]
        proj = h @ w_in[l]
        q_m, k_m, v_m, q_d, k_d, v_d, gate_m, gate_d = jnp.split(proj, IN_SPLITS, axis=-1)

        qm = apply_rope(to_heads(q_m, MOBA_HEADS, MOBA_HEAD_DIM), cos_m, sin_m)
        km = apply_rope(to_heads(k_m, MOBA_HEADS, MOBA_HEAD_DIM), cos_m, sin_m)
        vm = to_heads(v_m, MOBA_HEADS, MOBA_HEAD_DIM)
        o_m = moba_attention(qm, km, vm)
        y_m = o_m.transpose(0, 2, 1, 3).reshape(x.shape[0], S, MOBA_WIDTH) @ w_proj_moba[l]

        lam_init = 0.8 - 0.6 * math.exp(-0.3 * l)
        lam = (jnp.exp(jnp.sum(lambda_q1[l].astype(jnp.float32) * lambda_k1[l].astype(jnp.float32)))
               - jnp.exp(jnp.sum(lambda_q2[l].astype(jnp.float32) * lambda_k2[l].astype(jnp.float32)))
               + lam_init)
        qd = apply_rope(to_heads(q_d, 2 * DIFF_HEADS, DIFF_HEAD_DIM), cos_d, sin_d)
        kd = apply_rope(to_heads(k_d, 2 * DIFF_HEADS, DIFF_HEAD_DIM), cos_d, sin_d)
        vd = to_heads(v_d, DIFF_HEADS, 2 * DIFF_HEAD_DIM)
        o_d = diff_attention(qd, kd, vd, lam)
        o_d = rmsnorm(o_d, diff_subln_g[l]) * (1.0 - lam_init)
        y_d = o_d.transpose(0, 2, 1, 3).reshape(x.shape[0], S, DIFF_V_WIDTH) @ w_proj_diff[l]

        merged = jax.nn.sigmoid(gate_m) * y_m + jax.nn.sigmoid(gate_d) * y_d
        x = x + g1[:, None, :] * (merged @ w_out[l])

        h2 = rmsnorm(x, norm2_g[l]) * (1.0 + sc2[:, None, :]) + sh2[:, None, :]
        y_ffn = hierarchical_moe(h2, w_group[l], b_group[l], w_expert[l], b_expert[l],
                                 w_gate[l], w_up[l], w_down[l])
        x = x + g2[:, None, :] * y_ffn
    return rmsnorm(x, final_g)


def setup_inputs(seed=0):
    out = dict(first_inputs(seed))
    for name, value in second_inputs(seed + 1).items():
        if name != "x":
            out[name + "_2"] = value
    return out


def reference(
    x, ln_in_g, ln_in_b, w_in, conv_dw_w, conv_dw_b, conv_ln_g, conv_ln_b, w_conv_out,
    ssm_conv_w, ssm_conv_b, ssm_dt_bias, ssm_a_log, ssm_d, ssm_norm_w, w_ssm_out, w_o, ln1_g,
    ln1_b, w_ffn_up, ffn_dw_w, ffn_dw_b, w_ffn_down, ln2_g, ln2_b, c_2, w_ada_2, b_ada_2,
    norm1_g_2, w_in_2, lambda_q1_2, lambda_k1_2, lambda_q2_2, lambda_k2_2, diff_subln_g_2,
    w_proj_moba_2, w_proj_diff_2, w_out_2, norm2_g_2, w_group_2, b_group_2, w_expert_2,
    b_expert_2, w_gate_2, w_up_2, w_down_2, final_g_2,
):
    x = first_block(
        x, ln_in_g, ln_in_b, w_in, conv_dw_w, conv_dw_b, conv_ln_g, conv_ln_b, w_conv_out,
        ssm_conv_w, ssm_conv_b, ssm_dt_bias, ssm_a_log, ssm_d, ssm_norm_w, w_ssm_out, w_o,
        ln1_g, ln1_b, w_ffn_up, ffn_dw_w, ffn_dw_b, w_ffn_down, ln2_g, ln2_b,
    )
    return second_block(
        x, c_2, w_ada_2, b_ada_2, norm1_g_2, w_in_2, lambda_q1_2, lambda_k1_2, lambda_q2_2,
        lambda_k2_2, diff_subln_g_2, w_proj_moba_2, w_proj_diff_2, w_out_2, norm2_g_2,
        w_group_2, b_group_2, w_expert_2, b_expert_2, w_gate_2, w_up_2, w_down_2, final_g_2,
    )


_drawn_inputs = setup_inputs


def setup_inputs(seed=0):
    import zlib

    import numpy as np

    out = dict(_drawn_inputs(seed))
    spreads = {}
    factors = {'conv_dw_b': 6.866,
     'conv_ln_g': 5.606,
     'conv_ln_b': 8.0,
     'ssm_conv_b': 8.0,
     'ssm_d': 8.0,
     'ssm_norm_w': 3.841,
     'ffn_dw_b': 6.535,
     'b_ada_2': 2.769,
     'norm1_g_2': 8.0,
     'lambda_q1_2': 6.506,
     'lambda_k1_2': 5.391,
     'lambda_k2_2': 5.193,
     'diff_subln_g_2': 8.0,
     'norm2_g_2': 4.307,
     'b_group_2': 6.414,
     'b_expert_2': 8.0,
     'final_g_2': 2.947}
    for name, (base, spread) in spreads.items():
        noise = np.random.default_rng([zlib.crc32(name.encode()), seed]).standard_normal(out[name].shape)
        drawn = base * np.exp(spread * noise) if base else spread * noise
        out[name] = jnp.asarray(drawn.astype(out[name].dtype))
    for name, factor in factors.items():
        out[name] = (out[name] * factor).astype(out[name].dtype)
    return out
```

```python
from contextlib import ExitStack

import concourse.bass as bass
from concourse import mybir

P = 128
F32 = mybir.dt.float32
I32 = mybir.dt.int32
ALU = mybir.AluOpType
ACT = mybir.ActivationFunctionType
AX_X = mybir.AxisListType.X
ds = bass.ds

T = 256
TT = T // P
D = 1024
KD = D // P
CK = 31
SSM = 2048
KS = SSM // P
H = 32
HD = SSM // H
G = 4
XBC = SSM + 2 * G * P
KX = XBC // P
FF = 2816
KF = FF // P
QK = 512
E_ = 32
EG = 4
EP = E_ // EG
DE = 512
CAP = 64
ALPHA = 2.0 ** 0.25
LN_EPS = 1e-5
RMS_EPS = 1e-5
NORM_EPS = 1e-6
LAM_INIT = 0.2
NEG = -1e30
NB = 4

C_GLU, C_Z, C_XBC, C_DT, C_GA = 0, 2048, 4096, 7168, 7200

PARAMS = [("ln_in_g", 8), ("ln_in_b", 8), ("conv_w", 8 * CK), ("conv_b", 8), ("conv_ln_g", 8), ("conv_ln_b", 8),
          ("ssm_w", KX * 4), ("ssm_b", KX), ("ssm_d", KS), ("ssm_norm", KS), ("ln1_g", 8), ("ln1_b", 8),
          ("ffn_w", 2 * KF * 3), ("ffn_b", 2 * KF), ("ln2_g", 8), ("ln2_b", 8), ("b_ada", 48), ("c", 8),
          ("norm1_g", 8), ("norm2_g", 8), ("final_g", 8), ("subln_g", 1),
          ("dt_bias", H), ("a_log", H), ("b_route", EG + E_), ("lam_q1", 64), ("lam_q2", 64), ("lam_k1", 64),
          ("lam_k2", 64)]
CONSTS = [("ident", P), ("upper", P), ("before", P), ("ones", P), ("swap", P), ("ssm_mask", P), ("att_mask", 2 * T),
          ("cos", T), ("sin", T), ("slot", CAP), ("place", EP)]


def offsets(table):
    at, out = 0, {}
    for name, n in table:
        out[name] = (at, n)
        at += n
    return out, at


PAR, NPAR = offsets(PARAMS)
CON, NCON = offsets(CONSTS)

TILES = [("h", 4), ("xbc", 12), ("glu", 8), ("xtok", 9), ("z", 8), ("gate", 8), ("ada0", 1), ("ssd", 8), ("conv_out", 4),
         ("ssm_out", 4), ("mix", 4), ("ada1", 1), ("up", 22), ("down", 4), ("ada2", 1), ("qk", 8), ("v", 4), ("swap", 8),
         ("gate2", 8), ("proj_m", 4), ("proj_d", 4), ("out2", 4)]
TILE, NTILES = offsets(TILES)
UNITS = [("xbc", 6), ("glu", 4), ("z", 4), ("gate", 4), ("ada0", 4), ("conv_out", 2), ("ssm_out", 4), ("mix", 2), ("ada1", 4),
         ("up", 11), ("down", 8), ("ada2", 4), ("qk", 4), ("v", 2), ("gate2", 4), ("proj_m", 1), ("proj_d", 1), ("out2", 2)]
UNIT, NUNITS = offsets(UNITS)
HALVES = ("glu", "up")
SLOT = 4096


def T0(name):
    return TILE[name][0]


def U0(name):
    return UNIT[name][0]


def program(nc, x, params, consts, w_in, w_conv_out, w_ssm_out, w_o, w_up, w_down, w_ada, w_in2, w_pm, w_pd, w_out2,
            w_route, w_gate_e, w_up_e, w_down_e, out):
    with ExitStack() as ctx:
        def sb(name, n, dt=F32):
            return ctx.enter_context(nc.sbuf_tensor(name, [P, n], dt))

        def sem(name):
            return ctx.enter_context(nc.semaphore(name))

        def v3(ap, b):
            return ap.rearrange("p (a b) -> p a b", b=b)

        par_t, con_t = sb("par", NPAR), sb("con", NCON)

        def par(name, a=0, n=None):
            o, w = PAR[name]
            return par_t[:, o + a:o + a + (w - a if n is None else n)]

        def con(name):
            o, w = CON[name]
            return con_t[:, o:o + w]

        def par_at(name, j):
            return par_t[:, ds(j + PAR[name][0], 1)]

        ident, upper, before, ones, swap_m = (con(n) for n in ("ident", "upper", "before", "ones", "swap"))
        dense = [sb(f"dense{s}", SLOT) for s in range(2)]
        arena = sb("arena", 6 * SLOT)
        expert = [arena[:, s * SLOT:(s + 1) * SLOT] for s in range(6)]
        wdt = sb("wdt", KD * H)
        wroute = sb("wroute", KD * (EG + E_))
        hT_t, resid_t, sc1_t, sc2_t = sb("hT", KD * T), sb("resid", KD * T), sb("scratch1", KD * T), sb("scratch2", KD * T)
        hT, resid, scr1, scr2 = v3(hT_t[:], T), v3(resid_t[:], T), v3(sc1_t[:], T), v3(sc2_t[:], T)
        region = sb("region", KF * T)
        stat = sb("stat", 4 * T)
        small = sb("small", 448)

        at = [0]

        def carve(base, n):
            at[0] += n
            return base[:, at[0] - n:at[0]]

        x_tok = carve(arena, TT * D)
        conv_t = x_tok
        glu_v = carve(arena, KD * (T + CK - 1))
        xbc_t = carve(arena, KX * T)
        z_t = carve(arena, KS * T)
        ga_t = carve(arena, KS * T)
        yz_t = carve(arena, KS * T)
        assert at[0] <= 6 * SLOT
        x_tok, conv_o, glu_v, xbcT, zs, gates, yz = (v3(x_tok, D), v3(conv_t, T), v3(glu_v, T + CK - 1), v3(xbc_t, T),
                                                     v3(z_t, T), v3(ga_t, T), v3(yz_t, T))
        at[0] = 0
        xdt = v3(carve(region, TT * SSM), SSM)
        btok = carve(region, G * P)
        xds = v3(carve(region, 2 * 8 * HD), 8 * HD)
        abc = v3(sc1_t[:, 0:1024], 512)
        ein = v3(sc1_t[:, 1024:2048], 512)
        cexp = v3(sc2_t[:, 0:1024], 512)
        state = v3(sc2_t[:, 1024:2048], 512)
        ssm_sq = v3(region[:, 0:KS * T], T)
        half_t = v3(sc1_t[:, 0:1024], 512)
        sig_t = v3(sc2_t[:, 0:512], T)
        act_t = v3(region[:], T)
        at[0] = 0
        qk = v3(carve(region, 4 * 4 * T), T)
        vm = v3(carve(region, TT * QK), QK)
        at[0] = 4 * SLOT
        vd = v3(carve(arena, TT * QK), QK)
        om = v3(carve(arena, 4 * T), T)
        od = v3(carve(arena, 4 * T), T)
        gates2_t = carve(arena, KS * T)
        gates2 = v3(gates2_t, T)
        osq = v3(sc2_t[:, 1024:2048], T)
        raw = [sc1_t[:, i * 512:(i + 1) * 512] if i < 4 else sc2_t[:, (i - 4) * 512:(i - 3) * 512] for i in range(8)]
        srow = v3(sc1_t[:, 0:1024], 512)
        prob = v3(sc1_t[:, 1024:2048], 512)
        prT = v3(sc2_t[:, 0:768], 384)
        rtmp = stat[:, 0:512]
        sls, sgate = dense[0][:, 0:4 * TT * CAP], dense[0][:, 4 * TT * CAP:4 * TT * CAP + 8 * CAP]
        at[0] = 0
        htok = v3(carve(region, TT * D), D)
        oute = v3(carve(region, 2 * D), D)
        hid = carve(region, 2 * 4 * CAP)
        sel = v3(carve(region, 2 * 4 * CAP), 4 * CAP)
        wsel = v3(sls, 4 * CAP)
        selT = v3(carve(region, 2 * T), T)
        xe = v3(sc2_t[:, 0:2 * KD * 2 * CAP], KD * 2 * CAP)
        yacc = scr1

        at[0] = 0
        dtr, dtx, dte, dta, dts, eal = (carve(small, n) for n in (64, 64, 64, 64, 64, 32))
        mod = carve(small, 48)
        cact = carve(small, 8)
        lam = carve(small, 4)
        dstate = carve(small, 32)
        assert at[0] <= 448
        gs1, gs2, g1h = sb("gs1", 8), sb("gs2", 8), sb("g1h", 8)
        acs = sb("acs", 64)
        lamp = sb("lamp", 128)
        mx, ssum, rsum = sb("mx", 4), sb("ssum", 4), sb("rsum", 4)
        lg = sb("lg", TT * (EG + E_))
        rt = sb("rt", 640)
        wexp, rank = sb("wexp", TT * E_), sb("rank", TT * E_)

        at[0] = 0

        def rcarve(n, w=None):
            r = carve(rt, n)
            return r if w is None else v3(r, w)

        mask_t = rcarve(TT * E_)
        mask = v3(mask_t, E_)
        r_ghot, r_exp, r_prod = rcarve(TT * EG, EG), rcarve(TT * EG), rcarve(TT * E_)
        r_el, r_el2, r_hot1, r_hot2, r_wx = (rcarve(TT * EP, EP) for _ in range(5))
        r_top, r_tmp, r_m1, r_m2, r_e2, r_gs, r_w1, r_w2 = (rcarve(TT) for _ in range(8))
        cnt_f, cnt_i = sb("cnt_f", 1), sb("cnt_i", 1, I32)

        bank = [ctx.enter_context(nc.psum_tensor(f"bank{b}", [P, 512], F32)) for b in range(8)]

        sems = {}

        def sem_(name):
            if name not in sems:
                sems[name] = sem(name)
            return sems[name]

        params_in, x_in = sem("params_in"), sem("x_in")
        dense_in = [sem(f"dense_in{s}") for s in range(2)]
        expert_in = [sem(f"expert_in{s}") for s in range(6)]
        tile_done = sem("tile_done")
        tile_read = [sem(f"tile_read{b}") for b in range(NB)]
        act_step, dve_step = sem("act_step"), sem("dve_step")
        out_written = sem("out_written")

        class Own:

            def __init__(self, eng, sm):
                self.eng, self.sm, self.n = eng, sm, 0

            def do(self, ins):
                ins.then_inc(self.sm, 1)
                self.n = self.n + 1
                self.eng.wait_ge(self.sm, self.n)

            def turns(self, i, per, count):
                self.before, self.per, self.count = self.n, per, count
                self.n = self.n + i * per

            def end(self):
                self.n = self.before + self.per * self.count

        def wait_read(eng, n, turn=0):
            eng.wait_ge(tile_read[n % NB], n // NB + 2 + turn)

        def wait_all_read(eng, name):
            t0, k = TILE[name]
            for n in range(max(t0, t0 + k - NB), t0 + k):
                wait_read(eng, n)

        def wait_tile(eng, name, t, turn=0):
            eng.wait_ge(tile_done, T0(name) + t + 1 + NB * turn)
            return bank[(T0(name) + t) % NB]

        def read_sem(name, t):
            return tile_read[(T0(name) + t) % NB]

        def arrived(n):
            names = [k for m in range(n % 2, n + 1, 2) for k, (u, c) in UNIT.items() if u <= m < u + c]
            return sum(32 if k in HALVES else 16 for k in names)

        def rows(w):
            return w.rearrange("(k p) n -> p k n", p=P)

        wi, wco, wso, wo_, wdn = rows(w_in), rows(w_conv_out), rows(w_ssm_out), rows(w_o), rows(w_down)
        wada, wi2, wpm, wpd, wo2 = rows(w_ada), rows(w_in2), rows(w_pm), rows(w_pd), rows(w_out2)
        wge = w_gate_e.rearrange("e (k p) n -> p e k n", p=P)
        wue = w_up_e.rearrange("e (k p) n -> p e k n", p=P)
        wde = w_down_e.rearrange("e (k p) n -> p e k n", p=P)
        wup2 = w_up.rearrange("(k p) (h n) -> p k h n", p=P, h=2)
        wglu2 = w_in[:, 0:2 * D].rearrange("(k p) (h n) -> p k h n", p=P, h=2)

        NPAIR = E_ // 2
        NPASS = T // CAP

        block = ctx.enter_context(nc.Block())

        @block.sync
        def _(sp):
            sp.dma_start(x_tok, x.rearrange("(c p) n -> p c n", p=P)).then_inc(x_in, 16)

            def last_use(n):
                name = [k for k, (u, c) in UNIT.items() if u <= n < u + c][0]
                u, units, tiles = n - U0(name), UNIT[name][1], TILE[name][1]
                if name[:3] == "ada":
                    return (tile_done, T0(name) + 1) if u == 3 else (sem_("ada_unit"), 3 * int(name[3]) + u + 1)
                if name == "down":
                    return (tile_done, T0(name) + u // 2 + 1) if u % 2 else (sem_("down_unit"), u // 2 + 1)
                return tile_done, T0(name) + (u + 1) * tiles // units

            def load(name, u, shape, src, turn=0):
                n = U0(name) + u
                if n >= 2:
                    sm, v = last_use(n - 2)
                    if u >= 2:
                        v = v + turn * (last_use(n)[1] - v)
                    sp.wait_ge(sm, v)
                if name in HALVES:
                    for h in range(2):
                        sp.dma_start(shape(dense[n % 2])[:, :, h, :], src[:, :, h, :]).then_inc(dense_in[n % 2], 16)
                else:
                    sp.dma_start(shape(dense[n % 2]), src).then_inc(dense_in[n % 2], 16)

            def stage(name, units, shape, cols):
                for u in range(2):
                    load(name, u, shape, cols(u))
                if units >= 4:
                    with sp.Fori(0, units // 2 - 1) as i:
                        for u in range(2, 4):
                            load(name, u, shape, cols(i * 2 + u), i)

            def flat(t):
                return v3(t[:], 512)

            def halves(t):
                return t[:].rearrange("p (k h n) -> p k h n", k=KD, h=2)

            stage("xbc", 6, flat, lambda u: wi[:, :, ds(u * 512 + C_XBC, 512)])
            stage("glu", 4, halves, lambda u: wglu2[:, :, :, ds(u * 256, 256)])
            stage("z", 4, flat, lambda u: wi[:, :, ds(u * 512 + C_Z, 512)])
            stage("gate", 4, flat, lambda u: wi[:, :, ds(u * 512 + C_GA, 512)])
            for u in range(4):
                load("ada0", u, flat, wada[:, :, u * 512:(u + 1) * 512])
            stage("conv_out", 2, flat, lambda u: wco[:, :, ds(u * 512, 512)])
            stage("ssm_out", 4, lambda t: v3(t[:], 256), lambda u: wso[:, :, ds(u * 256, 256)])
            stage("mix", 2, flat, lambda u: wo_[:, :, ds(u * 512, 512)])
            for u in range(4):
                load("ada1", u, flat, wada[:, :, (u + 4) * 512:(u + 5) * 512])
            stage("up", 10, halves, lambda u: wup2[:, :, :, ds(u * 256, 256)])
            load("up", 10, halves, wup2[:, :, :, 2560:2816])
            for u in range(8):
                load("down", u, lambda t: v3(t[:, 0:KF * P], P), wdn[:, :, u * P:(u + 1) * P])
            for u in range(4):
                load("ada2", u, flat, wada[:, :, (u + 8) * 512:(u + 9) * 512])

            def load_expert(s, e, pair):
                w, k = [(wge, KD), (wue, KD), (wge, KD), (wue, KD), (wde, 4), (wde, 4)][s]
                src = w[:, ds(pair * 2 + e, 1), :, :].rearrange("p e k n -> p (e k) n")
                sp.dma_start(v3(expert[s], SLOT // k), src).then_inc(expert_in[s], 16)

            OF = [0, 0, 1, 1, 0, 1]

            wait_all_read(sp, "mix")
            for s in range(4):
                load_expert(s, OF[s], 0)
            for u, c in enumerate((0, 512, 1536, 2048)):
                load("qk", u, flat, wi2[:, :, c:c + 512])
            for u, c in enumerate((1024, 2560)):
                load("v", u, flat, wi2[:, :, c:c + 512])
            stage("gate2", 4, flat, lambda u: wi2[:, :, ds(u * 512 + 3072, 512)])
            load("proj_m", 0, lambda t: v3(t[:], D), wpm)
            load("proj_d", 0, lambda t: v3(t[:], D), wpd)
            stage("out2", 2, flat, lambda u: wo2[:, :, ds(u * 512, 512)])
            wait_all_read(sp, "out2")
            for s in (4, 5):
                load_expert(s, OF[s], 0)

            def refill(pair, v):
                for s in range(6):
                    sm, at_ = [("gate_used", v * 2 - 1), ("up_used", v * 2 - 1), ("gate_used", v * 2),
                               ("up_used", v * 2), ("down0_used", v), ("down1_used", v)][s]
                    sp.wait_ge(sem_(sm), at_)
                    load_expert(s, OF[s], pair)

            with sp.Fori(1, NPAIR) as i:
                refill(i, i)
            sp.wait_ge(sem_("counted"), 1)
            n_max = sp.value_load(cnt_i[0:1, 0:1], min_val=0, max_val=T)
            for b in range(1, NPASS):
                with sp.If(n_max > b * CAP):
                    with sp.Fori(0, NPAIR) as i:
                        refill(i, i + b * NPAIR)
            sp.wait_ge(sem_("out_ready"), 4)
            sp.dma_start(out.rearrange("(c p) n -> p c n", p=P), v3(sc1_t[:], D)).then_inc(out_written, 16)
            sp.wait_ge(out_written, 16)

        @block.gpsimd
        def _(pool):
            nc.gpsimd.memset(glu_v[:, :, 0:CK - 1], 0.0).then_inc(sem_("padded"), 1)
            n = 0
            pool.wait_ge(sem_("decay_ready"), 1)
            for g in range(G):
                wait_read(pool, T0("xtok") + g)
                if g >= 2:
                    pool.wait_ge(sem_("state_done"), g - 1)
                nc.gpsimd.tensor_tensor(
                    xds[:, g % 2, :].rearrange("p (h d) -> p h d", h=8),
                    xdt[:, 0, g * 512:(g + 1) * 512].rearrange("p (h d) -> p h d", h=8),
                    dstate[:, g * 8:(g + 1) * 8].unsqueeze(2).to_broadcast([P, 8, HD]), ALU.mult
                ).then_inc(sem_("xds_ready"), 1)
                if g == 0:
                    pool.wait_ge(sem_("cn_scaled"), KD)
                for hf in range(2):
                    for c in range(TT):
                        if n >= 2:
                            pool.wait_ge(sem_("seg_done"), n - 1)
                        h0 = c * H + g * 8 + hf * 4
                        nc.gpsimd.tensor_copy(abc[:, n % 2, :].rearrange("p (h t) -> p h t", h=4),
                                              dta[:, h0:h0 + 4].unsqueeze(2).to_broadcast([P, 4, P])
                                              ).then_inc(sem_("abc_ready"), 1)
                        n += 1

            def ffn_product(t, turn=0):
                pool.wait_ge(sem_("silu_gate"), t + 1 + 4 * turn)
                nc.gpsimd.tensor_tensor(act_t[:, ds(turn * 4 + t, 1), :], sig_t[:, t % 2:t % 2 + 1, :],
                                        half_t[:, t % 2, T:2 * T].unsqueeze(1), ALU.mult
                                        ).then_inc(sem_("act_ready"), 1)

            with pool.Fori(0, 5) as i:
                for t in range(4):
                    ffn_product(t, i)
            for t in (20, 21):
                ffn_product(t)

        @block.tensor
        def _(pe):
            mm, tr = nc.tensor.matmul, nc.tensor.transpose

            def open_tile(name, t, turn=0):
                n = T0(name) + t
                pe.wait_ge(tile_read[n % NB], n // NB + 1 + turn)
                return bank[n % NB]

            def have(name, u, turn=0):
                n = U0(name) + u
                pe.wait_ge(dense_in[n % 2], arrived(n) + turn * (32 if name in HALVES else 16))
                return dense[n % 2]

            def tile(name, t, turn, k_n, chunk, src):
                b = v3(open_tile(name, t, turn)[:], T)
                for m in range(2):
                    for k in range(k_n):
                        last = mm(b[:, m, :], chunk(k, m), src[:, k, :], start=k == 0, stop=k == k_n - 1)
                last.then_inc(tile_done, 1)

            def unit_512(name, u, src, turn=0):
                w = v3(have(name, u, turn)[:], 512)
                for j in range(2):
                    tile(name, 2 * u + j, turn, KD, lambda k, m: w[:, k, (2 * j + m) * P:(2 * j + m + 1) * P], src)

            def unit_halves(name, u, src, turn=0):
                w = have(name, u, turn)[:].rearrange("p (k h n) -> p k h n", k=KD, h=2)
                for j in range(2):
                    tile(name, 2 * u + j, turn, KD, lambda k, m: w[:, k, m, j * P:(j + 1) * P], src)

            def stage(name, units, unit, src):
                with pe.Fori(0, units // 2) as i:
                    for u in range(2):
                        unit(name, u, src, i)

            def stage_ada(name, half):
                b = open_tile(name, 0) if half == 0 else bank[T0(name) % NB]
                for u in range(2 * half, 2 * half + 2):
                    w = v3(have(name, u)[:], 512)
                    for m in range(4):
                        for k in range(KD):
                            last = mm(b[:, 4 * u + m:4 * u + m + 1], w[:, k, m * P:(m + 1) * P], cact[:, k:k + 1],
                                      start=k == 0, stop=k == KD - 1)
                    last.then_inc(sem_("ada_unit") if u < 3 else tile_done, 1)

            def norm(p, src, centre=True, filler=lambda: None):
                if centre:
                    for k in range(KD):
                        last = mm(bank[7][:, 0:T], ones, src[:, k, :], start=k == 0, stop=k == KD - 1)
                    last.then_inc(sem_(p + "_sum"), 1)
                filler()
                pe.wait_ge(sem_(p + "_sq"), 1)
                for k in range(KD):
                    last = mm(bank[7][:, 0:T], ones, scr2[:, k, :], start=k == 0, stop=k == KD - 1)
                last.then_inc(sem_(p + "_ssq"), 1)

            pe.wait_ge(params_in, 64)
            pe.wait_ge(sem_("xn_ready"), 1)
            for t in range(4):
                b = v3(open_tile("h", t)[:], T)
                for m in range(2):
                    for c in range(TT):
                        j = 2 * t + m
                        last = tr(b[:, m, c * P:(c + 1) * P], x_tok[:, c, j * P:(j + 1) * P], ident)
                last.then_inc(tile_done, 1)
            wait_all_read(pe, "h")
            wd = v3(wdt[:], H)
            for c in range(TT):
                for k in range(KD):
                    last = mm(bank[6][:, c * H:(c + 1) * H], hT[:, k, c * P:(c + 1) * P], wd[:, k, :],
                              start=k == 0, stop=k == KD - 1)
            last.then_inc(sem_("dt_done"), 1)
            stage("xbc", 6, unit_512, hT)
            pe.wait_ge(sem_("a_ready"), 1)
            for c in range(TT):
                mm(bank[6][:, c * H:(c + 1) * H], upper, dta[:, c * H:(c + 1) * H], start=True, stop=True)
            mm(bank[6][:, 2 * H:3 * H], ones, dta[:, 0:H], start=True, stop=True).then_inc(sem_("acs_done"), 1)
            stage("glu", 4, unit_halves, hT)
            pe.wait_ge(sem_("xbc_ready"), 12)
            for t in range(9):
                b = open_tile("xtok", t)
                for j in range(4):
                    if t < 8:
                        src = xbcT[:, (t % 4) * 4 + j, (t // 4) * P:(t // 4 + 1) * P]
                    else:
                        src = xbcT[:, KS + j, 0:P]
                    last = tr(b[:, j * P:(j + 1) * P], src, ident)
                last.then_inc(tile_done, 1)
            stage("z", 4, unit_512, hT)
            stage("gate", 4, unit_512, hT)
            pe.wait_ge(sem_("conv_ready"), 8)
            norm("cn", conv_o, filler=lambda: stage_ada("ada0", 0))
            stage_ada("ada0", 1)

            def seg(n):
                pe.wait_ge(sem_("abc_ready"), n + 1)
                if n >= 2:
                    pe.wait_ge(sem_("seg_masked"), n - 1)
                for j in range(4):
                    last = mm(bank[4 + n % 2][:, j * P:(j + 1) * P], abc[:, n % 2, j * P:(j + 1) * P], upper,
                              start=True, stop=True)
                last.then_inc(sem_("seg_done"), 1)

            order = [(g, hf, c) for g in range(G) for hf in range(2) for c in range(TT)]
            seg(0)
            for n, (g, hf, c) in enumerate(order):
                if hf == 0 and c == 0:
                    if g:
                        pe.wait_ge(sem_("mt_ready"), n)
                    for cc in range(TT):
                        last = mm(bank[6][:, cc * P:(cc + 1) * P], xbcT[:, KS + g, cc * P:(cc + 1) * P],
                                  xbcT[:, KS + G + g, cc * P:(cc + 1) * P], start=True, stop=True)
                    last.then_inc(sem_("cb_done"), 1)
                    if g == 0:
                        wait_read(pe, T0("xtok") + 8)
                        wait_read(pe, T0("xtok") + 7)
                    pe.wait_ge(sem_("xds_ready"), g + 1)
                    if g:
                        pe.wait_ge(sem_("state_ready"), g)
                    mm(bank[7][:, 0:512], btok[:, g * P:(g + 1) * P], xds[:, g % 2, :], start=True,
                       stop=True).then_inc(sem_("state_done"), 1)
                if n + 1 < len(order):
                    seg(n + 1)
                t = 2 * g + hf
                b = v3((open_tile("ssd", t) if c == 0 else bank[(T0("ssd") + t) % NB])[:], T)
                pe.wait_ge(sem_("mt_ready"), n + 1)
                if c == 1:
                    pe.wait_ge(sem_("ce_ready"), t + 1)
                    pe.wait_ge(sem_("state_ready"), g + 1)
                for j in range(4):
                    h, o = g * 8 + hf * 4 + j, (j % 2) * HD
                    dst = b[o:o + HD, j // 2, c * P:(c + 1) * P]
                    last = mm(dst, xdt[:, c, h * HD:(h + 1) * HD], ein[:, n % 2, j * P:(j + 1) * P],
                              start=True, stop=c == 0)
                    if c == 1:
                        last = mm(dst, state[:, g % 2, (hf * 4 + j) * HD:(hf * 4 + j + 1) * HD],
                                  cexp[:, hf, j * P:(j + 1) * P], start=False, stop=True)
                last.then_inc(sem_("y_half") if c == 0 else tile_done, 1)
            pe.wait_ge(sem_("cn_out"), KD)
            stage("conv_out", 2, unit_512, conv_o)
            for g in range(G):
                pe.wait_ge(sem_("ysq_ready"), g + 1)
                for k in range(4):
                    last = mm(bank[4 + g // 2][:, (g % 2) * T:(g % 2 + 1) * T], ones, ssm_sq[:, 4 * g + k, :],
                              start=k == 0, stop=k == 3)
            last.then_inc(sem_("yssq_done"), 1)
            pe.wait_ge(sem_("yn_ready"), KS)
            for u in range(4):
                w = v3(have("ssm_out", u)[:], 256)
                tile("ssm_out", u, 0, KS, lambda k, m: w[:, k, m * P:(m + 1) * P], yz)
            pe.wait_ge(sem_("merged"), 4)
            stage("mix", 2, unit_512, gates)
            stage_ada("ada1", 0)
            wait_all_read(pe, "mix")
            norm("n1", resid, filler=lambda: stage_ada("ada1", 1))
            pe.wait_ge(sem_("n1_out"), KD)
            stage("up", 10, unit_halves, hT)
            unit_halves("up", 10, hT)
            pe.wait_ge(sem_("act_ready"), KF)
            for t in range(4):
                b = v3(open_tile("down", t)[:], T)
                for m in range(2):
                    w = v3(have("down", 2 * t + m)[:, 0:KF * P], P)
                    for k in range(KF):
                        last = mm(b[:, m, :], w[:, k, :], act_t[:, k, :], start=k == 0, stop=k == KF - 1)
                    last.then_inc(tile_done if m else sem_("down_unit"), 1)
            stage_ada("ada2", 0)
            wait_all_read(pe, "down")
            norm("n2", resid, filler=lambda: stage_ada("ada2", 1))
            norm("r1", resid, centre=False)
            pe.wait_ge(sem_("r1_out"), KD)
            for u in range(4):
                unit_512("qk", u, hT)
            for u in range(2):
                w = v3(have("v", u)[:], 512)
                for c in range(TT):
                    b = open_tile("v", 2 * u + c)
                    for k in range(KD):
                        last = mm(b[:], hT[:, k, c * P:(c + 1) * P], w[:, k, :], start=k == 0, stop=k == KD - 1)
                    last.then_inc(tile_done, 1)
            wait_all_read(pe, "qk")
            for t in range(8):
                b = open_tile("swap", t)
                mm(b[:], swap_m, raw[t], start=True, stop=True).then_inc(tile_done, 1)
            pe.wait_ge(sem_("rope_ready"), 8)

            def scores(a):
                if a >= 2:
                    pe.wait_ge(sem_("masked"), a - 1)
                o, j = (a % 2) * 64, (a // 2) % 4 + (8 if a >= 8 else 0)
                b = v3(bank[4 + a % 2][:], T)
                for c in range(TT):
                    last = mm(b[:, c, :], qk[o:o + 64, j, c * P:(c + 1) * P], qk[o:o + 64, j + 4, :],
                              start=True, stop=True)
                last.then_inc(sem_("scored"), 1)

            def attend(a):
                if a >= 8 and a % 2 == 0:
                    return
                n = a if a < 8 else 8 + (a - 8) // 2
                pe.wait_ge(sem_("prob_ready"), n + 1)
                if n:
                    pe.wait_ge(sem_("prT_ready"), n)
                for q, (c, kc) in enumerate(((0, 0), (1, 0), (1, 1))):
                    last = tr(bank[6][:, q * P:(q + 1) * P], prob[:, a % 2, c * T + kc * P:c * T + (kc + 1) * P], ident)
                last.then_inc(sem_("prT_done"), 1)
                pe.wait_ge(sem_("prT_ready"), n + 1)
                p = prT[:, n % 2, :]
                o, w, vv, hh = ((a % 2) * 64, 64, vm, a) if a < 8 else (0, P, vd, n - 8)
                if a == 0:
                    wait_all_read(pe, "v")
                elif a < 8 and a % 2 == 0:
                    pe.wait_ge(sem_("o_read"), a // 2)
                elif a >= 8:
                    pe.wait_ge(sem_("o_read"), n - 4)
                mm(bank[7][o:o + w, 0:T], vv[:, 0, hh * w:(hh + 1) * w], p[:, 0:T], start=True, stop=False)
                mm(bank[7][o:o + w, P:T], vv[:, 1, hh * w:(hh + 1) * w], p[:, T:T + P], start=False,
                   stop=True).then_inc(sem_("o_done"), 1)

            scores(0)
            for a in range(16):
                if a + 1 < 16:
                    scores(a + 1)
                if a % 4 == 0:
                    unit_512("gate2", a // 4, hT)
                attend(a)
            pe.wait_ge(sem_("osq_ready"), 1)
            for h in range(4):
                last = mm(bank[4 + h // 2][:, (h % 2) * T:(h % 2 + 1) * T], ones, osq[:, h, :], start=True, stop=True)
            last.then_inc(sem_("ossq_done"), 1)
            for name, src, ready, n in (("proj_m", om, "o_read", 8), ("proj_d", od, "on_ready", 4)):
                pe.wait_ge(sem_(ready), n)
                w = v3(have(name, 0)[:], D)
                for t in range(4):
                    tile(name, t, 0, 4, lambda k, m: w[:, k, (2 * t + m) * P:(2 * t + m + 1) * P], src)
            pe.wait_ge(sem_("merged2"), 4)
            stage("out2", 2, unit_512, gates2)
            wait_all_read(pe, "out2")
            norm("r2", resid, centre=False)
            pe.wait_ge(sem_("r2_out"), KD)
            wr = v3(wroute[:], EG + E_)
            for c in range(TT):
                for k in range(KD):
                    last = mm(bank[6][:, c * 36:(c + 1) * 36], hT[:, k, c * P:(c + 1) * P], wr[:, k, :],
                              start=k == 0, stop=k == KD - 1)
            last.then_inc(sem_("logit_done"), 1)
            for t in range(4):
                c, half = t // 2, t % 2
                for j in range(4):
                    last = tr(bank[t][:, j * P:(j + 1) * P], hT[:, half * 4 + j, c * P:(c + 1) * P], ident)
                last.then_inc(sem_("htok_done"), 1)
            pe.wait_ge(sem_("mask_ready"), 1)
            mm(bank[7][:, 0:E_], before, mask[:, 0, :], start=True, stop=True)
            mm(bank[7][:, E_:2 * E_], before, mask[:, 1, :], start=True, stop=False)
            mm(bank[7][:, E_:2 * E_], ones, mask[:, 0, :], start=False, stop=True)
            mm(bank[7][:, 2 * E_:3 * E_], ones, mask[:, 0, :], start=True, stop=False)
            mm(bank[7][:, 2 * E_:3 * E_], ones, mask[:, 1, :], start=False, stop=True).then_inc(sem_("rank_done"), 1)
            pe.wait_ge(sem_("htok_ready"), 4)
            pe.wait_ge(sem_("zeroed"), 1)

            def gather(r, v):
                pe.wait_ge(sem_("sel_ready"), v + 1)
                for m in range(KD):
                    for c in range(TT):
                        last = mm(bank[m // 4][:, (m % 4) * 2 * CAP:(m % 4 + 1) * 2 * CAP], htok[:, c, m * P:(m + 1) * P],
                                  sel[:, r, c * 2 * CAP:(c + 1) * 2 * CAP], start=c == 0, stop=c == TT - 1)
                last.then_inc(sem_("gathered"), 1)

            def turn_selection(r, v):
                pe.wait_ge(sem_("y_added"), v * 4 + 4)
                for c in range(TT):
                    last = tr(bank[6][0:2 * CAP, c * P:(c + 1) * P],
                              wsel[:, r, c * 2 * CAP:(c + 1) * 2 * CAP], ident)
                last.then_inc(sem_("selT_done"), 1)

            def multiply(r, v):
                pe.wait_ge(sem_("xe_ready"), v * 2 + 2)
                for e in range(2):
                    pe.wait_ge(sem_("hid_ready"), v * 2 + e + 1)
                    for half in range(2):
                        pe.wait_ge(expert_in[2 * e + half], v * 16 + 16)
                        w = v3(expert[2 * e + half], 512)
                        for m in range(4):
                            for k in range(KD):
                                last = mm(bank[2 + e][:, (half * 4 + m) * CAP:(half * 4 + m + 1) * CAP],
                                          w[:, k, m * P:(m + 1) * P],
                                          xe[:, r, (k * 2 + e) * CAP:(k * 2 + e + 1) * CAP],
                                          start=k == 0, stop=k == KD - 1)
                        last.then_inc(sem_("up_used" if half else "gate_used"), 1)
                pe.wait_ge(sem_("oute_ready"), v * 2 + 2)
                for e in range(2):
                    pe.wait_ge(expert_in[4 + e], v * 16 + 16)
                    pe.wait_ge(sem_("hid_ready"), v * 2 + e + 3)
                    w = v3(expert[4 + e], D)
                    for half in range(2):
                        for k in range(4):
                            last = mm(bank[4 + half][e * CAP:(e + 1) * CAP, :],
                                      hid[:, (e * 4 + k) * CAP:(e * 4 + k + 1) * CAP],
                                      w[:, k, half * 512:(half + 1) * 512], start=k == 0, stop=k == 3)
                    last.then_inc(sem_(f"down{e}_used"), 1)

            def spread(r, v):
                pe.wait_ge(sem_("oute_ready"), v * 2 + 4)
                pe.wait_ge(sem_("selT_ready"), v + 1)
                for q in range(4):
                    pe.wait_ge(sem_("y_added"), v * 4 + max(q - 1, 0) + 4)
                    b = v3(bank[6 + q % 2][:], T)
                    for m in range(2):
                        j = 2 * q + m
                        last = mm(b[:, m, :], oute[0:2 * CAP, r, j * P:(j + 1) * P], selT[0:2 * CAP, r, :],
                                  start=True, stop=True)
                    last.then_inc(sem_("spread_done"), 1)

            def moe_pass(b):
                with pe.Fori(0, NPAIR // 2) as i:
                    v = i * 2 + b * NPAIR
                    gather(0, v)
                    turn_selection(0, v)
                    multiply(0, v)
                    gather(1, v + 1)
                    spread(0, v)
                    turn_selection(1, v + 1)
                    multiply(1, v + 1)
                    spread(1, v + 1)

            moe_pass(0)
            pe.wait_ge(sem_("counted"), 1)
            n_max = pe.value_load(cnt_i[0:1, 0:1], min_val=0, max_val=T)
            for b in range(1, NPASS):
                with pe.If(n_max > b * CAP):
                    moe_pass(b)
            norm("f", resid, centre=False)
            pe.wait_ge(sem_("f_scaled"), KD)
            for t in range(4):
                c, half = t // 2, t % 2
                for j in range(4):
                    last = tr(bank[t][:, j * P:(j + 1) * P], hT[:, half * 4 + j, c * P:(c + 1) * P], ident)
                last.then_inc(sem_("outT_done"), 1)

        @block.scalar
        def _(act):
            f = nc.scalar.activation
            own = Own(act, act_step)
            for dst, src in ((par_t[:], params), (con_t[:], consts),
                             (v3(wdt[:], H), rows(w_in)[:, :, C_DT:C_DT + H]),
                             (v3(wroute[:], EG + E_), rows(w_route))):
                act.dma_start(dst, src).then_inc(params_in, 16)

            def norm(p, src, b=None, func=ACT.Identity, dst=None, ready=None, ready_n=1):
                if ready is not None:
                    act.wait_ge(sem_(ready), ready_n)
                f(scr2[:], src[:], ACT.Square).then_inc(sem_(p + "_sq"), 1)
                act.wait_ge(sem_(p + "_var"), 1)
                f(stat[:, T:2 * T], stat[:, 0:T], ACT.Sqrt).then_inc(sem_(p + "_std"), 1)
                if b is not None:
                    for k in range(KD):
                        act.wait_ge(sem_(p + "_scaled"), k + 1)
                        f(dst[:, k, :], dst[:, k, :], func, bias=b(k)).then_inc(sem_(p + "_out"), 1)

            act.wait_ge(sem_("x_centred"), 1)
            for c in range(TT):
                f(sc2_t[:, c * D:(c + 1) * D], x_tok[:, c, :], ACT.Square,
                  accum_out=ssum[:, c:c + 1]).then_inc(sem_("x_sq"), 1)
            act.wait_ge(sem_("x_var"), 1)
            f(ssum[:, 0:2], ssum[:, 0:2], ACT.Sqrt).then_inc(sem_("x_std"), 1)
            act.wait_ge(params_in, 64)
            f(cact[:], par("c"), ACT.Silu).then_inc(sem_("c_ready"), 1)
            for t in range(4):
                b = wait_tile(act, "h", t)
                for m in range(2):
                    j = 2 * t + m
                    ins = f(hT[:, j, :], b[:, m * T:(m + 1) * T], ACT.Identity, scale=par("ln_in_g", j, 1),
                            bias=par("ln_in_b", j, 1))
                    if m == 0:
                        own.do(ins)
                    else:
                        ins.then_inc(read_sem("h", t), 1)
            wait_all_read(act, "h")
            f(resid_t[:], hT_t[:], ACT.Copy, scale=ALPHA).then_inc(sem_("resid_ready"), 1)
            act.wait_ge(sem_("dt_biased"), 1)
            own.do(f(dtx, dtr, ACT.Abs))
            own.do(f(dte, dtx, ACT.Exp, scale=-1.0))
            own.do(f(eal, par("a_log"), ACT.Exp))
            f(dtx, dte, ACT.Ln, bias=1.0).then_inc(sem_("log_ready"), 1)
            with act.Fori(0, 3) as i:
                for t in range(4):
                    wait_read(act, T0("xbc") + t, i)
                    own.turns(i, 4, 3) if t == 0 else None
                    for m in range(2):
                        j = i * 8 + (2 * t + m)
                        ins = f(xbcT[:, ds(j, 1), :], xbcT[:, ds(j, 1), :], ACT.Silu, bias=par_at("ssm_b", j))
                        if m == 0:
                            own.do(ins)
                        else:
                            ins.then_inc(sem_("xbc_ready"), 1)
            own.end()
            act.wait_ge(sem_("decay_diff"), 1)
            f(dstate, dstate, ACT.Exp).then_inc(sem_("decay_ready"), 1)
            with act.Fori(0, 2) as i:
                for t in range(4):
                    b = wait_tile(act, "glu", t, i)
                    f(sc2_t[:, t * T:(t + 1) * T], b[:, T:2 * T], ACT.Tanh, scale=0.5).then_inc(sem_("tanh_ready"), 1)
            b = wait_tile(act, "xtok", 8)
            f(btok, b[:], ACT.Copy).then_inc(read_sem("xtok", 8), 1)
            for name, func, dst, scale in (("z", ACT.Silu, z_t, 1.0), ("gate", ACT.Tanh, ga_t, 0.5)):
                with act.Fori(0, 2) as i:
                    for t in range(4):
                        b = wait_tile(act, name, t, i)
                        f(dst[:, ds(i * 2048 + t * 512, 512)], b[:], func, scale=scale).then_inc(read_sem(name, t), 1)
            norm("cn", scr1, b=lambda k: par("conv_ln_b", k, 1), func=ACT.Silu, dst=conv_o, ready="cn_centred")
            order = [(g, hf, c) for g in range(G) for hf in range(2) for c in range(TT)]

            def cexp_step(n):
                g, hf, c = order[n]
                if c == 1:
                    act.wait_ge(sem_("seg_done"), n + 1)
                    if g:
                        act.wait_ge(tile_done, T0("ssd") + 2 * (g - 1) + hf + 1)
                    f(cexp[:, hf, :], bank[4 + n % 2][:], ACT.Exp).then_inc(sem_("cexp_done"), 1)

            act.wait_ge(sem_("cn_ssq"), 1)
            cexp_step(0)
            for n, (g, hf, c) in enumerate(order):
                if n + 1 < len(order):
                    cexp_step(n + 1)
                act.wait_ge(sem_("seg_masked"), n + 1)
                f(ein[:, n % 2, :], ein[:, n % 2, :], ACT.Exp).then_inc(sem_("exp_done"), 1)
                if hf == 0 and c == 0:
                    act.wait_ge(sem_("state_done"), g + 1)
                    if g >= 2:
                        act.wait_ge(tile_done, T0("ssd") + 2 * (g - 2) + 2)
                    f(state[:, g % 2, :], bank[7][:], ACT.Copy).then_inc(sem_("state_ready"), 1)
            act.wait_ge(tile_done, T0("ssd") + 8)
            for g in range(G):
                act.wait_ge(sem_("yz_ready"), 2 * g + 2)
                f(ssm_sq[:, 4 * g:4 * g + 4, :], yz[:, 4 * g:4 * g + 4, :], ACT.Square).then_inc(sem_("ysq_ready"), 1)
            act.wait_ge(sem_("yvar_ready"), 2)
            f(stat[:], stat[:], ACT.Sqrt).then_inc(sem_("ystd_ready"), 1)
            norm("n1", scr1, b=lambda k: par("ln1_b", k, 1), dst=hT, ready="n1_centred")
            act.wait_ge(sem_("n1_out"), KD)
            f(resid_t[:], hT_t[:], ACT.Copy, scale=ALPHA).then_inc(sem_("resid_ready"), 1)

            def silu_gate(t, turn=0):
                act.wait_ge(sem_("ffn_conv"), t + 1 + 4 * turn)
                if t >= 2:
                    act.wait_ge(sem_("act_ready"), t - 1 + 4 * turn)
                f(sig_t[:, t % 2, :], half_t[:, t % 2, 0:T], ACT.Silu).then_inc(sem_("silu_gate"), 1)

            for t in range(4):
                silu_gate(t)
            with act.Fori(0, 4) as i:
                for t in range(4, 8):
                    silu_gate(t, i)
            for t in (20, 21):
                silu_gate(t)
            norm("n2", scr1, b=lambda k: par("ln2_b", k, 1), dst=resid, ready="n2_centred")
            norm("r1", resid, b=lambda k: mod[:, k:k + 1], dst=hT, ready="n2_out", ready_n=KD)
            act.wait_ge(sem_("r1_ssq"), 1)
            for t in range(8):
                b = wait_tile(act, "qk", t)
                f(raw[t], b[:], ACT.Copy).then_inc(read_sem("qk", t), 1)
            for t in range(4):
                b = wait_tile(act, "v", t)
                f((vm if t < 2 else vd)[:, t % 2, :], b[:], ACT.Copy).then_inc(read_sem("v", t), 1)

            def soften(a):
                act.wait_ge(sem_("max_ready"), a + 1)
                for c in range(TT):
                    f(prob[:, a % 2, c * T:(c + 1) * T], srow[:, a % 2, c * T:(c + 1) * T], ACT.Exp,
                      bias=mx[:, (a % 2) * 2 + c:(a % 2) * 2 + c + 1],
                      accum_out=ssum[:, (a % 2) * 2 + c:(a % 2) * 2 + c + 1]).then_inc(sem_("exped"), 1)

            def move(a):
                if a >= 8 and a % 2 == 0:
                    return
                n = a if a < 8 else 8 + (a - 8) // 2
                act.wait_ge(sem_("prT_done"), n + 1)
                f(prT[:, n % 2, :], bank[6][:, 0:384], ACT.Copy).then_inc(sem_("prT_ready"), 1)
                if a < 8 and a % 2 == 0:
                    return
                act.wait_ge(sem_("o_done"), n + 1)
                dst = om[:, a // 2, :] if a < 8 else od[:, n - 8, :]
                f(dst, bank[7][:, 0:T], ACT.Copy).then_inc(sem_("o_read"), 1)

            act.wait_ge(sem_("lam_sums"), 2)
            f(lam[:, 0:2], lam[:, 0:2], ACT.Exp).then_inc(sem_("lam_exp"), 1)
            soften(0)
            for a in range(16):
                if a + 1 < 16:
                    soften(a + 1)
                if a % 4 == 0:
                    for t in (a // 2, a // 2 + 1):
                        b = wait_tile(act, "gate2", t)
                        f(gates2_t[:, t * 512:(t + 1) * 512], b[:], ACT.Tanh, scale=0.5).then_inc(read_sem("gate2", t), 1)
                move(a)
            act.wait_ge(sem_("o_read"), 8)
            f(osq[:], od[:], ACT.Square).then_inc(sem_("osq_ready"), 1)
            act.wait_ge(sem_("ovar_ready"), 2)
            f(stat[:], stat[:], ACT.Sqrt).then_inc(sem_("ostd_ready"), 1)
            wait_all_read(act, "out2")
            norm("r2", resid, b=lambda k: mod[:, 24 + k:25 + k], dst=hT)
            act.wait_ge(sem_("route_exp"), 1)
            own.do(f(r_exp, r_exp, ACT.Exp))
            act.wait_ge(sem_("route_exp"), 2)
            f(r_e2, r_e2, ACT.Exp).then_inc(sem_("route_exped"), 1)
            for t in range(4):
                act.wait_ge(sem_("htok_done"), t + 1)
                c, half = t // 2, t % 2
                f(htok[:, c, half * 512:(half + 1) * 512], bank[t][:], ACT.Copy).then_inc(sem_("htok_ready"), 1)
            act.wait_ge(sem_("r2_ssq"), 1)

            def moe_pair(r, v):
                act.wait_ge(sem_("gathered"), v + 1)
                for q in range(2):
                    f(xe[:, r, q * 8 * CAP:(q + 1) * 8 * CAP], bank[q][:, 0:8 * CAP], ACT.Copy).then_inc(sem_("xe_ready"), 1)
                act.wait_ge(sem_("selT_done"), v + 3)
                f(selT[0:2 * CAP, r, :], bank[6][0:2 * CAP, 0:T], ACT.Copy).then_inc(sem_("selT_ready"), 1)
                for e in range(2):
                    act.wait_ge(sem_("up_used"), v * 2 + e + 1)
                    f(sgate[:, e * 4 * CAP:(e + 1) * 4 * CAP], bank[2 + e][:, 0:4 * CAP],
                      ACT.Silu).then_inc(sem_("gate_silu"), 1)
                act.wait_ge(sem_("down1_used"), v + 1)
                f(oute[0:2 * CAP, r, 0:512], bank[4][0:2 * CAP, :], ACT.Copy).then_inc(sem_("oute_ready"), 1)

            def moe_pass(b):
                with act.Fori(0, NPAIR // 2) as i:
                    for r in range(2):
                        moe_pair(r, i * 2 + (b * NPAIR + r))

            moe_pass(0)
            act.wait_ge(sem_("counted"), 1)
            n_max = act.value_load(cnt_i[0:1, 0:1], min_val=0, max_val=T)
            for b in range(1, NPASS):
                with act.If(n_max > b * CAP):
                    moe_pass(b)
            norm("f", resid, ready="x_final", ready_n=KD)
            for t in (0, 1):
                act.wait_ge(sem_("outT_done"), t + 1)
                f(sc1_t[:, t * 512:(t + 1) * 512], bank[t][:], ACT.Copy).then_inc(sem_("out_ready"), 1)

        @block.vector
        def _(dve):
            V = nc.vector
            own = Own(dve, dve_step)
            do = own.do
            stt, ts, tt = V.scalar_tensor_tensor, V.tensor_scalar, V.tensor_tensor

            def bc(ap, n):
                return ap.unsqueeze(1).to_broadcast([P, n, T])

            def norm(p, src, dst, g, eps, centre=True, scaled="_scaled"):
                x_ = src
                if centre:
                    dve.wait_ge(sem_(p + "_sum"), 1)
                    do(ts(stat[:, 0:T], bank[7][:, 0:T], 1.0 / D, None, ALU.mult))
                    tt(scr1[:], src[:], bc(stat[:, 0:T], KD), ALU.subtract).then_inc(sem_(p + "_centred"), 1)
                    x_ = scr1
                dve.wait_ge(sem_(p + "_ssq"), 1)
                if centre:
                    dve.wait_ge(sem_(p + "_centred"), 1)
                ts(stat[:, 0:T], bank[7][:, 0:T], 1.0 / D, eps, ALU.mult, ALU.add).then_inc(sem_(p + "_var"), 1)
                dve.wait_ge(sem_(p + "_std"), 1)
                do(V.reciprocal(stat[:, T:2 * T], stat[:, T:2 * T]))
                for k in range(KD):
                    stt(dst[:, k, :], x_[:, k, :], g(k), stat[:, T:2 * T], ALU.mult,
                        ALU.mult).then_inc(sem_(p + scaled), 1)

            for b in range(NB):
                dve.sem_inc(tile_read[b], 1)
            dve.wait_ge(x_in, 16)
            do(V.tensor_reduce(mx[:, 0:2], x_tok[:], AX_X, ALU.add))
            do(ts(mx[:, 0:2], mx[:, 0:2], 1.0 / D, None, ALU.mult))
            tt(x_tok[:], x_tok[:], mx[:, 0:2].unsqueeze(2).to_broadcast([P, TT, D]),
               ALU.subtract).then_inc(sem_("x_centred"), 1)
            dve.wait_ge(sem_("x_sq"), 2)
            ts(ssum[:, 0:2], ssum[:, 0:2], 1.0 / D, LN_EPS, ALU.mult, ALU.add).then_inc(sem_("x_var"), 1)
            dve.wait_ge(sem_("x_std"), 1)
            do(V.reciprocal(rsum[:, 0:2], ssum[:, 0:2]))
            tt(x_tok[:], x_tok[:], rsum[:, 0:2].unsqueeze(2).to_broadcast([P, TT, D]),
               ALU.mult).then_inc(sem_("xn_ready"), 1)
            dve.wait_ge(params_in, 64)
            dve.wait_ge(sem_("dt_done"), 1)
            tt(v3(dtr, H), v3(bank[6][:, 0:2 * H], H), par("dt_bias").unsqueeze(1).to_broadcast([P, TT, H]),
               ALU.add).then_inc(sem_("dt_biased"), 1)
            dve.wait_ge(sem_("log_ready"), 1)
            do(stt(dtr, dtr, 0.0, dtx, ALU.max, ALU.add))
            stt(v3(dta, H), v3(dtr, H), -1.0, eal.unsqueeze(1).to_broadcast([P, TT, H]), ALU.mult,
                ALU.mult).then_inc(sem_("a_ready"), 1)
            do(ts(par("conv_w"), par("conv_w"), 0.5, None, ALU.mult))
            with dve.Fori(0, 3) as i:
                own.turns(i, 28, 3)
                for t in range(4):
                    b = wait_tile(dve, "xbc", t, i)
                    for m in range(2):
                        j = i * 8 + (2 * t + m)
                        src = b[:, m * T:(m + 1) * T].unsqueeze(1)
                        do(ts(xbcT[:, ds(j, 1), :], src, par_at("ssm_w", j * 4 + 3), None, ALU.mult)) 
                        for s in range(1, 4):
                            ins = stt(xbcT[:, ds(j, 1), s:T], src[:, :, 0:T - s], par_at("ssm_w", j * 4 + (3 - s)),
                                      xbcT[:, ds(j, 1), s:T], ALU.mult, ALU.add)
                            if m == 1 and s == 3:
                                ins.then_inc(read_sem("xbc", t), 1)
                            else:
                                do(ins)
            own.end()
            dve.wait_ge(sem_("acs_done"), 1)
            do(V.tensor_copy(acs[:], bank[6][:, 0:2 * H]))
            tt(dstate, bank[6][:, 2 * H:3 * H], acs[:, 0:H], ALU.subtract).then_inc(sem_("decay_diff"), 1)
            with dve.Fori(0, 2) as i:
                for t in range(4):
                    b = wait_tile(dve, "glu", t, i)
                    dve.wait_ge(sem_("tanh_ready"), i * 4 + (t + 1))
                    stt(glu_v[:, ds(i * 4 + t, 1), CK - 1:], sc2_t[:, t * T:(t + 1) * T].unsqueeze(1), 1.0,
                        b[:, 0:T].unsqueeze(1), ALU.add, ALU.mult).then_inc(read_sem("glu", t), 1)
            for t in range(8):
                b = wait_tile(dve, "xtok", t)
                c, q = t // 4, t % 4
                tt(xdt[:, c, q * 512:(q + 1) * 512].rearrange("p (h d) -> p h d", h=8),
                   b[:].rearrange("p (h d) -> p h d", h=8),
                   dtr[:, c * H + q * 8:c * H + (q + 1) * 8].unsqueeze(2).to_broadcast([P, 8, HD]),
                   ALU.mult).then_inc(read_sem("xtok", t), 1)
            dve.wait_ge(sem_("padded"), 1)
            wait_all_read(dve, "glu")
            for k in range(KD):
                ts(conv_o[:, k, :], glu_v[:, k, 0:T], par("conv_w", k * CK, 1), par("conv_b", k, 1), ALU.mult,
                   ALU.add).then_inc(sem_("tap"), 1)
            with dve.Fori(1, CK) as i:
                for k in range(KD):
                    dve.wait_ge(sem_("tap"), i * KD + (k - KD + 1))
                    stt(conv_o[:, k, :], glu_v[:, k, ds(i, T)], par_at("conv_w", i + k * CK), conv_o[:, k, :],
                        ALU.mult, ALU.add).then_inc(sem_("tap"), 1)
            dve.wait_ge(sem_("tap"), CK * KD)
            dve.sem_inc(sem_("conv_ready"), 8)
            norm("cn", conv_o, conv_o, lambda k: par("conv_ln_g", k, 1), LN_EPS)
            dve.wait_ge(sem_("cn_scaled"), KD)

            def ada(q):
                b = wait_tile(dve, f"ada{q}", 0)
                tt(mod[:, 16 * q:16 * q + 16], b[:, 0:16], par("b_ada", 16 * q, 16),
                   ALU.add).then_inc(read_sem(f"ada{q}", 0), 1)

            ada(0)
            order = [(g, hf, c) for g in range(G) for hf in range(2) for c in range(TT)]

            def mask_step(n):
                g, hf, c = order[n]
                dve.wait_ge(sem_("seg_done"), n + 1)
                if c == 1:
                    dve.wait_ge(sem_("cexp_done"), 2 * g + hf + 1)
                if n >= 2:
                    dve.wait_ge(*((sem_("y_half"), n // 2) if c == 0 else (tile_done, T0("ssd") + (n - 2) // 2 + 1)))
                for j in range(4):
                    h = c * H + g * 8 + hf * 4 + j
                    ins = stt(ein[:, n % 2, j * P:(j + 1) * P], bank[4 + n % 2][:, j * P:(j + 1) * P], acs[:, h:h + 1],
                              con("ssm_mask"), ALU.subtract, ALU.add)
                    if j == 3:
                        ins.then_inc(sem_("seg_masked"), 1)
                    else:
                        ins.then_inc(dve_step, 1)
                        own.n = own.n + 1
                own.eng.wait_ge(dve_step, own.n)

            def gate_ssd(t):
                b = wait_tile(dve, "ssd", t)
                for m in range(2):
                    j = 2 * t + m
                    ins = stt(yz[:, j, :], xbcT[:, j, :], par("ssm_d", j, 1), b[:, m * T:(m + 1) * T], ALU.mult, ALU.add)
                    if m == 0:
                        do(ins)
                    else:
                        ins.then_inc(read_sem("ssd", t), 1)
                wait_read(dve, T0("ssd") + t)
                tt(yz[:, 2 * t:2 * t + 2, :], yz[:, 2 * t:2 * t + 2, :], zs[:, 2 * t:2 * t + 2, :],
                   ALU.mult).then_inc(sem_("yz_ready"), 1)

            wait_all_read(dve, "z")
            mask_step(0)
            for n, (g, hf, c) in enumerate(order):
                if n + 1 < len(order):
                    mask_step(n + 1)
                dve.wait_ge(sem_("exp_done"), n + 1)
                dve.wait_ge(sem_("cb_done"), g + 1)
                tt(v3(ein[:, n % 2, :], P), v3(ein[:, n % 2, :], P),
                   bank[6][:, c * P:(c + 1) * P].unsqueeze(1).to_broadcast([P, 4, P]),
                   ALU.mult).then_inc(sem_("mt_ready"), 1)
                if c == 1:
                    tt(v3(cexp[:, hf, :], P), v3(cexp[:, hf, :], P),
                       xbcT[:, KS + G + g, P:2 * P].unsqueeze(1).to_broadcast([P, 4, P]),
                       ALU.mult).then_inc(sem_("ce_ready"), 1)
                if c == 0 and n >= 2:
                    gate_ssd(n // 2 - 1)
            gate_ssd(7)
            wait_all_read(dve, "gate")
            for t in range(4):
                b = wait_tile(dve, "conv_out", t)
                stt(gates[:, 2 * t:2 * t + 2, :], gates[:, 2 * t:2 * t + 2, :], 1.0, v3(b[:], T), ALU.add,
                    ALU.mult).then_inc(read_sem("conv_out", t), 1)
            dve.wait_ge(sem_("yssq_done"), 1)
            for q in range(2):
                ts(stat[:, q * 512:(q + 1) * 512], bank[4 + q][:], 1.0 / 512, RMS_EPS, ALU.mult,
                   ALU.add).then_inc(sem_("yvar_ready"), 1)
            dve.wait_ge(sem_("ystd_ready"), 1)
            do(V.reciprocal(stat[:], stat[:]))
            dve.wait_ge(sem_("ysq_ready"), 4)
            for j in range(KS):
                g = j // 4
                stt(yz[:, j, :], yz[:, j, :], par("ssm_norm", j, 1), stat[:, g * T:(g + 1) * T], ALU.mult,
                    ALU.mult).then_inc(sem_("yn_ready"), 1)
            for t in range(4):
                b = wait_tile(dve, "ssm_out", t)
                stt(gates[:, 8 + 2 * t:10 + 2 * t, :], gates[:, 8 + 2 * t:10 + 2 * t, :], 1.0, v3(b[:], T), ALU.add,
                    ALU.mult).then_inc(read_sem("ssm_out", t), 1)
                wait_read(dve, T0("ssm_out") + t)
                wait_read(dve, T0("conv_out") + t)
                tt(gates[:, 2 * t:2 * t + 2, :], gates[:, 2 * t:2 * t + 2, :], gates[:, 8 + 2 * t:10 + 2 * t, :],
                   ALU.add).then_inc(sem_("merged"), 1)
            dve.wait_ge(sem_("resid_ready"), 1)
            for t in range(4):
                b = wait_tile(dve, "mix", t)
                stt(resid[:, 2 * t:2 * t + 2, :], v3(b[:], T), 0.5, resid[:, 2 * t:2 * t + 2, :], ALU.mult,
                    ALU.add).then_inc(read_sem("mix", t), 1)
            wait_all_read(dve, "mix")
            norm("n1", resid, hT, lambda k: par("ln1_g", k, 1), LN_EPS)
            ada(1)

            def ffn_conv(t, turn=0):
                b = wait_tile(dve, "up", t, turn)
                if t >= 2:
                    dve.wait_ge(sem_("act_ready"), t - 1 + 4 * turn)
                for m in range(2):
                    ch = turn * 4 + (t + m * KF)
                    src, dst = b[:, m * T:(m + 1) * T], half_t[:, t % 2, m * T:(m + 1) * T]
                    do(ts(dst, src, par_at("ffn_w", ch * 3 + 2), par_at("ffn_b", ch), ALU.mult, ALU.add))
                    for s in (1, 2):
                        ins = stt(dst[:, s:T], src[:, 0:T - s], par_at("ffn_w", ch * 3 + (2 - s)), dst[:, s:T],
                                  ALU.mult, ALU.add)
                        if (m, s) == (1, 2):
                            do(ins)
                        else:
                            do(ins)
                dve.sem_inc(read_sem("up", t), 1)
                dve.sem_inc(sem_("ffn_conv"), 1)

            dve.wait_ge(sem_("n1_scaled"), KD)
            for t in range(4):
                ffn_conv(t)
            with dve.Fori(0, 4) as i:
                own.turns(i, 24, 4)
                for t in range(4, 8):
                    ffn_conv(t, i)
            own.end()
            for t in (20, 21):
                ffn_conv(t)
            dve.wait_ge(sem_("resid_ready"), 2)
            for t in range(4):
                b = wait_tile(dve, "down", t)
                tt(resid[:, 2 * t:2 * t + 2, :], v3(b[:], T), resid[:, 2 * t:2 * t + 2, :],
                   ALU.add).then_inc(read_sem("down", t), 1)
            wait_all_read(dve, "down")
            norm("n2", resid, resid, lambda k: par("ln2_g", k, 1), LN_EPS)
            ada(2)
            wait_read(dve, T0("ada2"))
            do(stt(gs1[:], mod[:, 8:16], 1.0, par("norm1_g"), ALU.add, ALU.mult))
            do(stt(gs2[:], mod[:, 32:40], 1.0, par("norm2_g"), ALU.add, ALU.mult))
            do(ts(g1h[:], mod[:, 16:24], 0.5, None, ALU.mult))
            do(ts(par("subln_g"), par("subln_g"), 1.0 - LAM_INIT, None, ALU.mult))
            for q, (a, b) in enumerate((("lam_q1", "lam_k1"), ("lam_q2", "lam_k2"))):
                do(tt(lamp[:, q * 64:(q + 1) * 64], par(a), par(b), ALU.mult))
                V.tensor_reduce(lam[:, q:q + 1], lamp[:, q * 64:(q + 1) * 64], AX_X, ALU.add).then_inc(sem_("lam_sums"), 1)
            norm("r1", resid, hT, lambda k: gs1[:, k:k + 1], NORM_EPS, centre=False)
            dve.wait_ge(sem_("r1_scaled"), KD)
            cos, sin = bc(con("cos"), 2), bc(con("sin"), 2)
            for t in range(8):
                b = wait_tile(dve, "swap", t)
                dst = qk[:, 2 * t:2 * t + 2, :]
                do(tt(dst, v3(raw[t], T), cos, ALU.mult))
                tt(v3(rtmp, T), v3(b[:], T), sin, ALU.mult).then_inc(read_sem("swap", t), 1)
                wait_read(dve, T0("swap") + t)
                tt(dst, dst, v3(rtmp, T), ALU.add).then_inc(sem_("rope_ready"), 1)
                dve.wait_ge(sem_("rope_ready"), t + 1)
            dve.wait_ge(sem_("lam_exp"), 1)
            do(tt(lam[:, 2:3], lam[:, 1:2], lam[:, 0:1], ALU.subtract))
            do(ts(lam[:, 3:4], lam[:, 2:3], LAM_INIT, None, ALU.subtract))

            def maxima(a):
                r = a % 2
                dve.wait_ge(sem_("scored"), a + 1)
                if a >= 2:
                    dve.wait_ge(sem_("exped"), 2 * (a - 1))
                stt(srow[:, r, :], bank[4 + r][:], 0.125, con("att_mask"), ALU.mult, ALU.add).then_inc(sem_("masked"), 1)
                dve.wait_ge(sem_("masked"), a + 1)
                do(V.tensor_reduce(mx[:, 2 * r:2 * r + 2], v3(srow[:, r, :], T), AX_X, ALU.max))
                ts(mx[:, 2 * r:2 * r + 2], mx[:, 2 * r:2 * r + 2], -1.0, None, ALU.mult).then_inc(sem_("max_ready"), 1)

            maxima(0)
            for a in range(16):
                r = a % 2
                if a < 8 or r == 0:
                    if a >= 1:
                        dve.wait_ge(sem_("prT_done"), a if a <= 8 else 8 + (a - 8) // 2)
                    maxima(a + 1)
                dve.wait_ge(sem_("exped"), 2 * (a + 1))
                do(V.reciprocal(rsum[:, 2 * r:2 * r + 2], ssum[:, 2 * r:2 * r + 2]))
                pr = v3(prob[:, r, :], T)
                if a < 8 or r == 0:
                    ins = tt(pr, pr, rsum[:, 2 * r:2 * r + 2].unsqueeze(2).to_broadcast([P, TT, T]), ALU.mult)
                    if a < 8:
                        ins.then_inc(sem_("prob_ready"), 1)
                    else:
                        do(ins)
                else:
                    do(ts(rsum[:, 2:4], rsum[:, 2:4], lam[:, 3:4], None, ALU.mult))
                    for c in range(TT):
                        ins = stt(pr[:, c, :], pr[:, c, :], rsum[:, 2 + c:3 + c], prob[:, 0, c * T:(c + 1) * T],
                                  ALU.mult, ALU.add)
                        if c == 0:
                            do(ins)
                        else:
                            ins.then_inc(sem_("prob_ready"), 1)
                    if a + 1 < 16:
                        dve.wait_ge(sem_("prob_ready"), 9 + (a - 8) // 2)
                        maxima(a + 1)
            dve.wait_ge(sem_("ossq_done"), 1)
            for q in range(2):
                ts(stat[:, q * 512:(q + 1) * 512], bank[4 + q][:], 1.0 / P, NORM_EPS, ALU.mult,
                   ALU.add).then_inc(sem_("ovar_ready"), 1)
            dve.wait_ge(sem_("ostd_ready"), 1)
            do(V.reciprocal(stat[:], stat[:]))
            for h in range(4):
                stt(od[:, h, :], od[:, h, :], par("subln_g"), stat[:, h * T:(h + 1) * T], ALU.mult,
                    ALU.mult).then_inc(sem_("on_ready"), 1)
            wait_all_read(dve, "gate2")
            for t in range(4):
                b = wait_tile(dve, "proj_m", t)
                stt(gates2[:, 2 * t:2 * t + 2, :], gates2[:, 2 * t:2 * t + 2, :], 1.0, v3(b[:], T), ALU.add,
                    ALU.mult).then_inc(read_sem("proj_m", t), 1)
            for t in range(4):
                b = wait_tile(dve, "proj_d", t)
                stt(gates2[:, 8 + 2 * t:10 + 2 * t, :], gates2[:, 8 + 2 * t:10 + 2 * t, :], 1.0, v3(b[:], T), ALU.add,
                    ALU.mult).then_inc(read_sem("proj_d", t), 1)
                wait_read(dve, T0("proj_d") + t)
                wait_read(dve, T0("proj_m") + t)
                tt(gates2[:, 2 * t:2 * t + 2, :], gates2[:, 2 * t:2 * t + 2, :], gates2[:, 8 + 2 * t:10 + 2 * t, :],
                   ALU.add).then_inc(sem_("merged2"), 1)
            for t in range(4):
                b = wait_tile(dve, "out2", t)
                for m in range(2):
                    j = 2 * t + m
                    ins = stt(resid[:, j, :], b[:, m * T:(m + 1) * T], g1h[:, j:j + 1], resid[:, j, :], ALU.mult, ALU.add)
                    if m == 0:
                        do(ins)
                    else:
                        ins.then_inc(read_sem("out2", t), 1)
            wait_all_read(dve, "out2")
            norm("r2", resid, hT, lambda k: gs2[:, k:k + 1], NORM_EPS, centre=False)

            def per_tile(ap, n):
                return ap.unsqueeze(2).to_broadcast([P, TT, n])

            def first_of_max(src, n, hot, top, tmp):
                place = con("place")[:, 0:n].unsqueeze(1).to_broadcast([P, TT, n])
                do(V.tensor_reduce(top, src, AX_X, ALU.max))
                do(tt(hot, src, per_tile(top, n), ALU.is_lt))
                do(stt(hot, hot, 64.0, place, ALU.mult, ALU.add))
                do(V.tensor_reduce(tmp, hot, AX_X, ALU.min))
                do(tt(hot, place, per_tile(tmp, n), ALU.is_equal))

            lg3 = v3(lg[:], EG + E_)
            dve.wait_ge(sem_("logit_done"), 1)
            do(tt(lg3[:], v3(bank[6][:, 0:2 * (EG + E_)], EG + E_), par("b_route").unsqueeze(1).to_broadcast([P, TT, EG + E_]),
                  ALU.add))
            gl = lg3[:, :, 0:EG]
            first_of_max(gl, EG, r_ghot, r_top, r_tmp)
            tt(v3(r_exp, EG), gl, per_tile(r_top, EG), ALU.subtract).then_inc(sem_("route_exp"), 1)
            el = lg3[:, :, EG:].rearrange("p c (g e) -> p c g e", g=EG)
            pr4 = r_prod.rearrange("p (c g e) -> p c g e", c=TT, g=EG)
            for c in range(TT):
                do(tt(pr4[:, c], el[:, c], r_ghot[:, c, :].unsqueeze(2).to_broadcast([P, EG, EP]), ALU.mult))
                do(V.tensor_reduce(r_el[:, c, :], pr4[:, c].rearrange("p g e -> p e g"), AX_X, ALU.add))
            first_of_max(r_el, EP, r_hot1, r_m1, r_tmp)
            do(stt(r_el2, r_hot1, NEG, r_el, ALU.mult, ALU.add))
            first_of_max(r_el2, EP, r_hot2, r_m2, r_tmp)
            tt(r_e2, r_m2, r_m1, ALU.subtract).then_inc(sem_("route_exp"), 1)
            dve.wait_ge(sem_("route_exped"), 1)
            do(V.tensor_reduce(r_gs, v3(r_exp, EG), AX_X, ALU.add))
            do(stt(r_w1, r_e2, 1.0, r_gs, ALU.add, ALU.mult))
            do(V.reciprocal(r_w1, r_w1))
            do(tt(r_w2, r_w1, r_e2, ALU.mult))
            do(tt(r_wx, r_hot1, per_tile(r_w1, EP), ALU.mult))
            do(tt(r_el, r_hot2, per_tile(r_w2, EP), ALU.mult))
            do(tt(r_wx, r_wx, r_el, ALU.add))
            do(tt(r_hot1, r_hot1, r_hot2, ALU.add))
            m4 = mask_t.rearrange("p (c g e) -> p c g e", c=TT, g=EG)
            w4 = wexp[:].rearrange("p (c g e) -> p c g e", c=TT, g=EG)
            for c in range(TT):
                gh = r_ghot[:, c, :].unsqueeze(2).to_broadcast([P, EG, EP])
                do(tt(w4[:, c], gh, r_wx[:, c, :].unsqueeze(1).to_broadcast([P, EG, EP]), ALU.mult))
                ins = tt(m4[:, c], gh, r_hot1[:, c, :].unsqueeze(1).to_broadcast([P, EG, EP]), ALU.mult)
                if c == 0:
                    do(ins)
                else:
                    ins.then_inc(sem_("mask_ready"), 1)
            dve.wait_ge(sem_("mask_ready"), 1)
            dve.wait_ge(sem_("rank_done"), 1)
            do(ts(rank[:], mask_t, -65536.0, 65536.0, ALU.mult, ALU.add))
            do(tt(rank[:], rank[:], bank[7][:, 0:2 * E_], ALU.add))
            do(V.tensor_reduce(cnt_f[:], bank[7][:, 2 * E_:3 * E_], AX_X, ALU.max))
            V.tensor_copy(cnt_i[:], cnt_f[:]).then_inc(sem_("counted"), 1)
            dve.wait_ge(sem_("r2_scaled"), KD)
            for q in range(4):
                V.memset(yacc[:, 2 * q:2 * q + 2, :], 0.0).then_inc(sem_("y_added"), 1)
            dve.sem_inc(sem_("hid_ready"), 2)
            dve.sem_inc(sem_("oute_ready"), 2)
            dve.sem_inc(sem_("selT_done"), 2)
            dve.sem_inc(sem_("zeroed"), 1)

            def select(own, r, pair, v):
                dve.wait_ge(sem_("selT_done"), v + 1)
                for c in range(TT):
                    for e in range(2):
                        at_ = (c * 2 + e) * CAP
                        col = pair * 2 + (c * E_ + e)
                        own.do(ts(sel[:, r, at_:at_ + CAP], con("slot"), rank[:, ds(col, 1)], None, ALU.is_equal))
                        ins = ts(wsel[:, r, at_:at_ + CAP], con("slot"), rank[:, ds(col, 1)], wexp[:, ds(col, 1)],
                                 ALU.is_equal, ALU.mult)
                        if (c, e) == (1, 1):
                            ins.then_inc(sem_("sel_ready"), 1)
                        else:
                            own.do(ins)

            def add_spread(v):
                for q in range(4):
                    dve.wait_ge(sem_("spread_done"), v * 4 + (q + 1))
                    dve.wait_ge(sem_("y_added"), v * 4 + (q + 1))
                    tt(yacc[:, 2 * q:2 * q + 2, :], yacc[:, 2 * q:2 * q + 2, :], v3(bank[6 + q % 2][:], T),
                       ALU.add).then_inc(sem_("y_added"), 1)

            def hidden(v):
                for e in range(2):
                    dve.wait_ge(sem_("gate_silu"), v * 2 + (e + 1))
                    tt(hid[:, e * 4 * CAP:(e + 1) * 4 * CAP], sgate[:, e * 4 * CAP:(e + 1) * 4 * CAP],
                       bank[2 + e][:, 4 * CAP:8 * CAP], ALU.mult).then_inc(sem_("hid_ready"), 1)

            def second_half(r, v):
                dve.wait_ge(sem_("down1_used"), v + 1)
                V.tensor_copy(oute[0:2 * CAP, r, 512:D], bank[5][0:2 * CAP, :]).then_inc(sem_("oute_ready"), 1)

            def moe_pass(b, own):
                with dve.Fori(0, NPAIR // 2) as i:
                    own.turns(i, 14, NPAIR // 2)
                    v = i * 2 + b * NPAIR
                    select(own, 0, i * 2, v)
                    select(own, 1, i * 2 + 1, v + 1)
                    hidden(v)
                    second_half(0, v)
                    add_spread(v)
                    hidden(v + 1)
                    second_half(1, v + 1)
                    add_spread(v + 1)
                own.end()

            moe_pass(0, own)
            n_max = dve.value_load(cnt_i[0:1, 0:1], min_val=0, max_val=T)
            more = Own(dve, sem_("dve_more_step"))
            for b in range(1, NPASS):
                with dve.If(n_max > b * CAP):
                    more.do(ts(rank[:], rank[:], float(CAP), None, ALU.subtract))
                    moe_pass(b, more)
            dve.drain()
            for k in range(KD):
                stt(resid[:, k, :], yacc[:, k, :], mod[:, 40 + k:41 + k], resid[:, k, :], ALU.mult,
                    ALU.add).then_inc(sem_("x_final"), 1)
            dve.wait_ge(sem_("x_final"), KD)
            norm("f", resid, hT, lambda k: par("final_g", k, 1), NORM_EPS, centre=False)
            for t in (2, 3):
                dve.wait_ge(sem_("outT_done"), t + 1)
                V.tensor_copy(sc1_t[:, t * 512:(t + 1) * 512], bank[t][:]).then_inc(sem_("out_ready"), 1)


IN = ["x", "w_in", "w_conv_out", "w_ssm_out", "w_o", "w_ffn_up", "w_ffn_down", "w_ada_2", "w_in_2", "w_proj_moba_2",
      "w_proj_diff_2", "w_out_2", "w_route", "w_gate_2", "w_up_2", "w_down_2"]


def kernel(**inputs):
    import numpy as np
    import concourse.bacc as bacc
    from concourse.bass_utils import run_bass_kernel_spmd

    a = {k: np.ascontiguousarray(v) for k, v in inputs.items()}
    f32 = np.float32

    def cols(v):
        return np.reshape(v, (-1, P)).T

    def taps(w):
        return np.reshape(w.T, (-1, P, w.shape[0])).transpose(1, 0, 2).reshape(P, -1)

    def every(v):
        return np.broadcast_to(np.reshape(v, (1, -1)), (P, np.size(v)))

    values = {
        "ln_in_g": cols(a["ln_in_g"]), "ln_in_b": cols(a["ln_in_b"]), "conv_w": taps(a["conv_dw_w"][0]),
        "conv_b": cols(a["conv_dw_b"]), "conv_ln_g": cols(a["conv_ln_g"]), "conv_ln_b": cols(a["conv_ln_b"]),
        "ssm_w": taps(a["ssm_conv_w"][0]), "ssm_b": cols(a["ssm_conv_b"]),
        "ssm_d": cols(np.repeat(a["ssm_d"][0], HD)), "ssm_norm": cols(a["ssm_norm_w"]),
        "ln1_g": cols(a["ln1_g"]), "ln1_b": cols(a["ln1_b"]), "ffn_w": taps(a["ffn_dw_w"][0]),
        "ffn_b": cols(a["ffn_dw_b"]), "ln2_g": cols(a["ln2_g"]), "ln2_b": cols(a["ln2_b"]), "b_ada": cols(a["b_ada_2"]),
        "c": cols(a["c_2"]), "norm1_g": cols(a["norm1_g_2"]), "norm2_g": cols(a["norm2_g_2"]),
        "final_g": cols(a["final_g_2"]), "subln_g": cols(a["diff_subln_g_2"]),
        "dt_bias": every(a["ssm_dt_bias"]), "a_log": every(a["ssm_a_log"]),
        "b_route": every(np.concatenate([a["b_group_2"][0], a["b_expert_2"][0]])),
        "lam_q1": every(a["lambda_q1_2"]), "lam_q2": every(a["lambda_q2_2"]),
        "lam_k1": every(a["lambda_k1_2"]), "lam_k2": every(a["lambda_k2_2"]),
    }
    params = np.ascontiguousarray(np.concatenate([values[n] for n, _ in PARAMS], axis=1))

    i = np.arange(P)
    swap = np.zeros((P, P), f32)
    for m in range(P):
        swap[m + 32 if m % 64 < 32 else m - 32, m] = -1.0 if m % 64 < 32 else 1.0
    q, k = np.arange(T), np.arange(T)
    att = np.where(k[None, :] <= q[:, None], f32(0), f32(NEG)).reshape(TT, P, T).transpose(1, 0, 2).reshape(P, TT * T)
    inv = (f32(1.0) / (f32(10000.0) ** (np.arange(0, 64, 2, dtype=f32) / f32(64)))).astype(f32)
    ang = np.arange(T, dtype=f32)[None, :] * inv[i % 32][:, None]
    tables = {
        "ident": np.eye(P, dtype=f32), "upper": (i[:, None] <= i[None, :]).astype(f32),
        "before": (i[:, None] < i[None, :]).astype(f32), "ones": np.ones((P, P), f32), "swap": swap,
        "ssm_mask": np.where(i[None, :] >= i[:, None], f32(0), f32(NEG)), "att_mask": att,
        "cos": np.cos(ang).astype(f32), "sin": np.sin(ang).astype(f32),
        "slot": np.broadcast_to(np.arange(CAP, dtype=f32), (P, CAP)),
        "place": np.broadcast_to(np.arange(EP, dtype=f32), (P, EP)),
    }
    consts = np.ascontiguousarray(np.concatenate([tables[n] for n, _ in CONSTS], axis=1).astype(f32))

    arrays = {"params": params, "consts": consts, "x": a["x"][0]}
    for n in IN[1:]:
        if n == "w_route":
            arrays[n] = np.concatenate([a["w_group_2"][0], a["w_expert_2"][0]], axis=1)
        else:
            arrays[n] = a[n][0]
    nc = bacc.Bacc("TRN2", target_bir_lowering=False, num_devices=1)
    ap = {n: nc.dram_tensor(f"in_{n}", v.shape, F32, kind="ExternalInput").ap() for n, v in arrays.items()}
    out = nc.dram_tensor("out", (T, D), F32, kind="ExternalOutput").ap()
    program(nc, ap["x"], ap["params"], ap["consts"], *[ap[n] for n in IN[1:]], out)
    r = run_bass_kernel_spmd(nc, [{f"in_{n}": np.ascontiguousarray(v) for n, v in arrays.items()}], core_ids=[0])
    return r.results[0]["out"].reshape(1, T, D)
```

```python
from contextlib import ExitStack

import concourse.bass as bass
from concourse import mybir

P = 128
F32 = mybir.dt.float32
I32 = mybir.dt.int32
ALU = mybir.AluOpType
ACT = mybir.ActivationFunctionType
AX_X = mybir.AxisListType.X
ds = bass.ds

T = 256
TT = T // P
D = 1024
KD = D // P
CK = 31
SSM = 2048
KS = SSM // P
H = 32
HD = SSM // H
G = 4
XBC = SSM + 2 * G * P
KX = XBC // P
FF = 2816
KF = FF // P
QK = 512
E_ = 32
EG = 4
EP = E_ // EG
DE = 512
CAP = 64
ALPHA = 2.0 ** 0.25
LN_EPS = 1e-5
RMS_EPS = 1e-5
NORM_EPS = 1e-6
LAM_INIT = 0.2
NEG = -1e30
NB = 4

C_GLU, C_Z, C_XBC, C_DT, C_GA = 0, 2048, 4096, 7168, 7200

PARAMS = [("ln_in_g", 8), ("ln_in_b", 8), ("conv_w", 8 * CK), ("conv_b", 8), ("conv_ln_g", 8), ("conv_ln_b", 8),
          ("ssm_w", KX * 4), ("ssm_b", KX), ("ssm_d", KS), ("ssm_norm", KS), ("ln1_g", 8), ("ln1_b", 8),
          ("ffn_w", 2 * KF * 3), ("ffn_b", 2 * KF), ("ln2_g", 8), ("ln2_b", 8), ("b_ada", 48), ("c", 8),
          ("norm1_g", 8), ("norm2_g", 8), ("final_g", 8), ("subln_g", 1),
          ("dt_bias", H), ("a_log", H), ("b_route", EG + E_), ("lam_q1", 64), ("lam_q2", 64), ("lam_k1", 64),
          ("lam_k2", 64)]
CONSTS = [("ident", P), ("upper", P), ("before", P), ("ones", P), ("swap", P), ("ssm_mask", P), ("att_mask", 2 * T),
          ("cos", T), ("sin", T), ("slot", CAP), ("place", EP)]


def offsets(table):
    at, out = 0, {}
    for name, n in table:
        out[name] = (at, n)
        at += n
    return out, at


PAR, NPAR = offsets(PARAMS)
CON, NCON = offsets(CONSTS)

ROUNDS = [("glu", 2), ("glu", 3), ("z", 0), ("z", 1), ("z", 2), ("z", 3), ("gate", 0), ("gate", 1)]


def tile_order():
    def some(name, a, b):
        return [(name, t) for t in range(a, b)]

    out = some("h", 0, 4) + some("xbc", 0, 12) + some("glu", 0, 4) + some("xtok", 0, 9)
    for r, (name, u) in enumerate(ROUNDS):
        out += some(name, 2 * u, 2 * u + 2) + [("ssd", r)]
    out += some("gate", 4, 8)
    for name, n in (("ssm_out", 4), ("conv_out", 4), ("mix", 4), ("up", 22), ("down", 4), ("qk", 8), ("swap", 4), ("v", 4),
                    ("swap", 8), ("gate2", 8), ("proj_m", 4), ("proj_d", 4), ("out2", 4)):
        out += some(name, 4 if (name, n) == ("swap", 8) else 0, n)
    return {x: i for i, x in enumerate(out)}


TILE = tile_order()
UNITS = [("xbc", 6), ("glu", 4), ("z", 4), ("gate", 4), ("ssm_out", 4), ("conv_out", 2), ("mix", 2),
         ("up", 11), ("down", 8), ("qk", 4), ("v", 2), ("gate2", 4), ("proj_m", 1), ("proj_d", 1), ("out2", 2)]
UNIT, NUNITS = offsets(UNITS)
HALVES = ("glu", "up")
SLOT = 4096


def tiles_of(name):
    return [n for (k, _), n in TILE.items() if k == name]


def U0(name):
    return UNIT[name][0]


def program(nc, x, params, consts, w_in, w_conv_out, w_ssm_out, w_o, w_up, w_down, w_ada, w_in2, w_pm, w_pd, w_out2,
            w_route, w_gate_e, w_up_e, w_down_e, out):
    with ExitStack() as ctx:
        def sb(name, n, dt=F32):
            return ctx.enter_context(nc.sbuf_tensor(name, [P, n], dt))

        def sem(name):
            return ctx.enter_context(nc.semaphore(name))

        def v3(ap, b):
            return ap.rearrange("p (a b) -> p a b", b=b)

        par_t, con_t = sb("par", NPAR), sb("con", NCON)

        def par(name, a=0, n=None):
            o, w = PAR[name]
            return par_t[:, o + a:o + a + (w - a if n is None else n)]

        def con(name):
            o, w = CON[name]
            return con_t[:, o:o + w]

        def par_at(name, j):
            return par_t[:, ds(j + PAR[name][0], 1)]

        ident, upper, before, ones, swap_m = (con(n) for n in ("ident", "upper", "before", "ones", "swap"))
        dense = [sb(f"dense{s}", SLOT) for s in range(2)]
        arena = sb("arena", 6 * SLOT)
        expert = [arena[:, s * SLOT:(s + 1) * SLOT] for s in range(6)]
        wdt = sb("wdt", KD * H)
        wroute = sb("wroute", KD * (EG + E_))
        hT_t, resid_t, sc1_t, sc2_t = sb("hT", KD * T), sb("resid", KD * T), sb("scratch1", KD * T), sb("scratch2", KD * T)
        hT, resid, scr1, scr2 = v3(hT_t[:], T), v3(resid_t[:], T), v3(sc1_t[:], T), v3(sc2_t[:], T)
        region = sb("region", KF * T)
        stat = sb("stat", 4 * T)
        small = sb("small", 448)

        at = [0]

        def carve(base, n):
            at[0] += n
            return base[:, at[0] - n:at[0]]

        x_tok = carve(arena, TT * D)
        conv_t = x_tok
        glu_v = carve(arena, KD * (T + CK - 1))
        xbc_t = carve(arena, KX * T)
        z_t = carve(arena, KS * T)
        ga_t = carve(arena, KS * T)
        yz_t = carve(arena, KS * T)
        assert at[0] <= 6 * SLOT
        x_tok, conv_o, glu_v, xbcT, zs, gates, yz = (v3(x_tok, D), v3(conv_t, T), v3(glu_v, T + CK - 1), v3(xbc_t, T),
                                                     v3(z_t, T), v3(ga_t, T), v3(yz_t, T))
        at[0] = 0
        xdt = v3(carve(region, TT * SSM), SSM)
        btok = carve(region, G * P)
        xds = v3(carve(region, 2 * 8 * HD), 8 * HD)
        abc = v3(sc1_t[:, 0:1024], 512)
        ein = v3(sc1_t[:, 1024:2048], 512)
        cexp = v3(sc2_t[:, 0:1024], 512)
        state = v3(sc2_t[:, 1024:2048], 512)
        ssm_sq = v3(region[:, 0:KS * T], T)
        ada_acc = v3(sc2_t[:, 1024:2048], 512)
        half_t = v3(sc1_t[:, 0:1024], 512)
        sig_t = v3(sc2_t[:, 0:512], T)
        act_t = v3(region[:], T)
        at[0] = 0
        qk = v3(carve(region, 4 * 4 * T), T)
        vm = v3(carve(region, TT * QK), QK)
        at[0] = 4 * SLOT
        vd = v3(carve(arena, TT * QK), QK)
        om = v3(carve(arena, 4 * T), T)
        od = v3(carve(arena, 4 * T), T)
        gates2_t = carve(arena, KS * T)
        gates2 = v3(gates2_t, T)
        osq = v3(sc2_t[:, 1024:2048], T)
        raw = [sc1_t[:, i * 512:(i + 1) * 512] if i < 4 else sc2_t[:, (i - 4) * 512:(i - 3) * 512] for i in range(8)]
        srow = v3(sc1_t[:, 0:1024], 512)
        prob = v3(sc1_t[:, 1024:2048], 512)
        prT = v3(sc2_t[:, 0:768], 384)
        rtmp = stat[:, 0:512]
        at[0] = 0
        BF16 = mybir.dt.bfloat16
        hpart = [v3(carve(region, TT * D // 2).bitcast(BF16), D) for _ in range(3)]
        oute = v3(carve(region, 2 * D), D)
        selT = v3(carve(region, 2 * T), T)
        hrest = v3(sc2_t[:], D)
        xe = v3(sc2_t[:], KD * 2 * CAP)
        yacc = scr1
        dcarve = dense[0][:]
        at[0] = 0
        wsel = v3(carve(dcarve, 4 * TT * CAP), 2 * TT * CAP)
        sel = v3(carve(dcarve, 2 * TT * CAP).bitcast(BF16), 2 * TT * CAP)
        sgate, hid, hidT = (carve(dcarve, DE) for _ in range(3))

        at[0] = 0
        dtr, dtx, dte, dta, dts, eal = (carve(small, n) for n in (64, 64, 64, 64, 64, 32))
        mod = carve(small, 48)
        cact = carve(small, 8)
        lam = carve(small, 4)
        dstate = carve(small, 32)
        assert at[0] <= 448
        gs1, gs2, g1h = sb("gs1", 8), sb("gs2", 8), sb("g1h", 8)
        acs = sb("acs", 64)
        lamp = sb("lamp", 128)
        mx, ssum, rsum = sb("mx", 4), sb("ssum", 4), sb("rsum", 4)
        lg = sb("lg", TT * (EG + E_))
        rt = sb("rt", 640)
        wexp, rank = sb("wexp", TT * E_), sb("rank", TT * E_)

        at[0] = 0

        def rcarve(n, w=None):
            r = carve(rt, n)
            return r if w is None else v3(r, w)

        mask_t = rcarve(TT * E_)
        mask = v3(mask_t, E_)
        r_ghot, r_exp, r_prod = rcarve(TT * EG, EG), rcarve(TT * EG), rcarve(TT * E_)
        r_el, r_el2, r_hot1, r_hot2, r_wx = (rcarve(TT * EP, EP) for _ in range(5))
        r_top, r_tmp, r_m1, r_m2, r_e2, r_gs, r_w1, r_w2 = (rcarve(TT) for _ in range(8))
        cnt_f, cnt_i = sb("cnt_f", 1), sb("cnt_i", 1, I32)

        bank = [ctx.enter_context(nc.psum_tensor(f"bank{b}", [P, 512], F32)) for b in range(8)]

        sems = {}

        def sem_(name):
            if name not in sems:
                sems[name] = sem(name)
            return sems[name]

        params_in, consts_in, x_in = sem("params_in"), sem("consts_in"), sem("x_in")
        dense_in = [sem(f"dense_in{s}") for s in range(2)]
        expert_in = [sem(f"expert_in{s}") for s in range(6)]
        tile_done = sem("tile_done")
        tile_read = [sem(f"tile_read{b}") for b in range(NB)]
        act_step, dve_step = sem("act_step"), sem("dve_step")
        out_written = sem("out_written")

        class Own:

            def __init__(self, eng, sm):
                self.eng, self.sm, self.n = eng, sm, 0

            def do(self, ins):
                ins.then_inc(self.sm, 1)
                self.n = self.n + 1
                self.eng.wait_ge(self.sm, self.n)

            def turns(self, i, per, count):
                self.before, self.per, self.count = self.n, per, count
                self.n = self.n + i * per

            def end(self):
                self.n = self.before + self.per * self.count

        def wait_read(eng, n, turn=0):
            eng.wait_ge(tile_read[n % NB], n // NB + 2 + turn)

        def wait_all_read(eng, name):
            for n in {n % NB: n for n in tiles_of(name)}.values():
                wait_read(eng, n)

        def wait_tile(eng, name, t, turn=0):
            eng.wait_ge(tile_done, TILE[name, t] + 1 + NB * turn)
            return bank[TILE[name, t] % NB]

        def read_sem(name, t):
            return tile_read[TILE[name, t] % NB]

        def arrived(n):
            names = [k for m in range(n % 2, n + 1, 2) for k, (u, c) in UNIT.items() if u <= m < u + c]
            return sum(32 if k in HALVES else 16 for k in names)

        def rows(w):
            return w.rearrange("(k p) n -> p k n", p=P)

        wi, wco, wso, wo_, wdn = rows(w_in), rows(w_conv_out), rows(w_ssm_out), rows(w_o), rows(w_down)
        wada, wi2, wpm, wpd, wo2 = rows(w_ada), rows(w_in2), rows(w_pm), rows(w_pd), rows(w_out2)
        wge = w_gate_e.rearrange("e (k p) n -> p e k n", p=P)
        wue = w_up_e.rearrange("e (k p) n -> p e k n", p=P)
        wde = w_down_e.rearrange("e (k p) n -> p e k n", p=P)
        wup2 = w_up.rearrange("(k p) (h n) -> p k h n", p=P, h=2)
        wglu2 = w_in[:, 0:2 * D].rearrange("(k p) (h n) -> p k h n", p=P, h=2)

        NPAIR = E_ // 2
        NPASS = T // CAP

        block = ctx.enter_context(nc.Block())

        @block.sync
        def _(sp):
            sp.dma_start(x_tok, x.rearrange("(c p) n -> p c n", p=P)).then_inc(x_in, 16)

            def last_use(n):
                name = [k for k, (u, c) in UNIT.items() if u <= n < u + c][0]
                u, units, tiles = n - U0(name), UNIT[name][1], len(tiles_of(name))
                if name == "down":
                    return (tile_done, TILE[name, u // 2] + 1) if u % 2 else (sem_("down_unit"), u // 2 + 1)
                return tile_done, TILE[name, (u + 1) * tiles // units - 1] + 1

            def load(name, u, shape, src, turn=0):
                n = U0(name) + u
                if n >= 2:
                    sm, v = last_use(n - 2)
                    if u >= 2:
                        v = v + turn * (last_use(n)[1] - v)
                    sp.wait_ge(sm, v)
                if name in HALVES:
                    for h in range(2):
                        sp.dma_start(shape(dense[n % 2])[:, :, h, :], src[:, :, h, :]).then_inc(dense_in[n % 2], 16)
                else:
                    sp.dma_start(shape(dense[n % 2]), src).then_inc(dense_in[n % 2], 16)

            def stage(name, units, shape, cols):
                for u in range(2):
                    load(name, u, shape, cols(u))
                if units >= 4:
                    with sp.Fori(0, units // 2 - 1) as i:
                        for u in range(2, 4):
                            load(name, u, shape, cols(i * 2 + u), i)

            def flat(t):
                return v3(t[:], 512)

            def halves(t):
                return t[:].rearrange("p (k h n) -> p k h n", k=KD, h=2)

            stage("xbc", 6, flat, lambda u: wi[:, :, ds(u * 512 + C_XBC, 512)])
            stage("glu", 4, halves, lambda u: wglu2[:, :, :, ds(u * 256, 256)])
            stage("z", 4, flat, lambda u: wi[:, :, ds(u * 512 + C_Z, 512)])
            stage("gate", 4, flat, lambda u: wi[:, :, ds(u * 512 + C_GA, 512)])
            stage("ssm_out", 4, lambda t: v3(t[:], 256), lambda u: wso[:, :, ds(u * 256, 256)])
            stage("conv_out", 2, flat, lambda u: wco[:, :, ds(u * 512, 512)])
            stage("mix", 2, flat, lambda u: wo_[:, :, ds(u * 512, 512)])

            def load_ada(i, turn=0):
                if i >= 2:
                    sp.wait_ge(sem_("ada_summed"), turn * 2 + (i - 1))
                sp.dma_start(v3(expert[4 + i % 2], 512), wada[:, :, ds(turn * 1024 + i * 512, 512)]
                             ).then_inc(sem_(f"ada_in{i % 2}"), 16)

            def up(u, i=0):
                load("up", u, halves, wup2[:, :, :, ds(i * 512 + u * 256, 256)], i)

            up(0)
            up(1)
            wait_all_read(sp, "mix")
            load_ada(0)
            load_ada(1)
            with sp.Fori(0, 4) as i:
                for u in (2, 3):
                    up(u, i)
                    load_ada(u, i)
            up(10)
            for u in range(8):
                load("down", u, lambda t: v3(t[:, 0:KF * P], P), wdn[:, :, u * P:(u + 1) * P])
                if u < 2:
                    load_ada(10 + u)

            def load_expert(s, e, pair):
                w, k = [(wge, KD), (wge, KD), (wue, KD), (wue, KD), (wde, 4), (wde, 4)][s]
                src = w[:, ds(pair * 2 + e, 1), :, :].rearrange("p e k n -> p (e k) n")
                sp.dma_start(v3(expert[s], SLOT // k), src).then_inc(expert_in[s], 16)

            OF = [0, 1, 0, 1, 0, 1]

            for s in range(4):
                load_expert(s, OF[s], 0)
            for u, c in enumerate((0, 512, 1536, 2048)):
                load("qk", u, flat, wi2[:, :, c:c + 512])
            for u, c in enumerate((1024, 2560)):
                load("v", u, flat, wi2[:, :, c:c + 512])
            stage("gate2", 4, flat, lambda u: wi2[:, :, ds(u * 512 + 3072, 512)])
            load("proj_m", 0, lambda t: v3(t[:], D), wpm)
            load("proj_d", 0, lambda t: v3(t[:], D), wpd)
            stage("out2", 2, flat, lambda u: wo2[:, :, ds(u * 512, 512)])
            wait_all_read(sp, "out2")
            for s in (4, 5):
                load_expert(s, OF[s], 0)

            def refill(pair, v):
                for s in range(6):
                    sp.wait_ge(sem_(("gate_used", "up_used", "down_used")[s // 2]), v)
                    load_expert(s, OF[s], pair)

            with sp.Fori(1, NPAIR) as i:
                refill(i, i)
            sp.wait_ge(sem_("counted"), 1)
            n_max = sp.value_load(cnt_i[0:1, 0:1], min_val=0, max_val=T)
            for b in range(1, NPASS):
                with sp.If(n_max > b * CAP):
                    with sp.Fori(0, NPAIR) as i:
                        refill(i, i + b * NPAIR)
            sp.wait_ge(sem_("out_ready"), 4)
            sp.dma_start(out.rearrange("(c p) n -> p c n", p=P), v3(sc1_t[:], D)).then_inc(out_written, 16)
            sp.wait_ge(out_written, 16)

        @block.gpsimd
        def _(pool):
            nc.gpsimd.memset(glu_v[:, :, 0:CK - 1], 0.0).then_inc(sem_("padded"), 1)
            n = 0
            pool.wait_ge(sem_("decay_ready"), 1)
            for g in range(G):
                wait_read(pool, TILE["xtok", g])
                if g >= 2:
                    pool.wait_ge(sem_("state_done"), g - 1)
                nc.gpsimd.tensor_tensor(
                    xds[:, g % 2, :].rearrange("p (h d) -> p h d", h=8),
                    xdt[:, 0, g * 512:(g + 1) * 512].rearrange("p (h d) -> p h d", h=8),
                    dstate[:, g * 8:(g + 1) * 8].unsqueeze(2).to_broadcast([P, 8, HD]), ALU.mult
                ).then_inc(sem_("xds_ready"), 1)
                for hf in range(2):
                    for c in range(TT):
                        if n >= 2:
                            pool.wait_ge(sem_("seg_done"), n - 1)
                        h0 = c * H + g * 8 + hf * 4
                        nc.gpsimd.tensor_copy(abc[:, n % 2, :].rearrange("p (h t) -> p h t", h=4),
                                              dta[:, h0:h0 + 4].unsqueeze(2).to_broadcast([P, 4, P])
                                              ).then_inc(sem_("abc_ready"), 1)
                        n += 1
            for t in range(8):
                wait_read(pool, TILE["ssd", t])
                wait_read(pool, TILE["z", t])
                nc.gpsimd.tensor_tensor(yz[:, 2 * t:2 * t + 2, :], yz[:, 2 * t:2 * t + 2, :], zs[:, 2 * t:2 * t + 2, :],
                                        ALU.mult).then_inc(sem_("yz_ready"), 1)

            def ffn_product(t, turn=0):
                pool.wait_ge(sem_("silu_gate"), t + 1 + 4 * turn)
                nc.gpsimd.tensor_tensor(act_t[:, ds(turn * 4 + t, 1), :], sig_t[:, t % 2:t % 2 + 1, :],
                                        half_t[:, t % 2, T:2 * T].unsqueeze(1), ALU.mult
                                        ).then_inc(sem_("act_ready"), 1)

            with pool.Fori(0, 5) as i:
                for t in range(4):
                    ffn_product(t, i)
            for t in (20, 21):
                ffn_product(t)
            for c in range(TT):
                pool.wait_ge(sem_("part_ready"), c + 1)
                nc.gpsimd.tensor_tensor(hrest[:, c, :], hrest[:, c, :], hpart[0][:, c, :],
                                        ALU.subtract).then_inc(sem_("rest_ready"), 1)
            for c in range(TT):
                pool.wait_ge(sem_("part_ready"), TT + c + 1)
                nc.gpsimd.tensor_tensor(hpart[2][:, c, :], hrest[:, c, :], hpart[1][:, c, :],
                                        ALU.subtract).then_inc(sem_("rest_ready"), 1)

        @block.tensor
        def _(pe):
            mm, tr = nc.tensor.matmul, nc.tensor.transpose

            def open_tile(name, t, turn=0):
                n = TILE[name, t]
                pe.wait_ge(tile_read[n % NB], n // NB + 1 + turn)
                return bank[n % NB]

            def have(name, u, turn=0):
                n = U0(name) + u
                pe.wait_ge(dense_in[n % 2], arrived(n) + turn * (32 if name in HALVES else 16))
                return dense[n % 2]

            def tile(name, t, turn, k_n, chunk, src):
                b = v3(open_tile(name, t, turn)[:], T)
                for m in range(2):
                    for k in range(k_n):
                        last = mm(b[:, m, :], chunk(k, m), src[:, k, :], start=k == 0, stop=k == k_n - 1)
                last.then_inc(tile_done, 1)

            def unit_512(name, u, src, turn=0):
                w = v3(have(name, u, turn)[:], 512)
                for j in range(2):
                    tile(name, 2 * u + j, turn, KD, lambda k, m: w[:, k, (2 * j + m) * P:(2 * j + m + 1) * P], src)

            def unit_halves(name, u, src, turn=0):
                w = have(name, u, turn)[:].rearrange("p (k h n) -> p k h n", k=KD, h=2)
                for j in range(2):
                    tile(name, 2 * u + j, turn, KD, lambda k, m: w[:, k, m, j * P:(j + 1) * P], src)

            def stage(name, units, unit, src):
                with pe.Fori(0, units // 2) as i:
                    for u in range(2):
                        unit(name, u, src, i)

            def norm(p, src, ready, centre=True, filler=lambda: None):
                if centre:
                    for k in range(KD):
                        if k % 2 == 0:
                            ready(k // 2)
                        last = mm(bank[7][:, 0:T], ones, src[:, k, :], start=k == 0, stop=k == KD - 1)
                    last.then_inc(sem_(p + "_sum"), 1)
                filler()
                for k in range(KD):
                    if k % 2 == 0:
                        pe.wait_ge(sem_(p + "_sq"), k // 2 + 1)
                    last = mm(bank[7][:, 0:T], ones, scr2[:, k, :], start=k == 0, stop=k == KD - 1)
                last.then_inc(sem_(p + "_ssq"), 1)

            def after_tile(name):
                return lambda q: wait_read(pe, TILE[name, q])

            pe.wait_ge(consts_in, 16)
            pe.wait_ge(sem_("xn_ready"), 1)
            for t in range(4):
                b = v3(open_tile("h", t)[:], T)
                for m in range(2):
                    for c in range(TT):
                        j = 2 * t + m
                        last = tr(b[:, m, c * P:(c + 1) * P], x_tok[:, c, j * P:(j + 1) * P], ident)
                last.then_inc(tile_done, 1)
            wait_all_read(pe, "h")
            pe.wait_ge(params_in, 48)
            wd = v3(wdt[:], H)
            for c in range(TT):
                for k in range(KD):
                    last = mm(bank[6][:, c * H:(c + 1) * H], hT[:, k, c * P:(c + 1) * P], wd[:, k, :],
                              start=k == 0, stop=k == KD - 1)
            last.then_inc(sem_("dt_done"), 1)
            stage("xbc", 6, unit_512, hT)
            pe.wait_ge(sem_("a_ready"), 1)
            for c in range(TT):
                mm(bank[6][:, c * H:(c + 1) * H], upper, dta[:, c * H:(c + 1) * H], start=True, stop=True)
            mm(bank[6][:, 2 * H:3 * H], ones, dta[:, 0:H], start=True, stop=True).then_inc(sem_("acs_done"), 1)
            for u in range(2):
                unit_halves("glu", u, hT)
            pe.wait_ge(sem_("xbc_ready"), 12)
            for t in range(9):
                b = open_tile("xtok", t)
                for j in range(4):
                    if t < 8:
                        src = xbcT[:, (t % 4) * 4 + j, (t // 4) * P:(t // 4 + 1) * P]
                    else:
                        src = xbcT[:, KS + j, 0:P]
                    last = tr(b[:, j * P:(j + 1) * P], src, ident)
                last.then_inc(tile_done, 1)
            def seg(n):
                pe.wait_ge(sem_("abc_ready"), n + 1)
                if n >= 2:
                    pe.wait_ge(sem_("seg_masked"), n - 1)
                for j in range(4):
                    last = mm(bank[4 + n % 2][:, j * P:(j + 1) * P], abc[:, n % 2, j * P:(j + 1) * P], upper,
                              start=True, stop=True)
                last.then_inc(sem_("seg_done"), 1)

            order = [(g, hf, c) for g in range(G) for hf in range(2) for c in range(TT)]
            for rnd, (name, u) in enumerate(ROUNDS):
                g, hf = rnd // 2, rnd % 2
                if hf == 0:
                    if g:
                        pe.wait_ge(sem_("mt_ready"), 2 * rnd)
                    for cc in range(TT):
                        last = mm(bank[6][:, cc * P:(cc + 1) * P], xbcT[:, KS + g, cc * P:(cc + 1) * P],
                                  xbcT[:, KS + G + g, cc * P:(cc + 1) * P], start=True, stop=True)
                    last.then_inc(sem_("cb_done"), 1)
                    if g == 0:
                        wait_all_read(pe, "xtok")
                    pe.wait_ge(sem_("xds_ready"), g + 1)
                    if g:
                        pe.wait_ge(sem_("state_ready"), g)
                    mm(bank[7][:, 0:512], btok[:, g * P:(g + 1) * P], xds[:, g % 2, :], start=True,
                       stop=True).then_inc(sem_("state_done"), 1)
                seg(2 * rnd)
                seg(2 * rnd + 1)
                (unit_halves if name == "glu" else unit_512)(name, u, hT)
                b = v3(open_tile("ssd", rnd)[:], T)
                for c in range(TT):
                    n = 2 * rnd + c
                    pe.wait_ge(sem_("mt_ready"), n + 1)
                    if c == 1:
                        pe.wait_ge(sem_("ce_ready"), rnd + 1)
                        pe.wait_ge(sem_("state_ready"), g + 1)
                    for j in range(4):
                        h, o = g * 8 + hf * 4 + j, (j % 2) * HD
                        dst = b[o:o + HD, j // 2, c * P:(c + 1) * P]
                        last = mm(dst, xdt[:, c, h * HD:(h + 1) * HD], ein[:, n % 2, j * P:(j + 1) * P],
                                  start=True, stop=c == 0)
                        if c == 1:
                            last = mm(dst, state[:, g % 2, (hf * 4 + j) * HD:(hf * 4 + j + 1) * HD],
                                      cexp[:, hf, j * P:(j + 1) * P], start=False, stop=True)
                    last.then_inc(tile_done if c else sem_("y_half"), 1)
            for u in (2, 3):
                unit_512("gate", u, hT)
            for g in range(G):
                pe.wait_ge(sem_("ysq_ready"), g + 1)
                for k in range(4):
                    last = mm(bank[4 + g // 2][:, (g % 2) * T:(g % 2 + 1) * T], ones, ssm_sq[:, 4 * g + k, :],
                              start=k == 0, stop=k == 3)
            last.then_inc(sem_("yssq_done"), 1)

            def ssm_out(u):
                w = v3(have("ssm_out", u)[:], 256)
                tile("ssm_out", u, 0, KS, lambda k, m: w[:, k, m * P:(m + 1) * P], yz)

            pe.wait_ge(sem_("yn_ready"), KS)
            ssm_out(0)
            ssm_out(1)
            norm("cn", conv_o, lambda q: pe.wait_ge(sem_("tap"), CK * KD), filler=lambda: ssm_out(2))
            ssm_out(3)
            pe.wait_ge(sem_("cn_out"), KD)
            stage("conv_out", 2, unit_512, conv_o)
            pe.wait_ge(sem_("merged"), 4)
            stage("mix", 2, unit_512, gates)
            norm("n1", resid, after_tile("mix"))
            pe.wait_ge(sem_("n1_out"), KD)

            def ada_columns(i, turn=0):
                pe.wait_ge(sem_("ada_summed"), turn * 2 + (i + 1))
                for m in range(4):
                    last = mm(bank[6][:, ds(turn * 8 + (4 * i + m), 1)], ada_acc[:, i % 2, m * P:(m + 1) * P],
                              ones[:, 0:1], start=True, stop=True)
                last.then_inc(sem_("ada_done"), 1)

            with pe.Fori(0, 5) as i:
                for u in range(2):
                    unit_halves("up", u, hT, i)
                    ada_columns(u, i)
            unit_halves("up", 10, hT)
            pe.wait_ge(sem_("act_ready"), KF)
            for t in range(4):
                b = v3(open_tile("down", t)[:], T)
                for m in range(2):
                    w = v3(have("down", 2 * t + m)[:, 0:KF * P], P)
                    for k in range(KF):
                        last = mm(b[:, m, :], w[:, k, :], act_t[:, k, :], start=k == 0, stop=k == KF - 1)
                    last.then_inc(tile_done if m else sem_("down_unit"), 1)
                if t < 2:
                    ada_columns(10 + t)
            norm("n2", resid, after_tile("down"))
            norm("r1", resid, None, centre=False)
            pe.wait_ge(sem_("r1_out"), KD)
            for u in range(4):
                unit_512("qk", u, hT)

            def swap(t):
                b = open_tile("swap", t)
                wait_read(pe, TILE["qk", t])
                mm(b[:], swap_m, raw[t], start=True, stop=True).then_inc(tile_done, 1)

            for t in range(4):
                swap(t)
            for u in range(2):
                w = v3(have("v", u)[:], 512)
                for c in range(TT):
                    b = open_tile("v", 2 * u + c)
                    for k in range(KD):
                        last = mm(b[:], hT[:, k, c * P:(c + 1) * P], w[:, k, :], start=k == 0, stop=k == KD - 1)
                    last.then_inc(tile_done, 1)
            for t in range(4, 8):
                swap(t)
            pe.wait_ge(sem_("rope_ready"), 4)

            def scores(a):
                if a >= 2:
                    pe.wait_ge(sem_("masked"), a - 1)
                if a == 8:
                    pe.wait_ge(sem_("rope_ready"), 8)
                o, j = (a % 2) * 64, (a // 2) % 4 + (8 if a >= 8 else 0)
                b = v3(bank[4 + a % 2][:], T)
                for c in range(TT):
                    last = mm(b[:, c, :], qk[o:o + 64, j, c * P:(c + 1) * P], qk[o:o + 64, j + 4, :],
                              start=True, stop=True)
                last.then_inc(sem_("scored"), 1)

            def attend(a):
                if a >= 8 and a % 2 == 0:
                    return
                n = a if a < 8 else 8 + (a - 8) // 2
                pe.wait_ge(sem_("prob_ready"), n + 1)
                if n:
                    pe.wait_ge(sem_("prT_ready"), n)
                for q, (c, kc) in enumerate(((0, 0), (1, 0), (1, 1))):
                    last = tr(bank[6][:, q * P:(q + 1) * P], prob[:, a % 2, c * T + kc * P:c * T + (kc + 1) * P], ident)
                last.then_inc(sem_("prT_done"), 1)
                pe.wait_ge(sem_("prT_ready"), n + 1)
                p = prT[:, n % 2, :]
                o, w, vv, hh = ((a % 2) * 64, 64, vm, a) if a < 8 else (0, P, vd, n - 8)
                if a == 0:
                    wait_all_read(pe, "v")
                elif a < 8 and a % 2 == 0:
                    pe.wait_ge(sem_("o_read"), a // 2)
                elif a >= 8:
                    pe.wait_ge(sem_("o_read"), n - 4)
                mm(bank[7][o:o + w, 0:T], vv[:, 0, hh * w:(hh + 1) * w], p[:, 0:T], start=True, stop=False)
                mm(bank[7][o:o + w, P:T], vv[:, 1, hh * w:(hh + 1) * w], p[:, T:T + P], start=False,
                   stop=True).then_inc(sem_("o_done"), 1)

            scores(0)
            for a in range(16):
                if a + 1 < 16:
                    scores(a + 1)
                w = v3(have("gate2", a // 4)[:], 512)
                m = a % 2
                b = v3((bank[TILE["gate2", a // 2] % NB] if m else open_tile("gate2", a // 2))[:], T)
                for k in range(KD):
                    last = mm(b[:, m, :], w[:, k, (a % 4) * P:(a % 4 + 1) * P], hT[:, k, :], start=k == 0, stop=k == KD - 1)
                if m:
                    last.then_inc(tile_done, 1)
                attend(a)
            pe.wait_ge(sem_("osq_ready"), 1)
            for h in range(4):
                last = mm(bank[4 + h // 2][:, (h % 2) * T:(h % 2 + 1) * T], ones, osq[:, h, :], start=True, stop=True)
            last.then_inc(sem_("ossq_done"), 1)
            for name, src, ready, n in (("proj_m", om, "o_read", 8), ("proj_d", od, "on_ready", 4)):
                pe.wait_ge(sem_(ready), n)
                w = v3(have(name, 0)[:], D)
                for t in range(4):
                    tile(name, t, 0, 4, lambda k, m: w[:, k, (2 * t + m) * P:(2 * t + m + 1) * P], src)
            pe.wait_ge(sem_("merged2"), 4)
            stage("out2", 2, unit_512, gates2)
            norm("r2", resid, None, centre=False)
            pe.wait_ge(sem_("r2_out"), KD)
            wr = v3(wroute[:], EG + E_)
            for c in range(TT):
                for k in range(KD):
                    last = mm(bank[6][:, c * 36:(c + 1) * 36], hT[:, k, c * P:(c + 1) * P], wr[:, k, :],
                              start=k == 0, stop=k == KD - 1)
            last.then_inc(sem_("logit_done"), 1)
            for t in range(4):
                c, half = t // 2, t % 2
                for j in range(4):
                    last = tr(bank[t][:, j * P:(j + 1) * P], hT[:, half * 4 + j, c * P:(c + 1) * P], ident)
                last.then_inc(sem_("htok_done"), 1)
            pe.wait_ge(sem_("mask_ready"), 1)
            mm(bank[7][:, 0:E_], before, mask[:, 0, :], start=True, stop=True)
            mm(bank[7][:, E_:2 * E_], before, mask[:, 1, :], start=True, stop=False)
            mm(bank[7][:, E_:2 * E_], ones, mask[:, 0, :], start=False, stop=True)
            mm(bank[7][:, 2 * E_:3 * E_], ones, mask[:, 0, :], start=True, stop=False)
            mm(bank[7][:, 2 * E_:3 * E_], ones, mask[:, 1, :], start=False, stop=True).then_inc(sem_("rank_done"), 1)
            pe.wait_ge(sem_("rest_ready"), 2 * TT)
            pe.wait_ge(sem_("zeroed"), 1)

            def gather(r, v):
                pe.wait_ge(sem_("sel_ready"), v + 1)
                for m in range(KD):
                    for c in range(TT):
                        for n in range(3):
                            last = mm(bank[m // 4][:, (m % 4) * 2 * CAP:(m % 4 + 1) * 2 * CAP],
                                      hpart[n][:, c, m * P:(m + 1) * P], sel[:, r, c * 2 * CAP:(c + 1) * 2 * CAP],
                                      start=(c, n) == (0, 0), stop=(c, n) == (TT - 1, 2))
                last.then_inc(sem_("gathered"), 1)

            def turn_selection(r, v):
                pe.wait_ge(sem_("sel_ready"), v + 1)
                pe.wait_ge(sem_("y_added"), v * 4 + 4)
                for c in range(TT):
                    last = tr(bank[6][:, c * P:(c + 1) * P], wsel[:, r, c * 2 * CAP:(c + 1) * 2 * CAP], ident)
                last.then_inc(sem_("selT_done"), 1)

            def both(dst, tokens, w, k_n, done):
                for k in range(k_n):
                    for e in range(2):
                        last = mm(dst[e * CAP:(e + 1) * CAP, :], tokens(k, e), w[e][:, k, :], start=k == 0,
                                  stop=k == k_n - 1)
                if done is not None:
                    last.then_inc(sem_(done), 1)

            def gate_up(r, v):
                pe.wait_ge(sem_("xe_ready"), v * 2 + 2)
                for half, done in enumerate(("gate_used", "up_used")):
                    for e in range(2):
                        pe.wait_ge(expert_in[2 * half + e], v * 16 + 16)
                    both(bank[2 + half], lambda k, e: xe[:, r, (k * 2 + e) * CAP:(k * 2 + e + 1) * CAP],
                         [v3(expert[2 * half + e], DE) for e in range(2)], KD, done)

            def turn_hidden(v):
                pe.wait_ge(sem_("hid_ready"), v + 1)
                for k in range(4):
                    last = tr(bank[2][:, k * P:(k + 1) * P], hid[:, k * P:(k + 1) * P], ident)
                last.then_inc(sem_("hidT_done"), 1)

            def down(v):
                pe.wait_ge(sem_("hidT_ready"), v + 1)
                pe.wait_ge(sem_("oute_ready"), v * 2 + 2)
                for e in range(2):
                    pe.wait_ge(expert_in[4 + e], v * 16 + 16)
                for half in range(2):
                    both(bank[4 + half], lambda k, e: hidT[:, k * P + e * CAP:k * P + (e + 1) * CAP],
                         [v3(expert[4 + e], D)[:, :, half * 512:(half + 1) * 512] for e in range(2)], 4,
                         "down_used" if half else None)

            def spread(r, v):
                pe.wait_ge(sem_("oute_ready"), v * 2 + 4)
                pe.wait_ge(sem_("selT_ready"), v + 1)
                for q in range(4):
                    pe.wait_ge(sem_("y_added"), v * 4 + max(q - 1, 0) + 4)
                    b = v3(bank[6 + q % 2][:], T)
                    for m in range(2):
                        j = 2 * q + m
                        last = mm(b[:, m, :], oute[:, r, j * P:(j + 1) * P], selT[:, r, :],
                                  start=True, stop=True)
                    last.then_inc(sem_("spread_done"), 1)

            def two_pairs(v, more):
                gate_up(0, v)
                turn_selection(0, v)
                turn_hidden(v)
                gather(1, v + 1)
                down(v)
                gate_up(1, v + 1)
                spread(0, v)
                turn_hidden(v + 1)
                turn_selection(1, v + 1)
                down(v + 1)
                if more:
                    gather(0, v + 2)
                spread(1, v + 1)

            def moe_pass(b):
                gather(0, b * NPAIR)
                with pe.Fori(0, NPAIR // 2 - 1) as i:
                    two_pairs(i * 2 + b * NPAIR, True)
                two_pairs(NPAIR - 2 + b * NPAIR, False)

            moe_pass(0)
            pe.wait_ge(sem_("counted"), 1)
            n_max = pe.value_load(cnt_i[0:1, 0:1], min_val=0, max_val=T)
            for b in range(1, NPASS):
                with pe.If(n_max > b * CAP):
                    moe_pass(b)
            norm("f", resid, None, centre=False)
            pe.wait_ge(sem_("f_scaled"), KD)
            for t in range(4):
                c, half = t // 2, t % 2
                for j in range(4):
                    last = tr(bank[t][:, j * P:(j + 1) * P], hT[:, half * 4 + j, c * P:(c + 1) * P], ident)
                last.then_inc(sem_("outT_done"), 1)

        @block.scalar
        def _(act):
            f = nc.scalar.activation
            own = Own(act, act_step)
            act.dma_start(con_t[:], consts).then_inc(consts_in, 16)
            for dst, src in ((par_t[:], params), (v3(wdt[:], H), rows(w_in)[:, :, C_DT:C_DT + H]),
                             (v3(wroute[:], EG + E_), rows(w_route))):
                act.dma_start(dst, src).then_inc(params_in, 16)

            def norm(p, src, ready, b=None, func=ACT.Identity, dst=None):
                for q in range(4):
                    ready(q)
                    f(scr2[:, 2 * q:2 * q + 2, :], src[:, 2 * q:2 * q + 2, :], ACT.Square).then_inc(sem_(p + "_sq"), 1)
                act.wait_ge(sem_(p + "_var"), 1)
                f(stat[:, T:2 * T], stat[:, 0:T], ACT.Sqrt).then_inc(sem_(p + "_std"), 1)
                if b is not None:
                    for k in range(KD):
                        act.wait_ge(sem_(p + "_scaled"), k + 1)
                        f(dst[:, k, :], dst[:, k, :], func, bias=b(k)).then_inc(sem_(p + "_out"), 1)

            def by(name, step=1):
                return lambda q: act.wait_ge(sem_(name), step * (q + 1))

            act.wait_ge(sem_("x_centred"), 1)
            for c in range(TT):
                f(sc2_t[:, c * D:(c + 1) * D], x_tok[:, c, :], ACT.Square,
                  accum_out=ssum[:, c:c + 1]).then_inc(sem_("x_sq"), 1)
            act.wait_ge(sem_("x_var"), 1)
            f(ssum[:, 0:2], ssum[:, 0:2], ACT.Sqrt).then_inc(sem_("x_std"), 1)
            act.wait_ge(params_in, 48)
            f(cact[:], par("c"), ACT.Silu).then_inc(sem_("c_ready"), 1)
            for t in range(4):
                b = wait_tile(act, "h", t)
                for m in range(2):
                    j = 2 * t + m
                    ins = f(hT[:, j, :], b[:, m * T:(m + 1) * T], ACT.Identity, scale=par("ln_in_g", j, 1),
                            bias=par("ln_in_b", j, 1))
                    if m == 0:
                        own.do(ins)
                    else:
                        ins.then_inc(read_sem("h", t), 1)
            wait_all_read(act, "h")
            f(resid_t[:], hT_t[:], ACT.Copy, scale=ALPHA).then_inc(sem_("resid_ready"), 1)
            act.wait_ge(sem_("dt_biased"), 1)
            own.do(f(dtx, dtr, ACT.Abs))
            own.do(f(dte, dtx, ACT.Exp, scale=-1.0))
            own.do(f(eal, par("a_log"), ACT.Exp))
            f(dtx, dte, ACT.Ln, bias=1.0).then_inc(sem_("log_ready"), 1)
            with act.Fori(0, 3) as i:
                for t in range(4):
                    wait_read(act, TILE["xbc", t], i)
                    own.turns(i, 4, 3) if t == 0 else None
                    for m in range(2):
                        j = i * 8 + (2 * t + m)
                        ins = f(xbcT[:, ds(j, 1), :], xbcT[:, ds(j, 1), :], ACT.Silu, bias=par_at("ssm_b", j))
                        if m == 0:
                            own.do(ins)
                        else:
                            ins.then_inc(sem_("xbc_ready"), 1)
            own.end()
            act.wait_ge(sem_("decay_diff"), 1)
            f(dstate, dstate, ACT.Exp).then_inc(sem_("decay_ready"), 1)
            def glu_tanh(t):
                b = wait_tile(act, "glu", t)
                if t >= 4:
                    wait_read(act, TILE["glu", t - 4])
                f(stat[:, (t % 4) * T:(t % 4 + 1) * T], b[:, T:2 * T], ACT.Tanh, scale=0.5).then_inc(sem_("tanh_ready"), 1)

            def read_whole(name, t):
                b = wait_tile(act, name, t)
                dst, func, scale = (z_t, ACT.Silu, 1.0) if name == "z" else (ga_t, ACT.Tanh, 0.5)
                f(dst[:, t * 512:(t + 1) * 512], b[:], func, scale=scale).then_inc(read_sem(name, t), 1)

            for t in range(4):
                glu_tanh(t)
            b = wait_tile(act, "xtok", 8)
            f(btok, b[:], ACT.Copy).then_inc(read_sem("xtok", 8), 1)
            for rnd, (name, u) in enumerate(ROUNDS):
                g, hf = rnd // 2, rnd % 2
                if hf == 0:
                    act.wait_ge(sem_("state_done"), g + 1)
                    if g >= 2:
                        act.wait_ge(tile_done, TILE["ssd", rnd - 3] + 1)
                    f(state[:, g % 2, :], bank[7][:], ACT.Copy).then_inc(sem_("state_ready"), 1)
                for c in range(TT):
                    n = 2 * rnd + c
                    if c == 1:
                        act.wait_ge(sem_("seg_done"), n + 1)
                        if g:
                            act.wait_ge(tile_done, TILE["ssd", rnd - 2] + 1)
                        f(cexp[:, hf, :], bank[5][:], ACT.Exp).then_inc(sem_("cexp_done"), 1)
                    act.wait_ge(sem_("seg_masked"), n + 1)
                    f(ein[:, c, :], ein[:, c, :], ACT.Exp).then_inc(sem_("exp_done"), 1)
                for t in (2 * u, 2 * u + 1):
                    if name == "glu":
                        glu_tanh(t)
                    else:
                        read_whole(name, t)
            for g in range(G):
                act.wait_ge(tile_done, TILE["ssd", 7] + 1)
                act.wait_ge(sem_("yz_ready"), 2 * g + 2)
                f(ssm_sq[:, 4 * g:4 * g + 4, :], yz[:, 4 * g:4 * g + 4, :], ACT.Square).then_inc(sem_("ysq_ready"), 1)
            for t in range(4, 8):
                read_whole("gate", t)
            act.wait_ge(sem_("yvar_ready"), 2)
            f(stat[:], stat[:], ACT.Sqrt).then_inc(sem_("ystd_ready"), 1)
            norm("cn", scr1, by("cn_centred"), b=lambda k: par("conv_ln_b", k, 1), func=ACT.Silu, dst=conv_o)
            norm("n1", scr1, by("n1_centred"), b=lambda k: par("ln1_b", k, 1), dst=hT)
            act.wait_ge(sem_("n1_out"), KD)
            f(resid_t[:], hT_t[:], ACT.Copy, scale=ALPHA).then_inc(sem_("resid_ready"), 1)

            def silu_gate(t, turn=0):
                act.wait_ge(sem_("ffn_conv"), t + 1 + 4 * turn)
                if t >= 2:
                    act.wait_ge(sem_("act_ready"), t - 1 + 4 * turn)
                f(sig_t[:, t % 2, :], half_t[:, t % 2, 0:T], ACT.Silu).then_inc(sem_("silu_gate"), 1)

            for t in range(4):
                silu_gate(t)
            with act.Fori(0, 4) as i:
                for t in range(4, 8):
                    silu_gate(t, i)
            for t in (20, 21):
                silu_gate(t)
            norm("n2", scr1, by("n2_centred"), b=lambda k: par("ln2_b", k, 1), dst=resid)
            act.wait_ge(sem_("mod_ready"), 1)
            norm("r1", resid, by("n2_out", 2), b=lambda k: mod[:, k:k + 1], dst=hT)
            act.wait_ge(sem_("r1_ssq"), 1)
            for t in range(8):
                b = wait_tile(act, "qk", t)
                f(raw[t], b[:], ACT.Copy).then_inc(read_sem("qk", t), 1)
            for t in range(4):
                b = wait_tile(act, "v", t)
                f((vm if t < 2 else vd)[:, t % 2, :], b[:], ACT.Copy).then_inc(read_sem("v", t), 1)

            def soften(a):
                act.wait_ge(sem_("max_ready"), a + 1)
                for c in range(TT):
                    f(prob[:, a % 2, c * T:(c + 1) * T], srow[:, a % 2, c * T:(c + 1) * T], ACT.Exp,
                      bias=mx[:, (a % 2) * 2 + c:(a % 2) * 2 + c + 1],
                      accum_out=ssum[:, (a % 2) * 2 + c:(a % 2) * 2 + c + 1]).then_inc(sem_("exped"), 1)

            def move(a):
                if a >= 8 and a % 2 == 0:
                    return
                n = a if a < 8 else 8 + (a - 8) // 2
                act.wait_ge(sem_("prT_done"), n + 1)
                f(prT[:, n % 2, :], bank[6][:, 0:384], ACT.Copy).then_inc(sem_("prT_ready"), 1)
                if a < 8 and a % 2 == 0:
                    return
                act.wait_ge(sem_("o_done"), n + 1)
                dst = om[:, a // 2, :] if a < 8 else od[:, n - 8, :]
                f(dst, bank[7][:, 0:T], ACT.Copy).then_inc(sem_("o_read"), 1)

            act.wait_ge(sem_("lam_sums"), 2)
            f(lam[:, 0:2], lam[:, 0:2], ACT.Exp).then_inc(sem_("lam_exp"), 1)
            soften(0)
            for a in range(16):
                if a + 1 < 16:
                    soften(a + 1)
                if a % 2:
                    t = a // 2
                    b = wait_tile(act, "gate2", t)
                    f(gates2_t[:, t * 512:(t + 1) * 512], b[:], ACT.Tanh, scale=0.5).then_inc(read_sem("gate2", t), 1)
                move(a)
            act.wait_ge(sem_("o_read"), 8)
            f(osq[:], od[:], ACT.Square).then_inc(sem_("osq_ready"), 1)
            act.wait_ge(sem_("ovar_ready"), 2)
            f(stat[:], stat[:], ACT.Sqrt).then_inc(sem_("ostd_ready"), 1)
            norm("r2", resid, lambda q: wait_read(act, TILE["out2", q]), b=lambda k: mod[:, 24 + k:25 + k], dst=hT)
            act.wait_ge(sem_("route_exp"), 1)
            own.do(f(r_exp, r_exp, ACT.Exp))
            act.wait_ge(sem_("route_exp"), 2)
            f(r_e2, r_e2, ACT.Exp).then_inc(sem_("route_exped"), 1)
            act.wait_ge(sem_("r2_ssq"), 1)
            for c in range(TT):
                for half in range(2):
                    act.wait_ge(sem_("htok_done"), 2 * c + half + 1)
                    own.do(f(hrest[:, c, half * 512:(half + 1) * 512], bank[2 * c + half][:], ACT.Copy))
                f(hpart[0][:, c, :], hrest[:, c, :], ACT.Copy).then_inc(sem_("part_ready"), 1)
            for c in range(TT):
                act.wait_ge(sem_("rest_ready"), c + 1)
                f(hpart[1][:, c, :], hrest[:, c, :], ACT.Copy).then_inc(sem_("part_ready"), 1)

            def read_gathered(r, v):
                act.wait_ge(sem_("gathered"), v + 1)
                for q in range(2):
                    f(xe[:, r, q * 8 * CAP:(q + 1) * 8 * CAP], bank[q][:], ACT.Copy).then_inc(sem_("xe_ready"), 1)

            def read_selT(r, v):
                act.wait_ge(sem_("selT_done"), v + 1)
                f(selT[:, r, :], bank[6][:, 0:T], ACT.Copy).then_inc(sem_("selT_ready"), 1)

            def silu_gates(v):
                act.wait_ge(sem_("gate_used"), v + 1)
                f(sgate, bank[2][:], ACT.Silu).then_inc(sem_("gate_silu"), 1)

            def read_hidT(v):
                act.wait_ge(sem_("hidT_done"), v + 1)
                f(hidT, bank[2][:], ACT.Copy).then_inc(sem_("hidT_ready"), 1)

            def read_first_half(r, v):
                act.wait_ge(sem_("down_used"), v + 1)
                f(oute[:, r, 0:512], bank[4][:], ACT.Copy).then_inc(sem_("oute_ready"), 1)

            def two_pairs(v, more):
                silu_gates(v)
                read_selT(0, v)
                read_hidT(v)
                read_gathered(1, v + 1)
                read_first_half(0, v)
                silu_gates(v + 1)
                read_hidT(v + 1)
                read_selT(1, v + 1)
                read_first_half(1, v + 1)
                if more:
                    read_gathered(0, v + 2)

            def moe_pass(b):
                read_gathered(0, b * NPAIR)
                with act.Fori(0, NPAIR // 2 - 1) as i:
                    two_pairs(i * 2 + b * NPAIR, True)
                two_pairs(NPAIR - 2 + b * NPAIR, False)

            moe_pass(0)
            act.wait_ge(sem_("counted"), 1)
            n_max = act.value_load(cnt_i[0:1, 0:1], min_val=0, max_val=T)
            for b in range(1, NPASS):
                with act.If(n_max > b * CAP):
                    moe_pass(b)
            norm("f", resid, by("x_final", 2))
            for t in (0, 1):
                act.wait_ge(sem_("outT_done"), t + 1)
                f(sc1_t[:, t * 512:(t + 1) * 512], bank[t][:], ACT.Copy).then_inc(sem_("out_ready"), 1)

        @block.vector
        def _(dve):
            V = nc.vector
            own = Own(dve, dve_step)
            do = own.do
            stt, ts, tt = V.scalar_tensor_tensor, V.tensor_scalar, V.tensor_tensor

            def bc(ap, n):
                return ap.unsqueeze(1).to_broadcast([P, n, T])

            def norm(p, src, dst, g, eps, centre=True, filler=lambda: None):
                x_ = src
                if centre:
                    dve.wait_ge(sem_(p + "_sum"), 1)
                    do(ts(stat[:, 0:T], bank[7][:, 0:T], 1.0 / D, None, ALU.mult))
                    for q in range(4):
                        tt(scr1[:, 2 * q:2 * q + 2, :], src[:, 2 * q:2 * q + 2, :], bc(stat[:, 0:T], 2),
                           ALU.subtract).then_inc(sem_(p + "_centred"), 1)
                    x_ = scr1
                filler()
                dve.wait_ge(sem_(p + "_ssq"), 1)
                if centre:
                    dve.wait_ge(sem_(p + "_centred"), 4)
                ts(stat[:, 0:T], bank[7][:, 0:T], 1.0 / D, eps, ALU.mult, ALU.add).then_inc(sem_(p + "_var"), 1)
                dve.wait_ge(sem_(p + "_std"), 1)
                do(V.reciprocal(stat[:, T:2 * T], stat[:, T:2 * T]))
                for k in range(KD):
                    stt(dst[:, k, :], x_[:, k, :], g(k), stat[:, T:2 * T], ALU.mult,
                        ALU.mult).then_inc(sem_(p + "_scaled"), 1)

            for b in range(NB):
                dve.sem_inc(tile_read[b], 1)
            dve.wait_ge(x_in, 16)
            do(V.tensor_reduce(mx[:, 0:2], x_tok[:], AX_X, ALU.add))
            do(ts(mx[:, 0:2], mx[:, 0:2], 1.0 / D, None, ALU.mult))
            tt(x_tok[:], x_tok[:], mx[:, 0:2].unsqueeze(2).to_broadcast([P, TT, D]),
               ALU.subtract).then_inc(sem_("x_centred"), 1)
            dve.wait_ge(sem_("x_sq"), 2)
            ts(ssum[:, 0:2], ssum[:, 0:2], 1.0 / D, LN_EPS, ALU.mult, ALU.add).then_inc(sem_("x_var"), 1)
            dve.wait_ge(sem_("x_std"), 1)
            do(V.reciprocal(rsum[:, 0:2], ssum[:, 0:2]))
            tt(x_tok[:], x_tok[:], rsum[:, 0:2].unsqueeze(2).to_broadcast([P, TT, D]),
               ALU.mult).then_inc(sem_("xn_ready"), 1)
            dve.wait_ge(params_in, 48)
            dve.wait_ge(sem_("dt_done"), 1)
            tt(v3(dtr, H), v3(bank[6][:, 0:2 * H], H), par("dt_bias").unsqueeze(1).to_broadcast([P, TT, H]),
               ALU.add).then_inc(sem_("dt_biased"), 1)
            dve.wait_ge(sem_("log_ready"), 1)
            do(stt(dtr, dtr, 0.0, dtx, ALU.max, ALU.add))
            stt(v3(dta, H), v3(dtr, H), -1.0, eal.unsqueeze(1).to_broadcast([P, TT, H]), ALU.mult,
                ALU.mult).then_inc(sem_("a_ready"), 1)
            do(ts(par("conv_w"), par("conv_w"), 0.5, None, ALU.mult))
            with dve.Fori(0, 3) as i:
                own.turns(i, 28, 3)
                for t in range(4):
                    b = wait_tile(dve, "xbc", t, i)
                    for m in range(2):
                        j = i * 8 + (2 * t + m)
                        src = b[:, m * T:(m + 1) * T].unsqueeze(1)
                        do(ts(xbcT[:, ds(j, 1), :], src, par_at("ssm_w", j * 4 + 3), None, ALU.mult)) 
                        for s in range(1, 4):
                            ins = stt(xbcT[:, ds(j, 1), s:T], src[:, :, 0:T - s], par_at("ssm_w", j * 4 + (3 - s)),
                                      xbcT[:, ds(j, 1), s:T], ALU.mult, ALU.add)
                            if m == 1 and s == 3:
                                ins.then_inc(read_sem("xbc", t), 1)
                            else:
                                do(ins)
            own.end()
            dve.wait_ge(sem_("acs_done"), 1)
            do(V.tensor_copy(acs[:], bank[6][:, 0:2 * H]))
            tt(dstate, bank[6][:, 2 * H:3 * H], acs[:, 0:H], ALU.subtract).then_inc(sem_("decay_diff"), 1)
            def glu(t):
                b = wait_tile(dve, "glu", t)
                dve.wait_ge(sem_("tanh_ready"), t + 1)
                stt(glu_v[:, t, CK - 1:], stat[:, (t % 4) * T:(t % 4 + 1) * T], 1.0, b[:, 0:T], ALU.add,
                    ALU.mult).then_inc(read_sem("glu", t), 1)

            for t in range(4):
                glu(t)
            for t in range(8):
                b = wait_tile(dve, "xtok", t)
                c, q = t // 4, t % 4
                tt(xdt[:, c, q * 512:(q + 1) * 512].rearrange("p (h d) -> p h d", h=8),
                   b[:].rearrange("p (h d) -> p h d", h=8),
                   dtr[:, c * H + q * 8:c * H + (q + 1) * 8].unsqueeze(2).to_broadcast([P, 8, HD]),
                   ALU.mult).then_inc(read_sem("xtok", t), 1)
            def first_tap():
                dve.wait_ge(sem_("padded"), 1)
                wait_all_read(dve, "glu")
                for k in range(KD):
                    ts(conv_o[:, k, :], glu_v[:, k, 0:T], par("conv_w", k * CK, 1), par("conv_b", k, 1), ALU.mult,
                       ALU.add).then_inc(sem_("tap"), 1)

            def taps(a, b):
                with dve.Fori(a, b) as i:
                    for k in range(KD):
                        dve.wait_ge(sem_("tap"), i * KD + (k - KD + 1))
                        stt(conv_o[:, k, :], glu_v[:, k, ds(i, T)], par_at("conv_w", i + k * CK), conv_o[:, k, :],
                            ALU.mult, ALU.add).then_inc(sem_("tap"), 1)

            def mask_step(rnd, c):
                n, g, hf = 2 * rnd + c, rnd // 2, rnd % 2
                dve.wait_ge(sem_("seg_done"), n + 1)
                if c == 1:
                    dve.wait_ge(sem_("cexp_done"), rnd + 1)
                if rnd:
                    dve.wait_ge(*((tile_done, TILE["ssd", rnd - 1] + 1) if c else (sem_("y_half"), rnd)))
                for j in range(4):
                    h = c * H + g * 8 + hf * 4 + j
                    ins = stt(ein[:, c, j * P:(j + 1) * P], bank[4 + c][:, j * P:(j + 1) * P], acs[:, h:h + 1],
                              con("ssm_mask"), ALU.subtract, ALU.add)
                    if j == 3:
                        ins.then_inc(sem_("seg_masked"), 1)
                    else:
                        do(ins)

            def decay_step(rnd, c):
                n, g, hf = 2 * rnd + c, rnd // 2, rnd % 2
                dve.wait_ge(sem_("exp_done"), n + 1)
                dve.wait_ge(sem_("cb_done"), g + 1)
                tt(v3(ein[:, c, :], P), v3(ein[:, c, :], P),
                   bank[6][:, c * P:(c + 1) * P].unsqueeze(1).to_broadcast([P, 4, P]),
                   ALU.mult).then_inc(sem_("mt_ready"), 1)
                if c == 1:
                    tt(v3(cexp[:, hf, :], P), v3(cexp[:, hf, :], P),
                       xbcT[:, KS + G + g, P:2 * P].unsqueeze(1).to_broadcast([P, 4, P]),
                       ALU.mult).then_inc(sem_("ce_ready"), 1)

            def skip(t):
                b = wait_tile(dve, "ssd", t)
                for m in range(2):
                    j = 2 * t + m
                    ins = stt(yz[:, j, :], xbcT[:, j, :], par("ssm_d", j, 1), b[:, m * T:(m + 1) * T], ALU.mult, ALU.add)
                    if m == 0:
                        do(ins)
                    else:
                        ins.then_inc(read_sem("ssd", t), 1)

            for rnd, (name, u) in enumerate(ROUNDS):
                mask_step(rnd, 0)
                mask_step(rnd, 1)
                decay_step(rnd, 0)
                decay_step(rnd, 1)
                if name == "glu":
                    glu(2 * u)
                    glu(2 * u + 1)
                elif rnd == 2:
                    first_tap()
                    taps(1, 3)
                else:
                    taps(3 * (rnd - 2), 3 * (rnd - 1))
                skip(rnd)
            taps(18, 27)
            dve.wait_ge(sem_("yssq_done"), 1)
            for q in range(2):
                ts(stat[:, q * 512:(q + 1) * 512], bank[4 + q][:], 1.0 / 512, RMS_EPS, ALU.mult,
                   ALU.add).then_inc(sem_("yvar_ready"), 1)
            dve.wait_ge(sem_("ystd_ready"), 1)
            do(V.reciprocal(stat[:], stat[:]))
            dve.wait_ge(sem_("ysq_ready"), 4)
            dve.wait_ge(sem_("yz_ready"), 8)
            for j in range(KS):
                g = j // 4
                stt(yz[:, j, :], yz[:, j, :], par("ssm_norm", j, 1), stat[:, g * T:(g + 1) * T], ALU.mult,
                    ALU.mult).then_inc(sem_("yn_ready"), 1)
            taps(27, CK)
            def open_gate(name, t, first):
                b = wait_tile(dve, name, t)
                part = gates[:, first + 2 * t:first + 2 * t + 2, :]
                stt(part, part, 1.0, v3(b[:], T), ALU.add, ALU.mult).then_inc(read_sem(name, t), 1)

            wait_all_read(dve, "gate")
            open_gate("ssm_out", 0, 8)
            open_gate("ssm_out", 1, 8)
            dve.wait_ge(sem_("tap"), CK * KD)
            dve.wait_ge(sem_("yn_ready"), KS)
            norm("cn", conv_o, conv_o, lambda k: par("conv_ln_g", k, 1), LN_EPS,
                 filler=lambda: open_gate("ssm_out", 2, 8))
            open_gate("ssm_out", 3, 8)
            for t in range(4):
                open_gate("conv_out", t, 0)
                wait_read(dve, TILE["conv_out", t])
                wait_read(dve, TILE["ssm_out", t])
                tt(gates[:, 2 * t:2 * t + 2, :], gates[:, 2 * t:2 * t + 2, :], gates[:, 8 + 2 * t:10 + 2 * t, :],
                   ALU.add).then_inc(sem_("merged"), 1)
            dve.wait_ge(sem_("resid_ready"), 1)
            for t in range(4):
                b = wait_tile(dve, "mix", t)
                stt(resid[:, 2 * t:2 * t + 2, :], v3(b[:], T), 0.5, resid[:, 2 * t:2 * t + 2, :], ALU.mult,
                    ALU.add).then_inc(read_sem("mix", t), 1)
            wait_all_read(dve, "mix")
            norm("n1", resid, hT, lambda k: par("ln1_g", k, 1), LN_EPS)

            def ffn_conv(t, turn=0):
                b = wait_tile(dve, "up", t, turn)
                if t >= 2:
                    dve.wait_ge(sem_("act_ready"), t - 1 + 4 * turn)
                for m in range(2):
                    ch = turn * 4 + (t + m * KF)
                    src, dst = b[:, m * T:(m + 1) * T], half_t[:, t % 2, m * T:(m + 1) * T]
                    do(ts(dst, src, par_at("ffn_w", ch * 3 + 2), par_at("ffn_b", ch), ALU.mult, ALU.add))
                    for s in (1, 2):
                        ins = stt(dst[:, s:T], src[:, 0:T - s], par_at("ffn_w", ch * 3 + (2 - s)), dst[:, s:T],
                                  ALU.mult, ALU.add)
                        if (m, s) == (1, 2):
                            do(ins)
                        else:
                            do(ins)
                dve.sem_inc(read_sem("up", t), 1)
                dve.sem_inc(sem_("ffn_conv"), 1)

            def ada_sum(i, turn=0):
                dve.wait_ge(sem_(f"ada_in{i % 2}"), turn * 16 + (i // 2 + 1) * 16)
                if i >= 2:
                    dve.wait_ge(sem_("ada_done"), turn * 2 + (i - 1))
                w, acc = v3(expert[4 + i % 2], 512), ada_acc[:, i % 2, :]
                do(ts(acc, w[:, 0, :], cact[:, 0:1], None, ALU.mult))
                for k in range(1, KD):
                    ins = stt(acc, w[:, k, :], cact[:, k:k + 1], acc, ALU.mult, ALU.add)
                    if k < KD - 1:
                        do(ins)
                    else:
                        ins.then_inc(sem_("ada_summed"), 1)

            dve.wait_ge(sem_("n1_scaled"), KD)
            dve.wait_ge(sem_("n1_out"), KD)
            dve.wait_ge(sem_("c_ready"), 1)
            for t in range(4):
                ffn_conv(t)
                if t % 2:
                    ada_sum(t // 2)
            with dve.Fori(0, 4) as i:
                own.turns(i, 24 + 14, 4)
                for t in range(4, 8):
                    ffn_conv(t, i)
                    if t % 2:
                        ada_sum(t // 2, i)
            own.end()
            for t in (20, 21):
                ffn_conv(t)
            ada_sum(10)
            ada_sum(11)
            dve.wait_ge(sem_("resid_ready"), 2)
            for t in range(4):
                b = wait_tile(dve, "down", t)
                tt(resid[:, 2 * t:2 * t + 2, :], v3(b[:], T), resid[:, 2 * t:2 * t + 2, :],
                   ALU.add).then_inc(read_sem("down", t), 1)
            wait_all_read(dve, "down")
            norm("n2", resid, resid, lambda k: par("ln2_g", k, 1), LN_EPS)
            dve.wait_ge(sem_("ada_done"), 12)
            do(tt(mod, bank[6][:, 0:48], par("b_ada"), ALU.add))
            dve.sem_inc(sem_("mod_ready"), 1)
            do(stt(gs1[:], mod[:, 8:16], 1.0, par("norm1_g"), ALU.add, ALU.mult))
            do(stt(gs2[:], mod[:, 32:40], 1.0, par("norm2_g"), ALU.add, ALU.mult))
            do(ts(g1h[:], mod[:, 16:24], 0.5, None, ALU.mult))
            do(ts(par("subln_g"), par("subln_g"), 1.0 - LAM_INIT, None, ALU.mult))
            for q, (a, b) in enumerate((("lam_q1", "lam_k1"), ("lam_q2", "lam_k2"))):
                do(tt(lamp[:, q * 64:(q + 1) * 64], par(a), par(b), ALU.mult))
                V.tensor_reduce(lam[:, q:q + 1], lamp[:, q * 64:(q + 1) * 64], AX_X, ALU.add).then_inc(sem_("lam_sums"), 1)
            norm("r1", resid, hT, lambda k: gs1[:, k:k + 1], NORM_EPS, centre=False)
            dve.wait_ge(sem_("r1_scaled"), KD)
            cos, sin = bc(con("cos"), 2), bc(con("sin"), 2)
            for t in range(8):
                b = wait_tile(dve, "swap", t)
                dst = qk[:, 2 * t:2 * t + 2, :]
                do(tt(dst, v3(raw[t], T), cos, ALU.mult))
                tt(v3(rtmp, T), v3(b[:], T), sin, ALU.mult).then_inc(read_sem("swap", t), 1)
                wait_read(dve, TILE["swap", t])
                tt(dst, dst, v3(rtmp, T), ALU.add).then_inc(sem_("rope_ready"), 1)
                dve.wait_ge(sem_("rope_ready"), t + 1)
            dve.wait_ge(sem_("lam_exp"), 1)
            do(tt(lam[:, 2:3], lam[:, 1:2], lam[:, 0:1], ALU.subtract))
            do(ts(lam[:, 3:4], lam[:, 2:3], LAM_INIT, None, ALU.subtract))

            def maxima(a):
                r = a % 2
                dve.wait_ge(sem_("scored"), a + 1)
                if a >= 2:
                    dve.wait_ge(sem_("exped"), 2 * (a - 1))
                stt(srow[:, r, :], bank[4 + r][:], 0.125, con("att_mask"), ALU.mult, ALU.add).then_inc(sem_("masked"), 1)
                dve.wait_ge(sem_("masked"), a + 1)
                do(V.tensor_reduce(mx[:, 2 * r:2 * r + 2], v3(srow[:, r, :], T), AX_X, ALU.max))
                ts(mx[:, 2 * r:2 * r + 2], mx[:, 2 * r:2 * r + 2], -1.0, None, ALU.mult).then_inc(sem_("max_ready"), 1)

            maxima(0)
            for a in range(16):
                r = a % 2
                if a < 8 or r == 0:
                    if a >= 1:
                        dve.wait_ge(sem_("prT_done"), a if a <= 8 else 8 + (a - 8) // 2)
                    maxima(a + 1)
                dve.wait_ge(sem_("exped"), 2 * (a + 1))
                do(V.reciprocal(rsum[:, 2 * r:2 * r + 2], ssum[:, 2 * r:2 * r + 2]))
                pr = v3(prob[:, r, :], T)
                if a < 8 or r == 0:
                    ins = tt(pr, pr, rsum[:, 2 * r:2 * r + 2].unsqueeze(2).to_broadcast([P, TT, T]), ALU.mult)
                    if a < 8:
                        ins.then_inc(sem_("prob_ready"), 1)
                    else:
                        do(ins)
                else:
                    do(ts(rsum[:, 2:4], rsum[:, 2:4], lam[:, 3:4], None, ALU.mult))
                    for c in range(TT):
                        ins = stt(pr[:, c, :], pr[:, c, :], rsum[:, 2 + c:3 + c], prob[:, 0, c * T:(c + 1) * T],
                                  ALU.mult, ALU.add)
                        if c == 0:
                            do(ins)
                        else:
                            ins.then_inc(sem_("prob_ready"), 1)
                    if a + 1 < 16:
                        dve.wait_ge(sem_("prob_ready"), 9 + (a - 8) // 2)
                        maxima(a + 1)
            dve.wait_ge(sem_("ossq_done"), 1)
            for q in range(2):
                ts(stat[:, q * 512:(q + 1) * 512], bank[4 + q][:], 1.0 / P, NORM_EPS, ALU.mult,
                   ALU.add).then_inc(sem_("ovar_ready"), 1)
            dve.wait_ge(sem_("ostd_ready"), 1)
            do(V.reciprocal(stat[:], stat[:]))
            for h in range(4):
                stt(od[:, h, :], od[:, h, :], par("subln_g"), stat[:, h * T:(h + 1) * T], ALU.mult,
                    ALU.mult).then_inc(sem_("on_ready"), 1)
            wait_all_read(dve, "gate2")
            for t in range(4):
                b = wait_tile(dve, "proj_m", t)
                stt(gates2[:, 2 * t:2 * t + 2, :], gates2[:, 2 * t:2 * t + 2, :], 1.0, v3(b[:], T), ALU.add,
                    ALU.mult).then_inc(read_sem("proj_m", t), 1)
            for t in range(4):
                b = wait_tile(dve, "proj_d", t)
                stt(gates2[:, 8 + 2 * t:10 + 2 * t, :], gates2[:, 8 + 2 * t:10 + 2 * t, :], 1.0, v3(b[:], T), ALU.add,
                    ALU.mult).then_inc(read_sem("proj_d", t), 1)
                wait_read(dve, TILE["proj_d", t])
                wait_read(dve, TILE["proj_m", t])
                tt(gates2[:, 2 * t:2 * t + 2, :], gates2[:, 2 * t:2 * t + 2, :], gates2[:, 8 + 2 * t:10 + 2 * t, :],
                   ALU.add).then_inc(sem_("merged2"), 1)
            for t in range(4):
                b = wait_tile(dve, "out2", t)
                for m in range(2):
                    j = 2 * t + m
                    ins = stt(resid[:, j, :], b[:, m * T:(m + 1) * T], g1h[:, j:j + 1], resid[:, j, :], ALU.mult, ALU.add)
                    if m == 0:
                        do(ins)
                    else:
                        ins.then_inc(read_sem("out2", t), 1)
            wait_all_read(dve, "out2")
            norm("r2", resid, hT, lambda k: gs2[:, k:k + 1], NORM_EPS, centre=False)

            def per_tile(ap, n):
                return ap.unsqueeze(2).to_broadcast([P, TT, n])

            def first_of_max(src, n, hot, top, tmp):
                place = con("place")[:, 0:n].unsqueeze(1).to_broadcast([P, TT, n])
                do(V.tensor_reduce(top, src, AX_X, ALU.max))
                do(tt(hot, src, per_tile(top, n), ALU.is_lt))
                do(stt(hot, hot, 64.0, place, ALU.mult, ALU.add))
                do(V.tensor_reduce(tmp, hot, AX_X, ALU.min))
                do(tt(hot, place, per_tile(tmp, n), ALU.is_equal))

            lg3 = v3(lg[:], EG + E_)
            dve.wait_ge(sem_("logit_done"), 1)
            do(tt(lg3[:], v3(bank[6][:, 0:2 * (EG + E_)], EG + E_), par("b_route").unsqueeze(1).to_broadcast([P, TT, EG + E_]),
                  ALU.add))
            gl = lg3[:, :, 0:EG]
            first_of_max(gl, EG, r_ghot, r_top, r_tmp)
            tt(v3(r_exp, EG), gl, per_tile(r_top, EG), ALU.subtract).then_inc(sem_("route_exp"), 1)
            el = lg3[:, :, EG:].rearrange("p c (g e) -> p c g e", g=EG)
            pr4 = r_prod.rearrange("p (c g e) -> p c g e", c=TT, g=EG)
            for c in range(TT):
                do(tt(pr4[:, c], el[:, c], r_ghot[:, c, :].unsqueeze(2).to_broadcast([P, EG, EP]), ALU.mult))
                do(V.tensor_reduce(r_el[:, c, :], pr4[:, c].rearrange("p g e -> p e g"), AX_X, ALU.add))
            first_of_max(r_el, EP, r_hot1, r_m1, r_tmp)
            do(stt(r_el2, r_hot1, NEG, r_el, ALU.mult, ALU.add))
            first_of_max(r_el2, EP, r_hot2, r_m2, r_tmp)
            tt(r_e2, r_m2, r_m1, ALU.subtract).then_inc(sem_("route_exp"), 1)
            dve.wait_ge(sem_("route_exped"), 1)
            do(V.tensor_reduce(r_gs, v3(r_exp, EG), AX_X, ALU.add))
            do(stt(r_w1, r_e2, 1.0, r_gs, ALU.add, ALU.mult))
            do(V.reciprocal(r_w1, r_w1))
            do(tt(r_w2, r_w1, r_e2, ALU.mult))
            do(tt(r_wx, r_hot1, per_tile(r_w1, EP), ALU.mult))
            do(tt(r_el, r_hot2, per_tile(r_w2, EP), ALU.mult))
            do(tt(r_wx, r_wx, r_el, ALU.add))
            do(tt(r_hot1, r_hot1, r_hot2, ALU.add))
            m4 = mask_t.rearrange("p (c g e) -> p c g e", c=TT, g=EG)
            w4 = wexp[:].rearrange("p (c g e) -> p c g e", c=TT, g=EG)
            for c in range(TT):
                gh = r_ghot[:, c, :].unsqueeze(2).to_broadcast([P, EG, EP])
                do(tt(w4[:, c], gh, r_wx[:, c, :].unsqueeze(1).to_broadcast([P, EG, EP]), ALU.mult))
                ins = tt(m4[:, c], gh, r_hot1[:, c, :].unsqueeze(1).to_broadcast([P, EG, EP]), ALU.mult)
                if c == 0:
                    do(ins)
                else:
                    ins.then_inc(sem_("mask_ready"), 1)
            dve.wait_ge(sem_("mask_ready"), 1)
            dve.wait_ge(sem_("rank_done"), 1)
            do(ts(rank[:], mask_t, -65536.0, 65536.0, ALU.mult, ALU.add))
            do(tt(rank[:], rank[:], bank[7][:, 0:2 * E_], ALU.add))
            do(V.tensor_reduce(cnt_f[:], bank[7][:, 2 * E_:3 * E_], AX_X, ALU.max))
            V.tensor_copy(cnt_i[:], cnt_f[:]).then_inc(sem_("counted"), 1)
            dve.wait_ge(sem_("r2_scaled"), KD)
            for q in range(4):
                V.memset(yacc[:, 2 * q:2 * q + 2, :], 0.0).then_inc(sem_("y_added"), 1)
            dve.sem_inc(sem_("oute_ready"), 2)
            dve.sem_inc(sem_("zeroed"), 1)

            def select(own, r, pair, v, first=False):
                if not first:
                    dve.wait_ge(sem_("selT_done"), v - 1)
                for c in range(TT):
                    for e in range(2):
                        at_ = (c * 2 + e) * CAP
                        col = pair * 2 + (c * E_ + e)
                        own.do(ts(sel[:, r, at_:at_ + CAP], con("slot"), rank[:, ds(col, 1)], None, ALU.is_equal))
                        ins = ts(wsel[:, r, at_:at_ + CAP], con("slot"), rank[:, ds(col, 1)], wexp[:, ds(col, 1)],
                                 ALU.is_equal, ALU.mult)
                        if (c, e) == (1, 1):
                            ins.then_inc(sem_("sel_ready"), 1)
                        else:
                            own.do(ins)

            def add_spread(v):
                for q in range(4):
                    dve.wait_ge(sem_("spread_done"), v * 4 + (q + 1))
                    dve.wait_ge(sem_("y_added"), v * 4 + (q + 1))
                    tt(yacc[:, 2 * q:2 * q + 2, :], yacc[:, 2 * q:2 * q + 2, :], v3(bank[6 + q % 2][:], T),
                       ALU.add).then_inc(sem_("y_added"), 1)

            def hidden(v):
                dve.wait_ge(sem_("gate_silu"), v + 1)
                dve.wait_ge(sem_("up_used"), v + 1)
                tt(hid, sgate, bank[3][:], ALU.mult).then_inc(sem_("hid_ready"), 1)

            def read_second_half(r, v):
                dve.wait_ge(sem_("down_used"), v + 1)
                V.tensor_copy(oute[:, r, 512:D], bank[5][:]).then_inc(sem_("oute_ready"), 1)

            def two_pairs(own, pair, v, more):
                hidden(v)
                if more:
                    select(own, 0, pair + 2, v + 2)
                read_second_half(0, v)
                hidden(v + 1)
                add_spread(v)
                if more:
                    select(own, 1, pair + 3, v + 3)
                read_second_half(1, v + 1)
                add_spread(v + 1)

            def moe_pass(b, own):
                for r in range(2):
                    select(own, r, r, b * NPAIR + r, first=b == 0)
                turns = NPAIR // 2 - 1
                with dve.Fori(0, turns) as i:
                    own.turns(i, 14, turns)
                    two_pairs(own, i * 2, i * 2 + b * NPAIR, True)
                own.end()
                two_pairs(own, NPAIR - 2, NPAIR - 2 + b * NPAIR, False)

            moe_pass(0, own)
            n_max = dve.value_load(cnt_i[0:1, 0:1], min_val=0, max_val=T)
            more = Own(dve, sem_("dve_more_step"))
            for b in range(1, NPASS):
                with dve.If(n_max > b * CAP):
                    more.do(ts(rank[:], rank[:], float(CAP), None, ALU.subtract))
                    moe_pass(b, more)
            dve.drain()
            for k in range(KD):
                stt(resid[:, k, :], yacc[:, k, :], mod[:, 40 + k:41 + k], resid[:, k, :], ALU.mult,
                    ALU.add).then_inc(sem_("x_final"), 1)
            dve.wait_ge(sem_("x_final"), KD)
            norm("f", resid, hT, lambda k: par("final_g", k, 1), NORM_EPS, centre=False)
            for t in (2, 3):
                dve.wait_ge(sem_("outT_done"), t + 1)
                V.tensor_copy(sc1_t[:, t * 512:(t + 1) * 512], bank[t][:]).then_inc(sem_("out_ready"), 1)


IN = ["x", "w_in", "w_conv_out", "w_ssm_out", "w_o", "w_ffn_up", "w_ffn_down", "w_ada_2", "w_in_2", "w_proj_moba_2",
      "w_proj_diff_2", "w_out_2", "w_route", "w_gate_2", "w_up_2", "w_down_2"]


def kernel(**inputs):
    import numpy as np
    import concourse.bacc as bacc
    from concourse.bass_utils import run_bass_kernel_spmd

    a = {k: np.ascontiguousarray(v) for k, v in inputs.items()}
    f32 = np.float32

    def cols(v):
        return np.reshape(v, (-1, P)).T

    def taps(w):
        return np.reshape(w.T, (-1, P, w.shape[0])).transpose(1, 0, 2).reshape(P, -1)

    def every(v):
        return np.broadcast_to(np.reshape(v, (1, -1)), (P, np.size(v)))

    values = {
        "ln_in_g": cols(a["ln_in_g"]), "ln_in_b": cols(a["ln_in_b"]), "conv_w": taps(a["conv_dw_w"][0]),
        "conv_b": cols(a["conv_dw_b"]), "conv_ln_g": cols(a["conv_ln_g"]), "conv_ln_b": cols(a["conv_ln_b"]),
        "ssm_w": taps(a["ssm_conv_w"][0]), "ssm_b": cols(a["ssm_conv_b"]),
        "ssm_d": cols(np.repeat(a["ssm_d"][0], HD)), "ssm_norm": cols(a["ssm_norm_w"]),
        "ln1_g": cols(a["ln1_g"]), "ln1_b": cols(a["ln1_b"]), "ffn_w": taps(a["ffn_dw_w"][0]),
        "ffn_b": cols(a["ffn_dw_b"]), "ln2_g": cols(a["ln2_g"]), "ln2_b": cols(a["ln2_b"]), "b_ada": cols(a["b_ada_2"]),
        "c": cols(a["c_2"]), "norm1_g": cols(a["norm1_g_2"]), "norm2_g": cols(a["norm2_g_2"]),
        "final_g": cols(a["final_g_2"]), "subln_g": cols(a["diff_subln_g_2"]),
        "dt_bias": every(a["ssm_dt_bias"]), "a_log": every(a["ssm_a_log"]),
        "b_route": every(np.concatenate([a["b_group_2"][0], a["b_expert_2"][0]])),
        "lam_q1": every(a["lambda_q1_2"]), "lam_q2": every(a["lambda_q2_2"]),
        "lam_k1": every(a["lambda_k1_2"]), "lam_k2": every(a["lambda_k2_2"]),
    }
    params = np.ascontiguousarray(np.concatenate([values[n] for n, _ in PARAMS], axis=1))

    i = np.arange(P)
    swap = np.zeros((P, P), f32)
    for m in range(P):
        swap[m + 32 if m % 64 < 32 else m - 32, m] = -1.0 if m % 64 < 32 else 1.0
    q, k = np.arange(T), np.arange(T)
    att = np.where(k[None, :] <= q[:, None], f32(0), f32(NEG)).reshape(TT, P, T).transpose(1, 0, 2).reshape(P, TT * T)
    inv = (f32(1.0) / (f32(10000.0) ** (np.arange(0, 64, 2, dtype=f32) / f32(64)))).astype(f32)
    ang = np.arange(T, dtype=f32)[None, :] * inv[i % 32][:, None]
    tables = {
        "ident": np.eye(P, dtype=f32), "upper": (i[:, None] <= i[None, :]).astype(f32),
        "before": (i[:, None] < i[None, :]).astype(f32), "ones": np.ones((P, P), f32), "swap": swap,
        "ssm_mask": np.where(i[None, :] >= i[:, None], f32(0), f32(NEG)), "att_mask": att,
        "cos": np.cos(ang).astype(f32), "sin": np.sin(ang).astype(f32),
        "slot": np.broadcast_to(np.arange(CAP, dtype=f32), (P, CAP)),
        "place": np.broadcast_to(np.arange(EP, dtype=f32), (P, EP)),
    }
    consts = np.ascontiguousarray(np.concatenate([tables[n] for n, _ in CONSTS], axis=1).astype(f32))

    arrays = {"params": params, "consts": consts, "x": a["x"][0]}
    for n in IN[1:]:
        if n == "w_route":
            arrays[n] = np.concatenate([a["w_group_2"][0], a["w_expert_2"][0]], axis=1)
        else:
            arrays[n] = a[n][0]
    nc = bacc.Bacc("TRN2", target_bir_lowering=False, num_devices=1)
    ap = {n: nc.dram_tensor(f"in_{n}", v.shape, F32, kind="ExternalInput").ap() for n, v in arrays.items()}
    out = nc.dram_tensor("out", (T, D), F32, kind="ExternalOutput").ap()
    program(nc, ap["x"], ap["params"], ap["consts"], *[ap[n] for n in IN[1:]], out)
    r = run_bass_kernel_spmd(nc, [{f"in_{n}": np.ascontiguousarray(v) for n, v in arrays.items()}], core_ids=[0])
    return r.results[0]["out"].reshape(1, T, D)
```

```python
from contextlib import ExitStack

import concourse.bass as bass
from concourse import mybir

P = 128
F32 = mybir.dt.float32
I32 = mybir.dt.int32
ALU = mybir.AluOpType
ACT = mybir.ActivationFunctionType
AX_X = mybir.AxisListType.X
ds = bass.ds

T = 256
TT = T // P
D = 1024
KD = D // P
CK = 31
SSM = 2048
KS = SSM // P
H = 32
HD = SSM // H
G = 4
XBC = SSM + 2 * G * P
KX = XBC // P
FF = 2816
KF = FF // P
QK = 512
E_ = 32
EG = 4
EP = E_ // EG
DE = 512
CAP = 64
ALPHA = 2.0 ** 0.25
LN_EPS = 1e-5
RMS_EPS = 1e-5
NORM_EPS = 1e-6
LAM_INIT = 0.2
NEG = -1e30
NB = 4

C_GLU, C_Z, C_XBC, C_DT, C_GA = 0, 2048, 4096, 7168, 7200

PARAMS = [("ln_in_g", 8), ("ln_in_b", 8), ("conv_w", 8 * CK), ("conv_b", 8), ("conv_ln_g", 8), ("conv_ln_b", 8),
          ("ssm_w", KX * 4), ("ssm_b", KX), ("ssm_d", KS), ("ssm_norm", KS), ("ln1_g", 8), ("ln1_b", 8),
          ("ffn_w", 2 * KF * 3), ("ffn_b", 2 * KF), ("ln2_g", 8), ("ln2_b", 8), ("b_ada", 48), ("c", 8),
          ("norm1_g", 8), ("norm2_g", 8), ("subln_g", 1),
          ("dt_bias", H), ("a_log", H), ("b_route", EG + E_), ("lam_q1", 64), ("lam_q2", 64), ("lam_k1", 64),
          ("lam_k2", 64)]
CONSTS = [("ident", P), ("upper", P), ("before", P), ("ones", P), ("swap", P), ("ssm_mask", P), ("att_mask", 2 * T),
          ("cos", T), ("sin", T), ("slot", CAP), ("place", EP)]


def offsets(table):
    at, out = 0, {}
    for name, n in table:
        out[name] = (at, n)
        at += n
    return out, at


PAR, NPAR = offsets(PARAMS)
CON, NCON = offsets(CONSTS)

ROUNDS = [("glu", 2), ("glu", 3), ("z", 0), ("z", 1), ("z", 2), ("z", 3), ("gate", 0), ("gate", 1)]


def tile_order():
    def some(name, a, b):
        return [(name, t) for t in range(a, b)]

    out = some("h", 0, 4) + some("xbc", 0, 12) + some("glu", 0, 4) + some("xtok", 0, 9)
    for r, (name, u) in enumerate(ROUNDS):
        out += some(name, 2 * u, 2 * u + 2) + [("ssd", r)]
    out += some("gate", 4, 8)
    for name, n in (("ssm_out", 4), ("conv_out", 4), ("mix", 4), ("up", 22), ("down", 4), ("qk", 8), ("swap", 4), ("v", 4),
                    ("swap", 8), ("gate2", 8), ("proj_m", 4), ("proj_d", 4), ("out2", 4)):
        out += some(name, 4 if (name, n) == ("swap", 8) else 0, n)
    return {x: i for i, x in enumerate(out)}


TILE = tile_order()
UNITS = [("xbc", 6), ("glu", 4), ("z", 4), ("gate", 4), ("ssm_out", 4), ("conv_out", 2), ("mix", 2),
         ("up", 11), ("down", 8), ("qk", 4), ("v", 2), ("gate2", 4), ("proj_m", 1), ("proj_d", 1), ("out2", 2)]
UNIT, NUNITS = offsets(UNITS)
HALVES = ("glu", "up")
SLOT = 4096


def tiles_of(name):
    return [n for (k, _), n in TILE.items() if k == name]


def U0(name):
    return UNIT[name][0]


def program(nc, x, params, consts, final_rows, w_in, w_conv_out, w_ssm_out, w_o, w_up, w_down, w_ada, w_in2, w_pm,
            w_pd, w_out2, w_route, w_gate_e, w_up_e, w_down_e, out):
    with ExitStack() as ctx:
        def sb(name, n, dt=F32):
            return ctx.enter_context(nc.sbuf_tensor(name, [P, n], dt))

        def sem(name):
            return ctx.enter_context(nc.semaphore(name))

        def v3(ap, b):
            return ap.rearrange("p (a b) -> p a b", b=b)

        par_t, con_t = sb("par", NPAR), sb("con", NCON)

        def par(name, a=0, n=None):
            o, w = PAR[name]
            return par_t[:, o + a:o + a + (w - a if n is None else n)]

        def con(name):
            o, w = CON[name]
            return con_t[:, o:o + w]

        def par_at(name, j):
            return par_t[:, ds(j + PAR[name][0], 1)]

        ident, upper, before, ones, swap_m = (con(n) for n in ("ident", "upper", "before", "ones", "swap"))
        dense = [sb(f"dense{s}", SLOT) for s in range(2)]
        arena = sb("arena", 6 * SLOT)
        expert = [arena[:, s * SLOT:(s + 1) * SLOT] for s in range(6)]
        gate_slot = [[expert[0], expert[1]], [dense[0][:], dense[1][:]]]
        up_slot, down_slot = [expert[2], expert[3]], [expert[4], expert[5]]
        wdt = sb("wdt", KD * H)
        wroute = sb("wroute", KD * (EG + E_))
        hT_t, resid_t, sc1_t, sc2_t = sb("hT", KD * T), sb("resid", KD * T), sb("scratch1", KD * T), sb("scratch2", KD * T)
        hT, resid, scr1, scr2 = v3(hT_t[:], T), v3(resid_t[:], T), v3(sc1_t[:], T), v3(sc2_t[:], T)
        region = sb("region", KF * T)
        stat = sb("stat", 4 * T)
        small = sb("small", 448)

        at = [0]

        def carve(base, n):
            at[0] += n
            return base[:, at[0] - n:at[0]]

        x_tok = carve(arena, TT * D)
        conv_t = x_tok
        glu_v = carve(arena, KD * (T + CK - 1))
        xbc_t = carve(arena, KX * T)
        z_t = carve(arena, KS * T)
        ga_t = carve(arena, KS * T)
        yz_t = carve(arena, KS * T)
        assert at[0] <= 6 * SLOT
        x_tok, conv_o, glu_v, xbcT, zs, gates, yz = (v3(x_tok, D), v3(conv_t, T), v3(glu_v, T + CK - 1), v3(xbc_t, T),
                                                     v3(z_t, T), v3(ga_t, T), v3(yz_t, T))
        at[0] = 0
        xdt = v3(carve(region, TT * SSM), SSM)
        btok = carve(region, G * P)
        xds = v3(carve(region, 2 * 8 * HD), 8 * HD)
        abc = v3(sc1_t[:, 0:1024], 512)
        ein = v3(sc1_t[:, 1024:2048], 512)
        cexp = v3(sc2_t[:, 0:1024], 512)
        state = v3(sc2_t[:, 1024:2048], 512)
        ssm_sq = v3(region[:, 0:KS * T], T)
        ada_acc = v3(sc2_t[:, 1024:2048], 512)
        half_t = v3(sc1_t[:, 0:1024], 512)
        sig_t = v3(sc2_t[:, 0:512], T)
        act_t = v3(region[:], T)
        at[0] = 0
        qk = v3(carve(region, 4 * 4 * T), T)
        vm = v3(carve(region, TT * QK), QK)
        at[0] = 4 * SLOT
        vd = v3(carve(arena, TT * QK), QK)
        om = v3(carve(arena, 4 * T), T)
        od = v3(carve(arena, 4 * T), T)
        gates2_t = carve(arena, KS * T)
        gates2 = v3(gates2_t, T)
        osq = v3(sc2_t[:, 1024:2048], T)
        raw = [sc1_t[:, i * 512:(i + 1) * 512] if i < 4 else sc2_t[:, (i - 4) * 512:(i - 3) * 512] for i in range(8)]
        srow = v3(sc1_t[:, 0:1024], 512)
        prob = v3(sc1_t[:, 1024:2048], 512)
        prT = v3(sc2_t[:, 0:768], 384)
        rtmp = stat[:, 0:512]
        at[0] = 0
        BF16 = mybir.dt.bfloat16
        hpart = [v3(carve(region, TT * D // 2).bitcast(BF16), D) for _ in range(3)]
        oute = v3(carve(region, 2 * D), D)
        selT = v3(carve(region, 2 * T), T)
        hrest = v3(sc2_t[:], D)
        xe = v3(sc2_t[:], KD * 2 * CAP)
        yacc = scr1
        wsel = v3(stat[:], 2 * TT * CAP)
        at[0] = 0
        sgate, hid, hidT = (carve(hT_t, DE) for _ in range(3))
        sel = v3(carve(hT_t, 2 * TT * CAP).bitcast(BF16), 2 * TT * CAP)
        out_t = v3(hT_t[:], D)
        o, w = CON["att_mask"][0], sum(CON[n][1] for n in ("att_mask", "cos", "sin"))
        final_g = con_t[:, o:o + w]
        assert w == D

        at[0] = 0
        dtr, dtx, dte, dta, dts, eal = (carve(small, n) for n in (64, 64, 64, 64, 64, 32))
        mod = carve(small, 48)
        cact = carve(small, 8)
        lam = carve(small, 4)
        dstate = carve(small, 32)
        assert at[0] <= 448
        gs1, gs2, g1h = sb("gs1", 8), sb("gs2", 8), sb("g1h", 8)
        acs = sb("acs", 64)
        lamp = sb("lamp", 128)
        mx, ssum, rsum = sb("mx", 4), sb("ssum", 4), sb("rsum", 4)
        lg = sb("lg", TT * (EG + E_))
        rt = sb("rt", 640)
        wexp, rank = sb("wexp", TT * E_), sb("rank", TT * E_)

        at[0] = 0

        def rcarve(n, w=None):
            r = carve(rt, n)
            return r if w is None else v3(r, w)

        x_part, x_stat = rt[:, 0:12 * TT], rt[:, 12 * TT:14 * TT]
        dt_rows = rt[:, 14 * TT:14 * TT + T]
        logit_rows = stat[:, 2 * T:3 * T]
        mask_t = rcarve(TT * E_)
        mask = v3(mask_t, E_)
        r_ghot, r_exp, r_prod = rcarve(TT * EG, EG), rcarve(TT * EG), rcarve(TT * E_)
        r_el, r_el2, r_hot1, r_hot2, r_wx = (rcarve(TT * EP, EP) for _ in range(5))
        r_top, r_tmp, r_m1, r_m2, r_e2, r_gs, r_w1, r_w2 = (rcarve(TT) for _ in range(8))
        cnt_f, cnt_i = sb("cnt_f", 1), sb("cnt_i", 1, I32)

        bank = [ctx.enter_context(nc.psum_tensor(f"bank{b}", [P, 512], F32)) for b in range(8)]

        sems = {}

        def sem_(name):
            if name not in sems:
                sems[name] = sem(name)
            return sems[name]

        params_in, consts_in, wdt_in, wroute_in = (sem(n) for n in ("params_in", "consts_in", "wdt_in", "wroute_in"))
        x_in = [sem(f"x_in{c}") for c in range(TT)]
        dense_in = [sem(f"dense_in{s}") for s in range(2)]
        gate_in = [[sem(f"gate_in{r}_{e}") for e in range(2)] for r in range(2)]
        up_in, down_in = ([sem(f"{n}_in{e}") for e in range(2)] for n in ("up", "down"))
        tile_done = sem("tile_done")
        tile_read = [sem(f"tile_read{b}") for b in range(NB)]
        act_step, dve_step = sem("act_step"), sem("dve_step")
        final_in, out_written = sem("final_in"), sem("out_written")

        class Own:

            def __init__(self, eng, sm):
                self.eng, self.sm, self.n = eng, sm, 0

            def do(self, ins):
                ins.then_inc(self.sm, 1)
                self.n = self.n + 1
                self.eng.wait_ge(self.sm, self.n)

            def add(self, ins):
                ins.then_inc(self.sm, 1)
                self.n = self.n + 1

            def wait(self, ago=0):
                self.eng.wait_ge(self.sm, self.n - ago)

            def turns(self, i, per, count):
                self.before, self.per, self.count = self.n, per, count
                self.n = self.n + i * per

            def end(self):
                self.n = self.before + self.per * self.count

        def wait_read(eng, n, turn=0):
            eng.wait_ge(tile_read[n % NB], n // NB + 2 + turn)

        def wait_all_read(eng, name):
            for n in {n % NB: n for n in tiles_of(name)}.values():
                wait_read(eng, n)

        def wait_tile(eng, name, t, turn=0):
            eng.wait_ge(tile_done, TILE[name, t] + 1 + NB * turn)
            return bank[TILE[name, t] % NB]

        def read_sem(name, t):
            return tile_read[TILE[name, t] % NB]

        def arrived(n):
            names = [k for m in range(n % 2, n + 1, 2) for k, (u, c) in UNIT.items() if u <= m < u + c]
            return sum(32 if k in HALVES else 16 for k in names)

        def rows(w):
            return w.rearrange("(k p) n -> p k n", p=P)

        wi, wco, wso, wo_, wdn = rows(w_in), rows(w_conv_out), rows(w_ssm_out), rows(w_o), rows(w_down)
        wada, wi2, wpm, wpd, wo2 = rows(w_ada), rows(w_in2), rows(w_pm), rows(w_pd), rows(w_out2)
        wge = w_gate_e.rearrange("e (k p) n -> p e k n", p=P)
        wue = w_up_e.rearrange("e (k p) n -> p e k n", p=P)
        wde = w_down_e.rearrange("e (k p) n -> p e k n", p=P)
        wup2 = w_up.rearrange("(k p) (h n) -> p k h n", p=P, h=2)
        wglu2 = w_in[:, 0:2 * D].rearrange("(k p) (h n) -> p k h n", p=P, h=2)

        NPAIR = E_ // 2
        NPASS = T // CAP

        block = ctx.enter_context(nc.Block())

        @block.sync
        def _(sp):
            for c in range(TT):
                sp.dma_start(x_tok[:, c, :], x[c * P:(c + 1) * P, :]).then_inc(x_in[c], 16)
            sp.dma_start(par_t[:], params).then_inc(params_in, 16)

            def last_use(n):
                name = [k for k, (u, c) in UNIT.items() if u <= n < u + c][0]
                u, units, tiles = n - U0(name), UNIT[name][1], len(tiles_of(name))
                if name == "down":
                    return (tile_done, TILE[name, u // 2] + 1) if u % 2 else (sem_("down_unit"), u // 2 + 1)
                return tile_done, TILE[name, (u + 1) * tiles // units - 1] + 1

            def load(name, u, shape, src, turn=0):
                n = U0(name) + u
                if n >= 2:
                    sm, v = last_use(n - 2)
                    if u >= 2:
                        v = v + turn * (last_use(n)[1] - v)
                    sp.wait_ge(sm, v)
                if name in HALVES:
                    for h in range(2):
                        sp.dma_start(shape(dense[n % 2])[:, :, h, :], src[:, :, h, :]).then_inc(dense_in[n % 2], 16)
                else:
                    sp.dma_start(shape(dense[n % 2]), src).then_inc(dense_in[n % 2], 16)

            def stage(name, units, shape, cols):
                for u in range(2):
                    load(name, u, shape, cols(u))
                if units >= 4:
                    with sp.Fori(0, units // 2 - 1) as i:
                        for u in range(2, 4):
                            load(name, u, shape, cols(i * 2 + u), i)

            def flat(t):
                return v3(t[:], 512)

            def halves(t):
                return t[:].rearrange("p (k h n) -> p k h n", k=KD, h=2)

            stage("xbc", 6, flat, lambda u: wi[:, :, ds(u * 512 + C_XBC, 512)])
            stage("glu", 4, halves, lambda u: wglu2[:, :, :, ds(u * 256, 256)])
            stage("z", 4, flat, lambda u: wi[:, :, ds(u * 512 + C_Z, 512)])
            stage("gate", 4, flat, lambda u: wi[:, :, ds(u * 512 + C_GA, 512)])
            stage("ssm_out", 4, lambda t: v3(t[:], 256), lambda u: wso[:, :, ds(u * 256, 256)])
            stage("conv_out", 2, flat, lambda u: wco[:, :, ds(u * 512, 512)])
            stage("mix", 2, flat, lambda u: wo_[:, :, ds(u * 512, 512)])

            def load_ada(i, turn=0):
                if i >= 2:
                    sp.wait_ge(sem_("ada_summed"), turn * 2 + (i - 1))
                sp.dma_start(v3(expert[4 + i % 2], 512), wada[:, :, ds(turn * 1024 + i * 512, 512)]
                             ).then_inc(sem_(f"ada_in{i % 2}"), 16)

            def up(u, i=0):
                load("up", u, halves, wup2[:, :, :, ds(i * 512 + u * 256, 256)], i)

            up(0)
            up(1)
            wait_all_read(sp, "mix")
            load_ada(0)
            load_ada(1)
            with sp.Fori(0, 4) as i:
                for u in (2, 3):
                    up(u, i)
                    load_ada(u, i)
            up(10)
            for u in range(8):
                load("down", u, lambda t: v3(t[:, 0:KF * P], P), wdn[:, :, u * P:(u + 1) * P])
                if u < 2:
                    load_ada(10 + u)

            def load_expert(slot, arrival, w, k, e, pair):
                src = w[:, ds(pair * 2 + e, 1), :, :].rearrange("p e k n -> p (e k) n")
                sp.dma_start(v3(slot, SLOT // k), src).then_inc(arrival, 16)

            def load_gates(r, pair):
                for e in range(2):
                    load_expert(gate_slot[r][e], gate_in[r][e], wge, KD, e, pair)

            def load_ups(pair):
                for e in range(2):
                    load_expert(up_slot[e], up_in[e], wue, KD, e, pair)

            def load_downs(pair):
                for e in range(2):
                    load_expert(down_slot[e], down_in[e], wde, 4, e, pair)

            load_gates(0, 0)
            load_ups(0)
            for u, c in enumerate((0, 512, 1536, 2048)):
                load("qk", u, flat, wi2[:, :, c:c + 512])
            for u, c in enumerate((1024, 2560)):
                load("v", u, flat, wi2[:, :, c:c + 512])
            stage("gate2", 4, flat, lambda u: wi2[:, :, ds(u * 512 + 3072, 512)])
            load("proj_m", 0, lambda t: v3(t[:], D), wpm)
            load("proj_d", 0, lambda t: v3(t[:], D), wpd)
            stage("out2", 2, flat, lambda u: wo2[:, :, ds(u * 512, 512)])
            wait_all_read(sp, "out2")
            load_downs(0)
            sp.wait_ge(tile_done, TILE["out2", 3] + 1)
            load_gates(1, 1)
            sp.wait_ge(sem_("masked"), 16)
            sp.dma_start(final_g, final_rows).then_inc(final_in, 16)

            def refill(r, pair, v, gates=True):
                if gates:
                    sp.wait_ge(sem_("gate_used"), v)
                    load_gates(r, pair + 1)
                sp.wait_ge(sem_("up_used"), v)
                load_ups(pair)
                sp.wait_ge(sem_("down_used"), v)
                load_downs(pair)

            def rest(v):
                with sp.Fori(0, NPAIR // 2 - 1) as i:
                    refill(0, i * 2 + 1, i * 2 + (v + 1))
                    refill(1, i * 2 + 2, i * 2 + (v + 2))
                refill(0, NPAIR - 1, v + NPAIR - 1, gates=False)

            rest(0)
            sp.wait_ge(sem_("counted"), 1)
            n_max = sp.value_load(cnt_i[0:1, 0:1], min_val=0, max_val=T)
            for b in range(1, NPASS):
                with sp.If(n_max > b * CAP):
                    sp.wait_ge(sem_("gate_used"), b * NPAIR)
                    load_gates(0, 0)
                    refill(1, 0, b * NPAIR)
                    rest(b * NPAIR)
            for c in range(TT):
                for half in range(2):
                    sp.wait_ge(sem_("out_ready"), 2 * c + half + 1)
                    sp.dma_start(out[c * P:(c + 1) * P, half * 512:(half + 1) * 512],
                                 out_t[:, c, half * 512:(half + 1) * 512]).then_inc(out_written, 16)
            sp.wait_ge(out_written, 64)

        @block.gpsimd
        def _(pool):
            nc.gpsimd.memset(glu_v[:, :, 0:CK - 1], 0.0).then_inc(sem_("padded"), 1)
            n = 0
            pool.wait_ge(sem_("decay_ready"), 1)
            for g in range(G):
                wait_read(pool, TILE["xtok", g])
                if g >= 2:
                    pool.wait_ge(sem_("state_done"), g - 1)
                nc.gpsimd.tensor_tensor(
                    xds[:, g % 2, :].rearrange("p (h d) -> p h d", h=8),
                    xdt[:, 0, g * 512:(g + 1) * 512].rearrange("p (h d) -> p h d", h=8),
                    dstate[:, g * 8:(g + 1) * 8].unsqueeze(2).to_broadcast([P, 8, HD]), ALU.mult
                ).then_inc(sem_("xds_ready"), 1)
                for hf in range(2):
                    for c in range(TT):
                        if n >= 2:
                            pool.wait_ge(sem_("seg_done"), n - 1)
                        h0 = c * H + g * 8 + hf * 4
                        nc.gpsimd.tensor_copy(abc[:, n % 2, :].rearrange("p (h t) -> p h t", h=4),
                                              dta[:, h0:h0 + 4].unsqueeze(2).to_broadcast([P, 4, P])
                                              ).then_inc(sem_("abc_ready"), 1)
                        n += 1
            for t in range(8):
                wait_read(pool, TILE["ssd", t])
                wait_read(pool, TILE["z", t])
                nc.gpsimd.tensor_tensor(yz[:, 2 * t:2 * t + 2, :], yz[:, 2 * t:2 * t + 2, :], zs[:, 2 * t:2 * t + 2, :],
                                        ALU.mult).then_inc(sem_("yz_ready"), 1)

            def ffn_product(t, turn=0):
                pool.wait_ge(sem_("silu_gate"), t + 1 + 4 * turn)
                nc.gpsimd.tensor_tensor(act_t[:, ds(turn * 4 + t, 1), :], sig_t[:, t % 2:t % 2 + 1, :],
                                        half_t[:, t % 2, T:2 * T].unsqueeze(1), ALU.mult
                                        ).then_inc(sem_("act_ready"), 1)

            with pool.Fori(0, 5) as i:
                for t in range(4):
                    ffn_product(t, i)
            for t in (20, 21):
                ffn_product(t)
            for c in range(TT):
                pool.wait_ge(sem_("part_ready"), c + 1)
                nc.gpsimd.tensor_tensor(hrest[:, c, :], hrest[:, c, :], hpart[0][:, c, :],
                                        ALU.subtract).then_inc(sem_("rest_ready"), 1)
            for c in range(TT):
                pool.wait_ge(sem_("part_ready"), TT + c + 1)
                nc.gpsimd.tensor_tensor(hpart[2][:, c, :], hrest[:, c, :], hpart[1][:, c, :],
                                        ALU.subtract).then_inc(sem_("rest_ready"), 1)

        @block.tensor
        def _(pe):
            mm, tr = nc.tensor.matmul, nc.tensor.transpose

            def open_tile(name, t, turn=0):
                n = TILE[name, t]
                pe.wait_ge(tile_read[n % NB], n // NB + 1 + turn)
                return bank[n % NB]

            def have(name, u, turn=0):
                n = U0(name) + u
                pe.wait_ge(dense_in[n % 2], arrived(n) + turn * (32 if name in HALVES else 16))
                return dense[n % 2]

            def tile(name, t, turn, k_n, chunk, src, ready=None):
                b = v3(open_tile(name, t, turn)[:], T)
                for m in range(2):
                    for k in range(k_n):
                        if ready is not None and m == 0:
                            ready(k)
                        last = mm(b[:, m, :], chunk(k, m), src[:, k, :], start=k == 0, stop=k == k_n - 1)
                last.then_inc(tile_done, 1)

            def unit_512(name, u, src, turn=0, ready=None):
                w = v3(have(name, u, turn)[:], 512)
                for j in range(2):
                    tile(name, 2 * u + j, turn, KD, lambda k, m: w[:, k, (2 * j + m) * P:(2 * j + m + 1) * P], src,
                         None if j else ready)

            def unit_halves(name, u, src, turn=0, ready=None):
                w = have(name, u, turn)[:].rearrange("p (k h n) -> p k h n", k=KD, h=2)
                for j in range(2):
                    tile(name, 2 * u + j, turn, KD, lambda k, m: w[:, k, m, j * P:(j + 1) * P], src,
                         None if j else ready)

            def stage(name, units, unit, src):
                with pe.Fori(0, units // 2) as i:
                    for u in range(2):
                        unit(name, u, src, i)

            def norm(p, src, ready, centre=True, filler=lambda: None):
                if centre:
                    for k in range(KD):
                        if k % 2 == 0:
                            ready(k // 2)
                        last = mm(bank[7][:, 0:T], ones, src[:, k, :], start=k == 0, stop=k == KD - 1)
                    last.then_inc(sem_(p + "_sum"), 1)
                filler()
                for k in range(KD):
                    if k % 2 == 0:
                        pe.wait_ge(sem_(p + "_sq"), k // 2 + 1)
                    last = mm(bank[7][:, 0:T], ones, scr2[:, k, :], start=k == 0, stop=k == KD - 1)
                last.then_inc(sem_(p + "_ssq"), 1)

            def after_tile(name):
                return lambda q: wait_read(pe, TILE[name, q])

            def by_chunk(name):
                return lambda k: pe.wait_ge(sem_(name), k + 1)

            pe.wait_ge(consts_in, 16)
            for c in range(TT):
                pe.wait_ge(sem_("xn_ready"), c + 1)
                for t in range(4):
                    b = v3((bank[TILE["h", t] % NB] if c else open_tile("h", t))[:], T)
                    for m in range(2):
                        j = 2 * t + m
                        last = tr(b[:, m, c * P:(c + 1) * P], x_tok[:, c, j * P:(j + 1) * P], ident)
                    if c:
                        last.then_inc(tile_done, 1)
            wait_all_read(pe, "h")
            pe.wait_ge(wdt_in, 16)
            wd = v3(wdt[:], H)
            for k in range(KD):
                last = mm(bank[6][0:H, 0:T], wd[:, k, :], hT[:, k, :], start=k == 0, stop=k == KD - 1)
            last.then_inc(sem_("rows_done"), 1)
            unit_512("xbc", 0, hT)
            pe.wait_ge(sem_("rows_copied"), 1)
            for c in range(TT):
                last = tr(bank[6][:, T + c * H:T + (c + 1) * H], dt_rows[0:H, c * P:(c + 1) * P], ident[0:H, 0:H])
            last.then_inc(sem_("dt_done"), 1)
            unit_512("xbc", 1, hT)
            with pe.Fori(0, 2) as i:
                for u in (2, 3):
                    unit_512("xbc", u, hT, i)
            pe.wait_ge(sem_("a_ready"), 1)
            for c in range(TT):
                mm(bank[6][:, c * H:(c + 1) * H], upper, dta[:, c * H:(c + 1) * H], start=True, stop=True)
            mm(bank[6][:, 2 * H:3 * H], ones, dta[:, 0:H], start=True, stop=True).then_inc(sem_("acs_done"), 1)
            for u in range(2):
                unit_halves("glu", u, hT)
            pe.wait_ge(sem_("xbc_ready"), 12)
            for t in range(9):
                b = open_tile("xtok", t)
                for j in range(4):
                    if t < 8:
                        src = xbcT[:, (t % 4) * 4 + j, (t // 4) * P:(t // 4 + 1) * P]
                    else:
                        src = xbcT[:, KS + j, 0:P]
                    last = tr(b[:, j * P:(j + 1) * P], src, ident)
                last.then_inc(tile_done, 1)
            def seg(n):
                pe.wait_ge(sem_("abc_ready"), n + 1)
                if n >= 2:
                    pe.wait_ge(sem_("seg_masked"), n - 1)
                for j in range(4):
                    last = mm(bank[4 + n % 2][:, j * P:(j + 1) * P], abc[:, n % 2, j * P:(j + 1) * P], upper,
                              start=True, stop=True)
                last.then_inc(sem_("seg_done"), 1)

            order = [(g, hf, c) for g in range(G) for hf in range(2) for c in range(TT)]
            for rnd, (name, u) in enumerate(ROUNDS):
                g, hf = rnd // 2, rnd % 2
                if hf == 0:
                    if g:
                        pe.wait_ge(sem_("mt_ready"), 2 * rnd)
                    for cc in range(TT):
                        last = mm(bank[6][:, cc * P:(cc + 1) * P], xbcT[:, KS + g, cc * P:(cc + 1) * P],
                                  xbcT[:, KS + G + g, cc * P:(cc + 1) * P], start=True, stop=True)
                    last.then_inc(sem_("cb_done"), 1)
                    if g == 0:
                        wait_all_read(pe, "xtok")
                    pe.wait_ge(sem_("xds_ready"), g + 1)
                    if g:
                        pe.wait_ge(sem_("state_ready"), g)
                    mm(bank[7][:, 0:512], btok[:, g * P:(g + 1) * P], xds[:, g % 2, :], start=True,
                       stop=True).then_inc(sem_("state_done"), 1)
                seg(2 * rnd)
                seg(2 * rnd + 1)
                (unit_halves if name == "glu" else unit_512)(name, u, hT)
                b = v3(open_tile("ssd", rnd)[:], T)
                for c in range(TT):
                    n = 2 * rnd + c
                    pe.wait_ge(sem_("mt_ready"), n + 1)
                    if c == 1:
                        pe.wait_ge(sem_("ce_ready"), rnd + 1)
                        pe.wait_ge(sem_("state_ready"), g + 1)
                    for j in range(4):
                        h, o = g * 8 + hf * 4 + j, (j % 2) * HD
                        dst = b[o:o + HD, j // 2, c * P:(c + 1) * P]
                        last = mm(dst, xdt[:, c, h * HD:(h + 1) * HD], ein[:, n % 2, j * P:(j + 1) * P],
                                  start=True, stop=c == 0)
                        if c == 1:
                            last = mm(dst, state[:, g % 2, (hf * 4 + j) * HD:(hf * 4 + j + 1) * HD],
                                      cexp[:, hf, j * P:(j + 1) * P], start=False, stop=True)
                    last.then_inc(tile_done if c else sem_("y_half"), 1)
            unit_512("gate", 2, hT)
            for g in range(G):
                pe.wait_ge(sem_("ysq_ready"), g + 1)
                for k in range(4):
                    last = mm(bank[4 + g // 2][:, (g % 2) * T:(g % 2 + 1) * T], ones, ssm_sq[:, 4 * g + k, :],
                              start=k == 0, stop=k == 3)
            last.then_inc(sem_("yssq_done"), 1)
            unit_512("gate", 3, hT)

            def ssm_out(u):
                w = v3(have("ssm_out", u)[:], 256)
                tile("ssm_out", u, 0, KS, lambda k, m: w[:, k, m * P:(m + 1) * P], yz,
                     None if u else by_chunk("yn_ready"))

            for u in range(3):
                ssm_out(u)
            norm("cn", conv_o, lambda q: pe.wait_ge(sem_("tap"), CK * KD), filler=lambda: ssm_out(3))
            unit_512("conv_out", 0, conv_o, ready=by_chunk("cn_out"))
            unit_512("conv_out", 1, conv_o)
            unit_512("mix", 0, gates, ready=lambda k: pe.wait_ge(sem_("merged"), k // 2 + 1))
            unit_512("mix", 1, gates)
            norm("n1", resid, after_tile("mix"))

            def ada_columns(i, turn=0):
                pe.wait_ge(sem_("ada_summed"), turn * 2 + (i + 1))
                for m in range(4):
                    last = mm(bank[6][:, ds(turn * 8 + (4 * i + m), 1)], ada_acc[:, i % 2, m * P:(m + 1) * P],
                              ones[:, 0:1], start=True, stop=True)
                last.then_inc(sem_("ada_done"), 1)

            unit_halves("up", 0, hT, ready=by_chunk("n1_out"))
            unit_halves("up", 1, hT)
            ada_columns(0)
            with pe.Fori(0, 4) as i:
                for u in range(2, 4):
                    unit_halves("up", u, hT, i)
                    ada_columns(u - 1, i)
            unit_halves("up", 10, hT)
            ada_columns(9)
            for t in range(4):
                b = v3(open_tile("down", t)[:], T)
                for m in range(2):
                    w = v3(have("down", 2 * t + m)[:, 0:KF * P], P)
                    for k in range(KF):
                        if t == 0 and m == 0:
                            pe.wait_ge(sem_("act_ready"), k + 1)
                        last = mm(b[:, m, :], w[:, k, :], act_t[:, k, :], start=k == 0, stop=k == KF - 1)
                    last.then_inc(tile_done if m else sem_("down_unit"), 1)
                if t < 2:
                    ada_columns(10 + t)
            norm("n2", resid, after_tile("down"))
            norm("r1", resid, None, centre=False)
            for u in range(4):
                unit_512("qk", u, hT, ready=None if u else by_chunk("r1_out"))

            def swap(t):
                b = open_tile("swap", t)
                wait_read(pe, TILE["qk", t])
                mm(b[:], swap_m, raw[t], start=True, stop=True).then_inc(tile_done, 1)

            for t in range(4):
                swap(t)
            for u in range(2):
                w = v3(have("v", u)[:], 512)
                for c in range(TT):
                    b = open_tile("v", 2 * u + c)
                    for k in range(KD):
                        last = mm(b[:], hT[:, k, c * P:(c + 1) * P], w[:, k, :], start=k == 0, stop=k == KD - 1)
                    last.then_inc(tile_done, 1)
            for t in range(4, 8):
                swap(t)
            pe.wait_ge(sem_("rope_ready"), 4)

            def scores(a):
                if a >= 2:
                    pe.wait_ge(sem_("masked"), a - 1)
                if a == 8:
                    pe.wait_ge(sem_("rope_ready"), 8)
                o, j = (a % 2) * 64, (a // 2) % 4 + (8 if a >= 8 else 0)
                b = v3(bank[4 + a % 2][:], T)
                for c in range(TT):
                    last = mm(b[:, c, :], qk[o:o + 64, j, c * P:(c + 1) * P], qk[o:o + 64, j + 4, :],
                              start=True, stop=True)
                last.then_inc(sem_("scored"), 1)

            def attend(a, filler):
                if a >= 8 and a % 2 == 0:
                    filler()
                    return
                n = a if a < 8 else 8 + (a - 8) // 2
                pe.wait_ge(sem_("prob_ready"), n + 1)
                if n:
                    pe.wait_ge(sem_("prT_ready"), n)
                for q, (c, kc) in enumerate(((0, 0), (1, 0), (1, 1))):
                    last = tr(bank[6][:, q * P:(q + 1) * P], prob[:, a % 2, c * T + kc * P:c * T + (kc + 1) * P], ident)
                last.then_inc(sem_("prT_done"), 1)
                filler()
                pe.wait_ge(sem_("prT_ready"), n + 1)
                p = prT[:, n % 2, :]
                o, w, vv, hh = ((a % 2) * 64, 64, vm, a) if a < 8 else (0, P, vd, n - 8)
                if a == 0:
                    wait_all_read(pe, "v")
                elif a < 8 and a % 2 == 0:
                    pe.wait_ge(sem_("o_read"), a // 2)
                elif a >= 8:
                    pe.wait_ge(sem_("o_read"), n - 4)
                mm(bank[7][o:o + w, 0:T], vv[:, 0, hh * w:(hh + 1) * w], p[:, 0:T], start=True, stop=False)
                mm(bank[7][o:o + w, P:T], vv[:, 1, hh * w:(hh + 1) * w], p[:, T:T + P], start=False,
                   stop=True).then_inc(sem_("o_done"), 1)

            scores(0)
            for a in range(16):
                if a + 1 < 16:
                    scores(a + 1)
                w = v3(have("gate2", a // 4)[:], 512)
                m = a % 2
                b = v3((bank[TILE["gate2", a // 2] % NB] if m else open_tile("gate2", a // 2))[:], T)

                def some(k0, k1):
                    for k in range(k0, k1):
                        last = mm(b[:, m, :], w[:, k, (a % 4) * P:(a % 4 + 1) * P], hT[:, k, :], start=k == 0,
                                  stop=k == KD - 1)
                    if m and k1 == KD:
                        last.then_inc(tile_done, 1)

                some(0, 6)
                attend(a, lambda: some(6, KD))
            pe.wait_ge(sem_("osq_ready"), 1)
            for h in range(4):
                last = mm(bank[4 + h // 2][:, (h % 2) * T:(h % 2 + 1) * T], ones, osq[:, h, :], start=True, stop=True)
            last.then_inc(sem_("ossq_done"), 1)
            for name, src, ready, n in (("proj_m", om, "o_read", 8), ("proj_d", od, "on_ready", 4)):
                pe.wait_ge(sem_(ready), n)
                w = v3(have(name, 0)[:], D)
                for t in range(4):
                    tile(name, t, 0, 4, lambda k, m: w[:, k, (2 * t + m) * P:(2 * t + m + 1) * P], src)
            unit_512("out2", 0, gates2, ready=lambda k: pe.wait_ge(sem_("merged2"), k // 2 + 1))
            unit_512("out2", 1, gates2)
            norm("r2", resid, None, centre=False)
            pe.wait_ge(wroute_in, 16)
            wr = v3(wroute[:], EG + E_)
            R = EG + E_
            for k in range(KD):
                pe.wait_ge(sem_("r2_out"), k + 1)
                last = mm(bank[5][0:R, 0:T], wr[:, k, :], hT[:, k, :], start=k == 0, stop=k == KD - 1)
            last.then_inc(sem_("rows_done"), 1)
            for half in range(2):
                for c in range(TT):
                    for k in range(4):
                        last = tr(bank[2 * c + half][:, k * P:(k + 1) * P], hT[:, 4 * half + k, c * P:(c + 1) * P], ident)
                    last.then_inc(sem_("htok_done"), 1)
                if half == 0:
                    pe.wait_ge(sem_("rows_copied"), 2)
                    for c in range(TT):
                        last = tr(bank[6][:, c * R:(c + 1) * R], logit_rows[0:R, c * P:(c + 1) * P], ident[0:R, 0:R])
                    last.then_inc(sem_("logit_done"), 1)
            pe.wait_ge(sem_("mask_ready"), TT)
            mm(bank[7][:, 0:E_], before, mask[:, 0, :], start=True, stop=True)
            mm(bank[7][:, E_:2 * E_], before, mask[:, 1, :], start=True, stop=False)
            mm(bank[7][:, E_:2 * E_], ones, mask[:, 0, :], start=False, stop=True)
            mm(bank[7][:, 2 * E_:3 * E_], ones, mask[:, 0, :], start=True, stop=False)
            mm(bank[7][:, 2 * E_:3 * E_], ones, mask[:, 1, :], start=False, stop=True).then_inc(sem_("rank_done"), 1)
            pe.wait_ge(sem_("rest_ready"), 2 * TT)

            def gather(r, v):
                pe.wait_ge(sem_("sel_ready"), v + 1)
                for m in range(KD):
                    for c in range(TT):
                        for n in range(3):
                            last = mm(bank[m // 4][:, (m % 4) * 2 * CAP:(m % 4 + 1) * 2 * CAP],
                                      hpart[n][:, c, m * P:(m + 1) * P], sel[:, r, c * 2 * CAP:(c + 1) * 2 * CAP],
                                      start=(c, n) == (0, 0), stop=(c, n) == (TT - 1, 2))
                last.then_inc(sem_("gathered"), 1)

            def turn_selection(r, v):
                pe.wait_ge(sem_("wsel_ready"), v + 1)
                pe.wait_ge(sem_("y_added"), v * 4 + 4)
                for c in range(TT):
                    last = tr(bank[6][:, c * P:(c + 1) * P], wsel[:, r, c * 2 * CAP:(c + 1) * 2 * CAP], ident)
                last.then_inc(sem_("selT_done"), 1)

            def both(dst, tokens, w, k_n, done):
                for k in range(k_n):
                    for e in range(2):
                        last = mm(dst[e * CAP:(e + 1) * CAP, :], tokens(k, e), w[e][:, k, :], start=k == 0,
                                  stop=k == k_n - 1)
                if done is not None:
                    last.then_inc(sem_(done), 1)

            def gate_up(r, v):
                pe.wait_ge(sem_("xe_ready"), v * 2 + 2)
                for e in range(2):
                    pe.wait_ge(gate_in[r][e], (v - r) * 8 + 16)
                both(bank[2], lambda k, e: xe[:, r, (k * 2 + e) * CAP:(k * 2 + e + 1) * CAP],
                     [v3(gate_slot[r][e], DE) for e in range(2)], KD, "gate_used")
                for e in range(2):
                    pe.wait_ge(up_in[e], v * 16 + 16)
                both(bank[3], lambda k, e: xe[:, r, (k * 2 + e) * CAP:(k * 2 + e + 1) * CAP],
                     [v3(up_slot[e], DE) for e in range(2)], KD, "up_used")

            def turn_hidden(v):
                pe.wait_ge(sem_("hid_ready"), v + 1)
                for k in range(4):
                    last = tr(bank[2][:, k * P:(k + 1) * P], hid[:, k * P:(k + 1) * P], ident)
                last.then_inc(sem_("hidT_done"), 1)

            def down(v):
                pe.wait_ge(sem_("hidT_ready"), v + 1)
                pe.wait_ge(sem_("oute_ready"), v * 2 + 2)
                for e in range(2):
                    pe.wait_ge(down_in[e], v * 16 + 16)
                for half in range(2):
                    both(bank[4 + half], lambda k, e: hidT[:, k * P + e * CAP:k * P + (e + 1) * CAP],
                         [v3(down_slot[e], D)[:, :, half * 512:(half + 1) * 512] for e in range(2)], 4,
                         "down_used" if half else None)

            def spread(r, v):
                pe.wait_ge(sem_("oute_ready"), v * 2 + 4)
                pe.wait_ge(sem_("selT_ready"), v + 1)
                for q in range(4):
                    pe.wait_ge(sem_("y_added"), v * 4 + max(q - 1, 0) + 4)
                    b = v3(bank[6 + q % 2][:], T)
                    for m in range(2):
                        j = 2 * q + m
                        last = mm(b[:, m, :], oute[:, r, j * P:(j + 1) * P], selT[:, r, :],
                                  start=True, stop=True)
                    last.then_inc(sem_("spread_done"), 1)

            def two_pairs(v, more):
                gate_up(0, v)
                turn_selection(0, v)
                turn_hidden(v)
                gather(1, v + 1)
                down(v)
                gate_up(1, v + 1)
                spread(0, v)
                turn_hidden(v + 1)
                turn_selection(1, v + 1)
                down(v + 1)
                if more:
                    gather(0, v + 2)
                spread(1, v + 1)

            def moe_pass(b):
                gather(0, b * NPAIR)
                with pe.Fori(0, NPAIR // 2 - 1) as i:
                    two_pairs(i * 2 + b * NPAIR, True)
                two_pairs(NPAIR - 2 + b * NPAIR, False)

            moe_pass(0)
            pe.wait_ge(sem_("counted"), 1)
            n_max = pe.value_load(cnt_i[0:1, 0:1], min_val=0, max_val=T)
            for b in range(1, NPASS):
                with pe.If(n_max > b * CAP):
                    moe_pass(b)
            for half in range(2):
                pe.wait_ge(sem_("x_final"), 4 * half + 4)
                for c in range(TT):
                    for k in range(4):
                        last = tr(bank[2 * c + half][:, k * P:(k + 1) * P], resid[:, half * 4 + k, c * P:(c + 1) * P], ident)
                    last.then_inc(sem_("xT_done"), 1)

        @block.scalar
        def _(act):
            f = nc.scalar.activation
            own = Own(act, act_step)
            act.dma_start(con_t[:], consts).then_inc(consts_in, 16)
            act.dma_start(v3(wdt[:], H), rows(w_in)[:, :, C_DT:C_DT + H]).then_inc(wdt_in, 16)

            def norm(p, src, ready, b=None, func=ACT.Identity, dst=None):
                if ready is not None:
                    for q in range(4):
                        ready(q)
                        f(scr2[:, 2 * q:2 * q + 2, :], src[:, 2 * q:2 * q + 2, :], ACT.Square).then_inc(sem_(p + "_sq"), 1)
                act.wait_ge(sem_(p + "_var"), 1)
                f(stat[:, T:2 * T], stat[:, 0:T], ACT.Sqrt).then_inc(sem_(p + "_std"), 1)
                if p == "r1":
                    act.wait_ge(sem_("mod_ready"), 1)
                if b is not None:
                    for k in range(KD):
                        act.wait_ge(sem_(p + "_scaled"), k + 1)
                        f(dst[:, k, :], dst[:, k, :], func, bias=b(k)).then_inc(sem_(p + "_out"), 1)

            def by(name, step=1):
                return lambda q: act.wait_ge(sem_(name), step * (q + 1))

            for c in range(TT):
                act.wait_ge(sem_("x_var"), c + 1)
                f(rsum[:, c:c + 1], x_stat[:, 2 * c + 1:2 * c + 2], ACT.Sqrt).then_inc(sem_("x_std"), 1)
            act.wait_ge(params_in, 16)
            for t in (0, 2):
                b = wait_tile(act, "h", t)
                for m in range(2):
                    j = 2 * t + m
                    ins = f(hT[:, j, :], b[:, m * T:(m + 1) * T], ACT.Identity, scale=par("ln_in_g", j, 1),
                            bias=par("ln_in_b", j, 1))
                    if m == 0:
                        own.do(ins)
                    else:
                        ins.then_inc(read_sem("h", t), 1)
            wait_all_read(act, "h")
            f(resid_t[:], hT_t[:], ACT.Copy, scale=ALPHA).then_inc(sem_("resid_ready"), 1)
            act.dma_start(v3(wroute[:], EG + E_), rows(w_route)).then_inc(wroute_in, 16)
            act.wait_ge(sem_("rows_done"), 1)
            f(dt_rows[0:H, :], bank[6][0:H, 0:T], ACT.Copy).then_inc(sem_("rows_copied"), 1)
            act.wait_ge(sem_("dt_biased"), 1)
            own.do(f(dtx, dtr, ACT.Abs))
            own.do(f(dte, dtx, ACT.Exp, scale=-1.0))
            own.do(f(eal, par("a_log"), ACT.Exp))
            f(dtx, dte, ACT.Ln, bias=1.0).then_inc(sem_("log_ready"), 1)
            f(cact[:], par("c"), ACT.Silu).then_inc(sem_("c_ready"), 1)
            with act.Fori(0, 3) as i:
                for t in range(4):
                    wait_read(act, TILE["xbc", t], i)
                    own.turns(i, 4, 3) if t == 0 else None
                    for m in range(2):
                        j = i * 8 + (2 * t + m)
                        ins = f(xbcT[:, ds(j, 1), :], xbcT[:, ds(j, 1), :], ACT.Silu, bias=par_at("ssm_b", j))
                        if m == 0:
                            own.do(ins)
                        else:
                            ins.then_inc(sem_("xbc_ready"), 1)
            own.end()
            act.wait_ge(sem_("decay_diff"), 1)
            f(dstate, dstate, ACT.Exp).then_inc(sem_("decay_ready"), 1)
            def glu_tanh(t):
                b = wait_tile(act, "glu", t)
                if t >= 4:
                    wait_read(act, TILE["glu", t - 4])
                f(stat[:, (t % 4) * T:(t % 4 + 1) * T], b[:, T:2 * T], ACT.Tanh, scale=0.5).then_inc(sem_("tanh_ready"), 1)

            def read_whole(name, t):
                b = wait_tile(act, name, t)
                dst, func, scale = (z_t, ACT.Silu, 1.0) if name == "z" else (ga_t, ACT.Tanh, 0.5)
                f(dst[:, t * 512:(t + 1) * 512], b[:], func, scale=scale).then_inc(read_sem(name, t), 1)

            for t in range(4):
                glu_tanh(t)
            b = wait_tile(act, "xtok", 8)
            f(btok, b[:], ACT.Copy).then_inc(read_sem("xtok", 8), 1)
            for rnd, (name, u) in enumerate(ROUNDS):
                g, hf = rnd // 2, rnd % 2
                if hf == 0:
                    act.wait_ge(sem_("state_done"), g + 1)
                    if g >= 2:
                        act.wait_ge(tile_done, TILE["ssd", rnd - 3] + 1)
                    f(state[:, g % 2, :], bank[7][:], ACT.Copy).then_inc(sem_("state_ready"), 1)
                for c in range(TT):
                    n = 2 * rnd + c
                    if c == 1:
                        act.wait_ge(sem_("seg_done"), n + 1)
                        if g:
                            act.wait_ge(tile_done, TILE["ssd", rnd - 2] + 1)
                        f(cexp[:, hf, :], bank[5][:], ACT.Exp).then_inc(sem_("cexp_done"), 1)
                    act.wait_ge(sem_("seg_masked"), n + 1)
                    f(ein[:, c, :], ein[:, c, :], ACT.Exp).then_inc(sem_("exp_done"), 1)
                for t in (2 * u, 2 * u + 1):
                    if name == "glu":
                        glu_tanh(t)
                    else:
                        read_whole(name, t)
            for g in range(G):
                act.wait_ge(tile_done, TILE["ssd", 7] + 1)
                act.wait_ge(sem_("yz_ready"), 2 * g + 2)
                f(ssm_sq[:, 4 * g:4 * g + 4, :], yz[:, 4 * g:4 * g + 4, :], ACT.Square).then_inc(sem_("ysq_ready"), 1)
            for t in range(4, 6):
                read_whole("gate", t)
            act.wait_ge(sem_("yvar_ready"), 2)
            f(stat[:], stat[:], ACT.Sqrt).then_inc(sem_("ystd_ready"), 1)
            for t in range(6, 8):
                read_whole("gate", t)
            norm("cn", scr1, by("cn_centred"), b=lambda k: par("conv_ln_b", k, 1), func=ACT.Silu, dst=conv_o)
            norm("n1", scr1, by("n1_centred"), b=lambda k: par("ln1_b", k, 1), dst=hT)
            act.wait_ge(sem_("n1_out"), KD)
            f(resid_t[:], hT_t[:], ACT.Copy, scale=ALPHA).then_inc(sem_("resid_ready"), 1)

            def silu_gate(t, turn=0):
                act.wait_ge(sem_("ffn_conv"), t + 1 + 4 * turn)
                if t >= 2:
                    act.wait_ge(sem_("act_ready"), t - 1 + 4 * turn)
                f(sig_t[:, t % 2, :], half_t[:, t % 2, 0:T], ACT.Silu).then_inc(sem_("silu_gate"), 1)

            for t in range(4):
                silu_gate(t)
            with act.Fori(0, 4) as i:
                for t in range(4, 8):
                    silu_gate(t, i)
            for t in (20, 21):
                silu_gate(t)
            norm("n2", scr1, by("n2_centred"), b=lambda k: par("ln2_b", k, 1), dst=resid)
            norm("r1", resid, None, b=lambda k: mod[:, k:k + 1], dst=hT)
            act.wait_ge(sem_("r1_ssq"), 1)
            for t in range(8):
                b = wait_tile(act, "qk", t)
                f(raw[t], b[:], ACT.Copy).then_inc(read_sem("qk", t), 1)
            for t in range(4):
                b = wait_tile(act, "v", t)
                f((vm if t < 2 else vd)[:, t % 2, :], b[:], ACT.Copy).then_inc(read_sem("v", t), 1)

            def soften(a):
                act.wait_ge(sem_("max_ready"), a + 1)
                for c in range(TT):
                    f(prob[:, a % 2, c * T:(c + 1) * T], srow[:, a % 2, c * T:(c + 1) * T], ACT.Exp,
                      bias=mx[:, (a % 2) * 2 + c:(a % 2) * 2 + c + 1],
                      accum_out=ssum[:, (a % 2) * 2 + c:(a % 2) * 2 + c + 1]).then_inc(sem_("exped"), 1)

            def move(a):
                if a >= 8 and a % 2 == 0:
                    return
                n = a if a < 8 else 8 + (a - 8) // 2
                act.wait_ge(sem_("prT_done"), n + 1)
                f(prT[:, n % 2, :], bank[6][:, 0:384], ACT.Copy).then_inc(sem_("prT_ready"), 1)
                if a < 8 and a % 2 == 0:
                    return
                act.wait_ge(sem_("o_done"), n + 1)
                dst = om[:, a // 2, :] if a < 8 else od[:, n - 8, :]
                f(dst, bank[7][:, 0:T], ACT.Copy).then_inc(sem_("o_read"), 1)

            act.wait_ge(sem_("lam_sums"), 2)
            f(lam[:, 0:2], lam[:, 0:2], ACT.Exp).then_inc(sem_("lam_exp"), 1)
            soften(0)
            for a in range(16):
                if a == 0:
                    move(0)
                if a + 1 < 16:
                    soften(a + 1)
                if a:
                    move(a)
                if a % 2:
                    t = a // 2
                    b = wait_tile(act, "gate2", t)
                    f(gates2_t[:, t * 512:(t + 1) * 512], b[:], ACT.Tanh, scale=0.5).then_inc(read_sem("gate2", t), 1)
            act.wait_ge(sem_("o_read"), 8)
            f(osq[:], od[:], ACT.Square).then_inc(sem_("osq_ready"), 1)
            act.wait_ge(sem_("ovar_ready"), 2)
            f(stat[:], stat[:], ACT.Sqrt).then_inc(sem_("ostd_ready"), 1)
            norm("r2", resid, lambda q: wait_read(act, TILE["out2", q]), b=lambda k: mod[:, 24 + k:25 + k], dst=hT)
            act.wait_ge(sem_("rows_done"), 2)
            f(logit_rows[0:EG + E_, :], bank[5][0:EG + E_, 0:T], ACT.Copy).then_inc(sem_("rows_copied"), 1)
            act.wait_ge(sem_("r2_ssq"), 1)

            def read_h(c):
                for half in range(2):
                    act.wait_ge(sem_("htok_done"), 2 * half + c + 1)
                    own.do(f(hrest[:, c, half * 512:(half + 1) * 512], bank[2 * c + half][:], ACT.Copy))
                f(hpart[0][:, c, :], hrest[:, c, :], ACT.Copy).then_inc(sem_("part_ready"), 1)

            read_h(0)
            act.wait_ge(sem_("route_exp"), 1)
            f(r_exp, r_exp, ACT.Exp).then_inc(sem_("route_exped"), 1)
            read_h(1)
            act.wait_ge(sem_("route_exp"), 2)
            f(r_e2, r_e2, ACT.Exp).then_inc(sem_("route_exped"), 1)
            for c in range(TT):
                act.wait_ge(sem_("rest_ready"), c + 1)
                f(hpart[1][:, c, :], hrest[:, c, :], ACT.Copy).then_inc(sem_("part_ready"), 1)

            def read_gathered(r, v):
                act.wait_ge(sem_("gathered"), v + 1)
                for q in range(2):
                    f(xe[:, r, q * 8 * CAP:(q + 1) * 8 * CAP], bank[q][:], ACT.Copy).then_inc(sem_("xe_ready"), 1)

            def read_selT(r, v):
                act.wait_ge(sem_("selT_done"), v + 1)
                f(selT[:, r, :], bank[6][:, 0:T], ACT.Copy).then_inc(sem_("selT_ready"), 1)

            def silu_gates(v):
                act.wait_ge(sem_("gate_used"), v + 1)
                f(sgate, bank[2][:], ACT.Silu).then_inc(sem_("gate_silu"), 1)

            def read_hidT(v):
                act.wait_ge(sem_("hidT_done"), v + 1)
                f(hidT, bank[2][:], ACT.Copy).then_inc(sem_("hidT_ready"), 1)

            def read_first_half(r, v):
                act.wait_ge(sem_("down_used"), v + 1)
                f(oute[:, r, 0:512], bank[4][:], ACT.Copy).then_inc(sem_("oute_ready"), 1)

            def two_pairs(v, more):
                silu_gates(v)
                read_selT(0, v)
                read_hidT(v)
                read_gathered(1, v + 1)
                read_first_half(0, v)
                silu_gates(v + 1)
                read_hidT(v + 1)
                read_selT(1, v + 1)
                read_first_half(1, v + 1)
                if more:
                    read_gathered(0, v + 2)

            def moe_pass(b):
                read_gathered(0, b * NPAIR)
                with act.Fori(0, NPAIR // 2 - 1) as i:
                    two_pairs(i * 2 + b * NPAIR, True)
                two_pairs(NPAIR - 2 + b * NPAIR, False)

            moe_pass(0)
            act.wait_ge(sem_("counted"), 1)
            n_max = act.value_load(cnt_i[0:1, 0:1], min_val=0, max_val=T)
            for b in range(1, NPASS):
                with act.If(n_max > b * CAP):
                    moe_pass(b)
            for half in range(2):
                for c in range(TT):
                    act.wait_ge(sem_("xT_done"), 2 * half + c + 1)
                    f(oute[:, c, half * 512:(half + 1) * 512], bank[2 * c + half][:], ACT.Square,
                      accum_out=ssum[:, 2 * c + half:2 * c + half + 1]).then_inc(sem_("out_sq"), 1)
            act.wait_ge(sem_("out_var"), 1)
            f(rsum[:, 0:2], rsum[:, 0:2], ACT.Sqrt).then_inc(sem_("out_std"), 1)

        @block.vector
        def _(dve):
            V = nc.vector
            own = Own(dve, dve_step)
            do = own.do
            stt, ts, tt = V.scalar_tensor_tensor, V.tensor_scalar, V.tensor_tensor

            def bc(ap, n):
                return ap.unsqueeze(1).to_broadcast([P, n, T])

            def norm(p, src, dst, g, eps, centre=True, filler=lambda: None):
                x_ = src
                if centre:
                    dve.wait_ge(sem_(p + "_sum"), 1)
                    do(ts(stat[:, 0:T], bank[7][:, 0:T], 1.0 / D, None, ALU.mult))
                    for q in range(4):
                        tt(scr1[:, 2 * q:2 * q + 2, :], src[:, 2 * q:2 * q + 2, :], bc(stat[:, 0:T], 2),
                           ALU.subtract).then_inc(sem_(p + "_centred"), 1)
                    x_ = scr1
                filler()
                dve.wait_ge(sem_(p + "_ssq"), 1)
                if centre:
                    dve.wait_ge(sem_(p + "_centred"), 4)
                ts(stat[:, 0:T], bank[7][:, 0:T], 1.0 / D, eps, ALU.mult, ALU.add).then_inc(sem_(p + "_var"), 1)
                dve.wait_ge(sem_(p + "_std"), 1)
                do(V.reciprocal(stat[:, T:2 * T], stat[:, T:2 * T]))
                for k in range(KD):
                    stt(dst[:, k, :], x_[:, k, :], g(k), stat[:, T:2 * T], ALU.mult,
                        ALU.mult).then_inc(sem_(p + "_scaled"), 1)

            for b in range(NB):
                dve.sem_inc(tile_read[b], 1)
            for c in range(TT):
                dve.wait_ge(x_in[c], 16)
                for half in range(2):
                    do(V.bn_stats(x_part[:, 12 * c + 6 * half:12 * c + 6 * half + 6],
                                  x_tok[:, c, half * 512:(half + 1) * 512]))
                do(V.bn_aggr(x_stat[:, 2 * c:2 * c + 2], x_part[:, 12 * c:12 * c + 12]))
                ts(x_stat[:, 2 * c + 1:2 * c + 2], x_stat[:, 2 * c + 1:2 * c + 2], LN_EPS, None,
                   ALU.add).then_inc(sem_("x_var"), 1)
            for c in range(TT):
                dve.wait_ge(sem_("x_std"), c + 1)
                do(V.reciprocal(rsum[:, c:c + 1], rsum[:, c:c + 1]))
                ts(x_tok[:, c, :], x_tok[:, c, :], x_stat[:, 2 * c:2 * c + 1], rsum[:, c:c + 1], ALU.subtract,
                   ALU.mult).then_inc(sem_("xn_ready"), 1)
            dve.wait_ge(params_in, 16)
            for t in (1, 3):
                b = wait_tile(dve, "h", t)
                for m in range(2):
                    j = 2 * t + m
                    ins = ts(hT[:, j, :], b[:, m * T:(m + 1) * T], par("ln_in_g", j, 1), par("ln_in_b", j, 1), ALU.mult,
                             ALU.add)
                    if m == 0:
                        do(ins)
                    else:
                        ins.then_inc(read_sem("h", t), 1)
            dve.wait_ge(sem_("dt_done"), 1)
            tt(v3(dtr, H), v3(bank[6][:, T:T + 2 * H], H), par("dt_bias").unsqueeze(1).to_broadcast([P, TT, H]),
               ALU.add).then_inc(sem_("dt_biased"), 1)
            dve.wait_ge(sem_("log_ready"), 1)
            do(stt(dtr, dtr, 0.0, dtx, ALU.max, ALU.add))
            stt(v3(dta, H), v3(dtr, H), -1.0, eal.unsqueeze(1).to_broadcast([P, TT, H]), ALU.mult,
                ALU.mult).then_inc(sem_("a_ready"), 1)
            do(ts(par("conv_w"), par("conv_w"), 0.5, None, ALU.mult))
            with dve.Fori(0, 3) as i:
                own.turns(i, 28, 3)
                for t in range(4):
                    b = wait_tile(dve, "xbc", t, i)
                    for m in range(2):
                        j = i * 8 + (2 * t + m)
                        src = b[:, m * T:(m + 1) * T].unsqueeze(1)
                        do(ts(xbcT[:, ds(j, 1), :], src, par_at("ssm_w", j * 4 + 3), None, ALU.mult))
                        for s in range(1, 4):
                            ins = stt(xbcT[:, ds(j, 1), s:T], src[:, :, 0:T - s], par_at("ssm_w", j * 4 + (3 - s)),
                                      xbcT[:, ds(j, 1), s:T], ALU.mult, ALU.add)
                            if m == 1 and s == 3:
                                ins.then_inc(read_sem("xbc", t), 1)
                            else:
                                do(ins)
            own.end()
            dve.wait_ge(sem_("acs_done"), 1)
            do(V.tensor_copy(acs[:], bank[6][:, 0:2 * H]))
            tt(dstate, bank[6][:, 2 * H:3 * H], acs[:, 0:H], ALU.subtract).then_inc(sem_("decay_diff"), 1)
            def glu(t):
                b = wait_tile(dve, "glu", t)
                dve.wait_ge(sem_("tanh_ready"), t + 1)
                stt(glu_v[:, t, CK - 1:], stat[:, (t % 4) * T:(t % 4 + 1) * T], 1.0, b[:, 0:T], ALU.add,
                    ALU.mult).then_inc(read_sem("glu", t), 1)

            for t in range(4):
                glu(t)
            for t in range(8):
                b = wait_tile(dve, "xtok", t)
                c, q = t // 4, t % 4
                tt(xdt[:, c, q * 512:(q + 1) * 512].rearrange("p (h d) -> p h d", h=8),
                   b[:].rearrange("p (h d) -> p h d", h=8),
                   dtr[:, c * H + q * 8:c * H + (q + 1) * 8].unsqueeze(2).to_broadcast([P, 8, HD]),
                   ALU.mult).then_inc(read_sem("xtok", t), 1)
            def first_tap():
                dve.wait_ge(sem_("padded"), 1)
                wait_all_read(dve, "glu")
                for k in range(KD):
                    ts(conv_o[:, k, :], glu_v[:, k, 0:T], par("conv_w", k * CK, 1), par("conv_b", k, 1), ALU.mult,
                       ALU.add).then_inc(sem_("tap"), 1)

            def taps(a, b):
                with dve.Fori(a, b) as i:
                    for k in range(KD):
                        dve.wait_ge(sem_("tap"), i * KD + (k - KD + 1))
                        stt(conv_o[:, k, :], glu_v[:, k, ds(i, T)], par_at("conv_w", i + k * CK), conv_o[:, k, :],
                            ALU.mult, ALU.add).then_inc(sem_("tap"), 1)

            def mask_step(rnd, c):
                n, g, hf = 2 * rnd + c, rnd // 2, rnd % 2
                dve.wait_ge(sem_("seg_done"), n + 1)
                if c == 1:
                    dve.wait_ge(sem_("cexp_done"), rnd + 1)
                if rnd:
                    dve.wait_ge(*((tile_done, TILE["ssd", rnd - 1] + 1) if c else (sem_("y_half"), rnd)))
                for j in range(4):
                    h = c * H + g * 8 + hf * 4 + j
                    ins = stt(ein[:, c, j * P:(j + 1) * P], bank[4 + c][:, j * P:(j + 1) * P], acs[:, h:h + 1],
                              con("ssm_mask"), ALU.subtract, ALU.add)
                    if j == 3:
                        ins.then_inc(sem_("seg_masked"), 1)
                    else:
                        do(ins)

            def decay_step(rnd, c):
                n, g, hf = 2 * rnd + c, rnd // 2, rnd % 2
                dve.wait_ge(sem_("exp_done"), n + 1)
                dve.wait_ge(sem_("cb_done"), g + 1)
                tt(v3(ein[:, c, :], P), v3(ein[:, c, :], P),
                   bank[6][:, c * P:(c + 1) * P].unsqueeze(1).to_broadcast([P, 4, P]),
                   ALU.mult).then_inc(sem_("mt_ready"), 1)
                if c == 1:
                    tt(v3(cexp[:, hf, :], P), v3(cexp[:, hf, :], P),
                       xbcT[:, KS + G + g, P:2 * P].unsqueeze(1).to_broadcast([P, 4, P]),
                       ALU.mult).then_inc(sem_("ce_ready"), 1)

            def skip(t):
                b = wait_tile(dve, "ssd", t)
                for m in range(2):
                    j = 2 * t + m
                    ins = stt(yz[:, j, :], xbcT[:, j, :], par("ssm_d", j, 1), b[:, m * T:(m + 1) * T], ALU.mult, ALU.add)
                    if m == 0:
                        do(ins)
                    else:
                        ins.then_inc(read_sem("ssd", t), 1)

            for rnd, (name, u) in enumerate(ROUNDS):
                mask_step(rnd, 0)
                mask_step(rnd, 1)
                decay_step(rnd, 0)
                decay_step(rnd, 1)
                if name == "glu":
                    glu(2 * u)
                    glu(2 * u + 1)
                elif rnd == 2:
                    first_tap()
                    taps(1, 3)
                else:
                    taps(3 * (rnd - 2), 3 * (rnd - 1))
                skip(rnd)
            taps(18, 22)
            dve.wait_ge(sem_("yssq_done"), 1)
            for q in range(2):
                ts(stat[:, q * 512:(q + 1) * 512], bank[4 + q][:], 1.0 / 512, RMS_EPS, ALU.mult,
                   ALU.add).then_inc(sem_("yvar_ready"), 1)
            dve.wait_ge(sem_("ystd_ready"), 1)
            do(V.reciprocal(stat[:], stat[:]))
            dve.wait_ge(sem_("ysq_ready"), 4)
            dve.wait_ge(sem_("yz_ready"), 8)
            for j in range(KS):
                g = j // 4
                stt(yz[:, j, :], yz[:, j, :], par("ssm_norm", j, 1), stat[:, g * T:(g + 1) * T], ALU.mult,
                    ALU.mult).then_inc(sem_("yn_ready"), 1)
            taps(22, CK)
            def open_gate(name, t, first):
                b = wait_tile(dve, name, t)
                part = gates[:, first + 2 * t:first + 2 * t + 2, :]
                stt(part, part, 1.0, v3(b[:], T), ALU.add, ALU.mult).then_inc(read_sem(name, t), 1)

            wait_all_read(dve, "gate")
            for t in range(3):
                open_gate("ssm_out", t, 8)
            dve.wait_ge(sem_("tap"), CK * KD)
            dve.wait_ge(sem_("yn_ready"), KS)
            norm("cn", conv_o, conv_o, lambda k: par("conv_ln_g", k, 1), LN_EPS)
            open_gate("ssm_out", 3, 8)
            for t in range(4):
                open_gate("conv_out", t, 0)
                wait_read(dve, TILE["conv_out", t])
                wait_read(dve, TILE["ssm_out", t])
                tt(gates[:, 2 * t:2 * t + 2, :], gates[:, 2 * t:2 * t + 2, :], gates[:, 8 + 2 * t:10 + 2 * t, :],
                   ALU.add).then_inc(sem_("merged"), 1)
            dve.wait_ge(sem_("resid_ready"), 1)
            for t in range(4):
                b = wait_tile(dve, "mix", t)
                stt(resid[:, 2 * t:2 * t + 2, :], v3(b[:], T), 0.5, resid[:, 2 * t:2 * t + 2, :], ALU.mult,
                    ALU.add).then_inc(read_sem("mix", t), 1)
            wait_all_read(dve, "mix")
            norm("n1", resid, hT, lambda k: par("ln1_g", k, 1), LN_EPS)

            def ffn_conv(t, turn=0):
                b = wait_tile(dve, "up", t, turn)
                if t >= 2:
                    dve.wait_ge(sem_("act_ready"), t - 1 + 4 * turn)
                for step in range(3):
                    for m in range(2):
                        ch = turn * 4 + (t + m * KF)
                        src, dst = b[:, m * T:(m + 1) * T], half_t[:, t % 2, m * T:(m + 1) * T]
                        if step == 0:
                            own.add(ts(dst, src, par_at("ffn_w", ch * 3 + 2), par_at("ffn_b", ch), ALU.mult, ALU.add))
                        else:
                            own.wait(1)
                            own.add(stt(dst[:, step:T], src[:, 0:T - step], par_at("ffn_w", ch * 3 + (2 - step)),
                                        dst[:, step:T], ALU.mult, ALU.add))
                own.wait()
                dve.sem_inc(read_sem("up", t), 1)
                dve.sem_inc(sem_("ffn_conv"), 1)

            def ada_sum(i, turn=0):
                dve.wait_ge(sem_(f"ada_in{i % 2}"), turn * 16 + (i // 2 + 1) * 16)
                if i >= 2:
                    dve.wait_ge(sem_("ada_done"), turn * 2 + (i - 1))
                w, acc = v3(expert[4 + i % 2], 512), ada_acc[:, i % 2, :]
                do(ts(acc, w[:, 0, :], cact[:, 0:1], None, ALU.mult))
                for k in range(1, KD):
                    ins = stt(acc, w[:, k, :], cact[:, k:k + 1], acc, ALU.mult, ALU.add)
                    if k < KD - 1:
                        do(ins)
                    else:
                        ins.then_inc(sem_("ada_summed"), 1)

            dve.wait_ge(sem_("n1_scaled"), KD)
            dve.wait_ge(sem_("n1_out"), KD)
            dve.wait_ge(sem_("c_ready"), 1)
            for t in range(4):
                ffn_conv(t)
                if t % 2:
                    ada_sum(t // 2)
            with dve.Fori(0, 4) as i:
                own.turns(i, 24 + 14, 4)
                for t in range(4, 8):
                    ffn_conv(t, i)
                    if t % 2:
                        ada_sum(t // 2, i)
            own.end()
            for t in (20, 21):
                ffn_conv(t)
            ada_sum(10)
            ada_sum(11)
            dve.wait_ge(sem_("resid_ready"), 2)
            for t in range(4):
                b = wait_tile(dve, "down", t)
                tt(resid[:, 2 * t:2 * t + 2, :], v3(b[:], T), resid[:, 2 * t:2 * t + 2, :],
                   ALU.add).then_inc(read_sem("down", t), 1)
            wait_all_read(dve, "down")
            norm("n2", resid, resid, lambda k: par("ln2_g", k, 1), LN_EPS)
            for q in range(4):
                dve.wait_ge(sem_("n2_out"), 2 * q + 2)
                part = resid[:, 2 * q:2 * q + 2, :]
                tt(scr2[:, 2 * q:2 * q + 2, :], part, part, ALU.mult).then_inc(sem_("r1_sq"), 1)
            dve.wait_ge(sem_("ada_done"), 12)
            do(tt(mod, bank[6][:, 0:48], par("b_ada"), ALU.add))
            dve.sem_inc(sem_("mod_ready"), 1)
            do(stt(gs1[:], mod[:, 8:16], 1.0, par("norm1_g"), ALU.add, ALU.mult))
            do(stt(gs2[:], mod[:, 32:40], 1.0, par("norm2_g"), ALU.add, ALU.mult))
            do(ts(g1h[:], mod[:, 16:24], 0.5, None, ALU.mult))
            do(ts(par("subln_g"), par("subln_g"), 1.0 - LAM_INIT, None, ALU.mult))
            for q, (a, b) in enumerate((("lam_q1", "lam_k1"), ("lam_q2", "lam_k2"))):
                do(tt(lamp[:, q * 64:(q + 1) * 64], par(a), par(b), ALU.mult))
                V.tensor_reduce(lam[:, q:q + 1], lamp[:, q * 64:(q + 1) * 64], AX_X, ALU.add).then_inc(sem_("lam_sums"), 1)
            norm("r1", resid, hT, lambda k: gs1[:, k:k + 1], NORM_EPS, centre=False)
            dve.wait_ge(sem_("r1_scaled"), KD)
            def maxima(a):
                r = a % 2
                dve.wait_ge(sem_("scored"), a + 1)
                if a >= 2:
                    dve.wait_ge(sem_("exped"), 2 * (a - 1))
                stt(srow[:, r, :], bank[4 + r][:], 0.125, con("att_mask"), ALU.mult, ALU.add).then_inc(sem_("masked"), 1)
                dve.wait_ge(sem_("masked"), a + 1)
                do(V.tensor_reduce(mx[:, 2 * r:2 * r + 2], v3(srow[:, r, :], T), AX_X, ALU.max))
                ts(mx[:, 2 * r:2 * r + 2], mx[:, 2 * r:2 * r + 2], -1.0, None, ALU.mult).then_inc(sem_("max_ready"), 1)

            def finish(a):
                r = a % 2
                dve.wait_ge(sem_("exped"), 2 * (a + 1))
                do(V.reciprocal(rsum[:, 2 * r:2 * r + 2], ssum[:, 2 * r:2 * r + 2]))
                pr = v3(prob[:, r, :], T)
                if a < 8 or r == 0:
                    ins = tt(pr, pr, rsum[:, 2 * r:2 * r + 2].unsqueeze(2).to_broadcast([P, TT, T]), ALU.mult)
                    if a < 8:
                        ins.then_inc(sem_("prob_ready"), 1)
                    else:
                        do(ins)
                else:
                    do(ts(rsum[:, 2:4], rsum[:, 2:4], lam[:, 3:4], None, ALU.mult))
                    for c in range(TT):
                        ins = stt(pr[:, c, :], pr[:, c, :], rsum[:, 2 + c:3 + c], prob[:, 0, c * T:(c + 1) * T],
                                  ALU.mult, ALU.add)
                        if c == 0:
                            do(ins)
                        else:
                            ins.then_inc(sem_("prob_ready"), 1)

            cos, sin = bc(con("cos"), 2), bc(con("sin"), 2)
            for t in range(8):
                b = wait_tile(dve, "swap", t)
                dst = qk[:, 2 * t:2 * t + 2, :]
                do(tt(dst, v3(raw[t], T), cos, ALU.mult))
                tt(v3(rtmp, T), v3(b[:], T), sin, ALU.mult).then_inc(read_sem("swap", t), 1)
                wait_read(dve, TILE["swap", t])
                tt(dst, dst, v3(rtmp, T), ALU.add).then_inc(sem_("rope_ready"), 1)
                dve.wait_ge(sem_("rope_ready"), t + 1)
                if t == 5:
                    maxima(0)
                if t == 6:
                    finish(0)
            dve.wait_ge(sem_("lam_exp"), 1)
            do(tt(lam[:, 2:3], lam[:, 1:2], lam[:, 0:1], ALU.subtract))
            do(ts(lam[:, 3:4], lam[:, 2:3], LAM_INIT, None, ALU.subtract))

            for a in range(16):
                r = a % 2
                if a < 8 or r == 0:
                    if a >= 1:
                        dve.wait_ge(sem_("prT_done"), a if a <= 8 else 8 + (a - 8) // 2)
                    maxima(a + 1)
                if a:
                    finish(a)
                if a >= 8 and r and a + 1 < 16:
                    dve.wait_ge(sem_("prob_ready"), 9 + (a - 8) // 2)
                    maxima(a + 1)
            dve.wait_ge(sem_("ossq_done"), 1)
            for q in range(2):
                ts(stat[:, q * 512:(q + 1) * 512], bank[4 + q][:], 1.0 / P, NORM_EPS, ALU.mult,
                   ALU.add).then_inc(sem_("ovar_ready"), 1)
            dve.wait_ge(sem_("ostd_ready"), 1)
            do(V.reciprocal(stat[:], stat[:]))
            for h in range(4):
                stt(od[:, h, :], od[:, h, :], par("subln_g"), stat[:, h * T:(h + 1) * T], ALU.mult,
                    ALU.mult).then_inc(sem_("on_ready"), 1)
            wait_all_read(dve, "gate2")
            for t in range(4):
                b = wait_tile(dve, "proj_m", t)
                stt(gates2[:, 2 * t:2 * t + 2, :], gates2[:, 2 * t:2 * t + 2, :], 1.0, v3(b[:], T), ALU.add,
                    ALU.mult).then_inc(read_sem("proj_m", t), 1)
            for t in range(4):
                b = wait_tile(dve, "proj_d", t)
                stt(gates2[:, 8 + 2 * t:10 + 2 * t, :], gates2[:, 8 + 2 * t:10 + 2 * t, :], 1.0, v3(b[:], T), ALU.add,
                    ALU.mult).then_inc(read_sem("proj_d", t), 1)
                wait_read(dve, TILE["proj_d", t])
                wait_read(dve, TILE["proj_m", t])
                tt(gates2[:, 2 * t:2 * t + 2, :], gates2[:, 2 * t:2 * t + 2, :], gates2[:, 8 + 2 * t:10 + 2 * t, :],
                   ALU.add).then_inc(sem_("merged2"), 1)
            for t in range(4):
                b = wait_tile(dve, "out2", t)
                for m in range(2):
                    j = 2 * t + m
                    ins = stt(resid[:, j, :], b[:, m * T:(m + 1) * T], g1h[:, j:j + 1], resid[:, j, :], ALU.mult, ALU.add)
                    if m == 0:
                        do(ins)
                    else:
                        ins.then_inc(read_sem("out2", t), 1)
            wait_all_read(dve, "out2")
            norm("r2", resid, hT, lambda k: gs2[:, k:k + 1], NORM_EPS, centre=False)

            def per_tile(ap, n):
                return ap.unsqueeze(2).to_broadcast([P, TT, n])

            def first_of_max(src, n, hot, top, tmp):
                place = con("place")[:, 0:n].unsqueeze(1).to_broadcast([P, TT, n])
                do(V.tensor_reduce(top, src, AX_X, ALU.max))
                do(tt(hot, src, per_tile(top, n), ALU.is_lt))
                do(stt(hot, hot, 64.0, place, ALU.mult, ALU.add))
                do(V.tensor_reduce(tmp, hot, AX_X, ALU.min))
                do(tt(hot, place, per_tile(tmp, n), ALU.is_equal))

            for q in range(4):
                V.memset(yacc[:, 2 * q:2 * q + 2, :], 0.0).then_inc(sem_("y_added"), 1)
            lg3 = v3(lg[:], EG + E_)
            dve.wait_ge(sem_("logit_done"), 1)
            do(tt(lg3[:], v3(bank[6][:, 0:2 * (EG + E_)], EG + E_), par("b_route").unsqueeze(1).to_broadcast([P, TT, EG + E_]),
                  ALU.add))
            gl = lg3[:, :, 0:EG]
            first_of_max(gl, EG, r_ghot, r_top, r_tmp)
            tt(v3(r_exp, EG), gl, per_tile(r_top, EG), ALU.subtract).then_inc(sem_("route_exp"), 1)
            el = lg3[:, :, EG:].rearrange("p c (g e) -> p c g e", g=EG)
            pr4 = r_prod.rearrange("p (c g e) -> p c g e", c=TT, g=EG)
            for c in range(TT):
                do(tt(pr4[:, c], el[:, c], r_ghot[:, c, :].unsqueeze(2).to_broadcast([P, EG, EP]), ALU.mult))
                do(V.tensor_reduce(r_el[:, c, :], pr4[:, c].rearrange("p g e -> p e g"), AX_X, ALU.add))
            first_of_max(r_el, EP, r_hot1, r_m1, r_tmp)
            do(stt(r_el2, r_hot1, NEG, r_el, ALU.mult, ALU.add))
            first_of_max(r_el2, EP, r_hot2, r_m2, r_tmp)
            tt(r_e2, r_m2, r_m1, ALU.subtract).then_inc(sem_("route_exp"), 1)
            do(tt(r_el2, r_hot1, r_hot2, ALU.add))
            m4 = mask_t.rearrange("p (c g e) -> p c g e", c=TT, g=EG)
            w4 = wexp[:].rearrange("p (c g e) -> p c g e", c=TT, g=EG)
            for c in range(TT):
                gh = r_ghot[:, c, :].unsqueeze(2).to_broadcast([P, EG, EP])
                tt(m4[:, c], gh, r_el2[:, c, :].unsqueeze(1).to_broadcast([P, EG, EP]),
                   ALU.mult).then_inc(sem_("mask_ready"), 1)
            dve.wait_ge(sem_("route_exped"), 2)
            do(V.tensor_reduce(r_gs, v3(r_exp, EG), AX_X, ALU.add))
            do(stt(r_w1, r_e2, 1.0, r_gs, ALU.add, ALU.mult))
            do(V.reciprocal(r_w1, r_w1))
            do(tt(r_w2, r_w1, r_e2, ALU.mult))
            do(tt(r_wx, r_hot1, per_tile(r_w1, EP), ALU.mult))
            do(tt(r_el, r_hot2, per_tile(r_w2, EP), ALU.mult))
            do(tt(r_wx, r_wx, r_el, ALU.add))
            for c in range(TT):
                gh = r_ghot[:, c, :].unsqueeze(2).to_broadcast([P, EG, EP])
                do(tt(w4[:, c], gh, r_wx[:, c, :].unsqueeze(1).to_broadcast([P, EG, EP]), ALU.mult))
            dve.wait_ge(sem_("mask_ready"), TT)
            dve.wait_ge(sem_("rank_done"), 1)
            do(ts(rank[:], mask_t, -65536.0, 65536.0, ALU.mult, ALU.add))
            do(tt(rank[:], rank[:], bank[7][:, 0:2 * E_], ALU.add))
            dve.sem_inc(sem_("oute_ready"), 2)

            def select(own, r, pair, v, first=False):
                if not first:
                    dve.wait_ge(sem_("selT_done"), v - 1)
                places = [((c * 2 + e) * CAP, pair * 2 + (c * E_ + e)) for c in range(TT) for e in range(2)]
                for n, (o, col) in enumerate(places):
                    ins = ts(sel[:, r, o:o + CAP], con("slot"), rank[:, ds(col, 1)], None, ALU.is_equal)
                    own.do(ins) if n < 3 else ins.then_inc(sem_("sel_ready"), 1)
                for n, (o, col) in enumerate(places):
                    ins = ts(wsel[:, r, o:o + CAP], con("slot"), rank[:, ds(col, 1)], wexp[:, ds(col, 1)],
                             ALU.is_equal, ALU.mult)
                    own.do(ins) if n < 3 else ins.then_inc(sem_("wsel_ready"), 1)

            def add_spread(v):
                for q in range(4):
                    dve.wait_ge(sem_("spread_done"), v * 4 + (q + 1))
                    dve.wait_ge(sem_("y_added"), v * 4 + (q + 1))
                    tt(yacc[:, 2 * q:2 * q + 2, :], yacc[:, 2 * q:2 * q + 2, :], v3(bank[6 + q % 2][:], T),
                       ALU.add).then_inc(sem_("y_added"), 1)

            def hidden(v):
                dve.wait_ge(sem_("gate_silu"), v + 1)
                dve.wait_ge(sem_("up_used"), v + 1)
                tt(hid, sgate, bank[3][:], ALU.mult).then_inc(sem_("hid_ready"), 1)

            def read_second_half(r, v):
                dve.wait_ge(sem_("down_used"), v + 1)
                V.tensor_copy(oute[:, r, 512:D], bank[5][:]).then_inc(sem_("oute_ready"), 1)

            def two_pairs(own, pair, v, more):
                hidden(v)
                if more:
                    select(own, 0, pair + 2, v + 2)
                read_second_half(0, v)
                hidden(v + 1)
                add_spread(v)
                if more:
                    select(own, 1, pair + 3, v + 3)
                read_second_half(1, v + 1)
                add_spread(v + 1)

            def moe_pass(b, own):
                for r in range(2):
                    select(own, r, r, b * NPAIR + r, first=b == 0)
                    if b == 0 and r == 0:
                        own.do(V.tensor_reduce(cnt_f[:], bank[7][:, 2 * E_:3 * E_], AX_X, ALU.max))
                        V.tensor_copy(cnt_i[:], cnt_f[:]).then_inc(sem_("counted"), 1)
                turns = NPAIR // 2 - 1
                with dve.Fori(0, turns) as i:
                    own.turns(i, 12, turns)
                    two_pairs(own, i * 2, i * 2 + b * NPAIR, True)
                own.end()
                two_pairs(own, NPAIR - 2, NPAIR - 2 + b * NPAIR, False)

            moe_pass(0, own)
            n_max = dve.value_load(cnt_i[0:1, 0:1], min_val=0, max_val=T)
            more = Own(dve, sem_("dve_more_step"))
            for b in range(1, NPASS):
                with dve.If(n_max > b * CAP):
                    more.do(ts(rank[:], rank[:], float(CAP), None, ALU.subtract))
                    moe_pass(b, more)
            dve.drain()
            for k in range(KD):
                stt(resid[:, k, :], yacc[:, k, :], mod[:, 40 + k:41 + k], resid[:, k, :], ALU.mult,
                    ALU.add).then_inc(sem_("x_final"), 1)
            dve.wait_ge(sem_("out_sq"), 4)
            sums = ssum[:, 0:4].rearrange("p (c h) -> p c h", c=TT)
            do(V.tensor_reduce(rsum[:, 0:2], sums, AX_X, ALU.add))
            ts(rsum[:, 0:2], rsum[:, 0:2], 1.0 / D, NORM_EPS, ALU.mult, ALU.add).then_inc(sem_("out_var"), 1)
            dve.wait_ge(sem_("out_std"), 1)
            do(V.reciprocal(rsum[:, 0:2], rsum[:, 0:2]))
            dve.wait_ge(final_in, 16)
            for c in range(TT):
                for half in range(2):
                    stt(out_t[:, c, half * 512:(half + 1) * 512], bank[2 * c + half][:], rsum[:, c:c + 1],
                        final_g[:, half * 512:(half + 1) * 512], ALU.mult, ALU.mult).then_inc(sem_("out_ready"), 1)


IN = ["x", "w_in", "w_conv_out", "w_ssm_out", "w_o", "w_ffn_up", "w_ffn_down", "w_ada_2", "w_in_2", "w_proj_moba_2",
      "w_proj_diff_2", "w_out_2", "w_route", "w_gate_2", "w_up_2", "w_down_2"]


def kernel(**inputs):
    import numpy as np
    import concourse.bacc as bacc
    from concourse.bass_utils import run_bass_kernel_spmd

    a = {k: np.ascontiguousarray(v) for k, v in inputs.items()}
    f32 = np.float32

    def cols(v):
        return np.reshape(v, (-1, P)).T

    def taps(w):
        return np.reshape(w.T, (-1, P, w.shape[0])).transpose(1, 0, 2).reshape(P, -1)

    def every(v):
        return np.broadcast_to(np.reshape(v, (1, -1)), (P, np.size(v)))

    values = {
        "ln_in_g": cols(a["ln_in_g"]), "ln_in_b": cols(a["ln_in_b"]), "conv_w": taps(a["conv_dw_w"][0]),
        "conv_b": cols(a["conv_dw_b"]), "conv_ln_g": cols(a["conv_ln_g"]), "conv_ln_b": cols(a["conv_ln_b"]),
        "ssm_w": taps(a["ssm_conv_w"][0]), "ssm_b": cols(a["ssm_conv_b"]),
        "ssm_d": cols(np.repeat(a["ssm_d"][0], HD)), "ssm_norm": cols(a["ssm_norm_w"]),
        "ln1_g": cols(a["ln1_g"]), "ln1_b": cols(a["ln1_b"]), "ffn_w": taps(a["ffn_dw_w"][0]),
        "ffn_b": cols(a["ffn_dw_b"]), "ln2_g": cols(a["ln2_g"]), "ln2_b": cols(a["ln2_b"]), "b_ada": cols(a["b_ada_2"]),
        "c": cols(a["c_2"]), "norm1_g": cols(a["norm1_g_2"]), "norm2_g": cols(a["norm2_g_2"]),
        "subln_g": cols(a["diff_subln_g_2"]),
        "dt_bias": every(a["ssm_dt_bias"]), "a_log": every(a["ssm_a_log"]),
        "b_route": every(np.concatenate([a["b_group_2"][0], a["b_expert_2"][0]])),
        "lam_q1": every(a["lambda_q1_2"]), "lam_q2": every(a["lambda_q2_2"]),
        "lam_k1": every(a["lambda_k1_2"]), "lam_k2": every(a["lambda_k2_2"]),
    }
    params = np.ascontiguousarray(np.concatenate([values[n] for n, _ in PARAMS], axis=1))

    i = np.arange(P)
    swap = np.zeros((P, P), f32)
    for m in range(P):
        swap[m + 32 if m % 64 < 32 else m - 32, m] = -1.0 if m % 64 < 32 else 1.0
    q, k = np.arange(T), np.arange(T)
    att = np.where(k[None, :] <= q[:, None], f32(0), f32(NEG)).reshape(TT, P, T).transpose(1, 0, 2).reshape(P, TT * T)
    inv = (f32(1.0) / (f32(10000.0) ** (np.arange(0, 64, 2, dtype=f32) / f32(64)))).astype(f32)
    ang = np.arange(T, dtype=f32)[None, :] * inv[i % 32][:, None]
    tables = {
        "ident": np.eye(P, dtype=f32), "upper": (i[:, None] <= i[None, :]).astype(f32),
        "before": (i[:, None] < i[None, :]).astype(f32), "ones": np.ones((P, P), f32), "swap": swap,
        "ssm_mask": np.where(i[None, :] >= i[:, None], f32(0), f32(NEG)), "att_mask": att,
        "cos": np.cos(ang).astype(f32), "sin": np.sin(ang).astype(f32),
        "slot": np.broadcast_to(np.arange(CAP, dtype=f32), (P, CAP)),
        "place": np.broadcast_to(np.arange(EP, dtype=f32), (P, EP)),
    }
    consts = np.ascontiguousarray(np.concatenate([tables[n] for n, _ in CONSTS], axis=1).astype(f32))

    arrays = {"params": params, "consts": consts, "final_g": np.ascontiguousarray(every(a["final_g_2"])), "x": a["x"][0]}
    for n in IN[1:]:
        if n == "w_route":
            arrays[n] = np.concatenate([a["w_group_2"][0], a["w_expert_2"][0]], axis=1)
        else:
            arrays[n] = a[n][0]
    nc = bacc.Bacc("TRN2", target_bir_lowering=False, num_devices=1)
    ap = {n: nc.dram_tensor(f"in_{n}", v.shape, F32, kind="ExternalInput").ap() for n, v in arrays.items()}
    out = nc.dram_tensor("out", (T, D), F32, kind="ExternalOutput").ap()
    program(nc, ap["x"], ap["params"], ap["consts"], ap["final_g"], *[ap[n] for n in IN[1:]], out)
    r = run_bass_kernel_spmd(nc, [{f"in_{n}": np.ascontiguousarray(v) for n, v in arrays.items()}], core_ids=[0])
    return r.results[0]["out"].reshape(1, T, D)
```
